# Optimizing a Trainium2 kernel written in Bass

```python
import math
import jax, jax.numpy as jnp
from jax import lax
import numpy as np

D_MODEL = 1024
BATCH = 1
SEQ = 512
DEPTH = 2

CHUNK = 64
Q_BLOCK = 128
HEAD_DIM = 64
ROPE_THETA = 10000.0
EPS = 1e-6
A_HEADS = 8
A_LAT = 128
IDX_HEADS = 4
IDX_DIM = 64
TOPK_MAX = 256
B_HEADS = 4
B_VDIM = 2 * HEAD_DIM
C_GROUPS = 8
C_WIDTH = C_GROUPS * HEAD_DIM
SGU_BLOCK = 128
D_WIDTH = 512
CONV_W = 31
D_FF = 2816
PLE_DIM = 256

EVEN_SIZES = (A_HEADS * HEAD_DIM, HEAD_DIM, A_LAT, IDX_HEADS * IDX_DIM, IDX_DIM, IDX_HEADS,
              B_HEADS * 2 * HEAD_DIM, B_HEADS * 2 * HEAD_DIM, B_HEADS * B_VDIM)
EVEN_IN = sum(EVEN_SIZES)
EVEN_OUT = A_HEADS * HEAD_DIM + B_HEADS * B_VDIM
ODD_IN = 2 * C_WIDTH + 2 * D_WIDTH
ODD_OUT = C_WIDTH + D_WIDTH
N_EVEN = (DEPTH + 1) // 2
N_ODD = DEPTH // 2


def rms_norm(x, g):
    xf = x.astype(jnp.float32)
    y = xf * lax.rsqrt(jnp.mean(xf * xf, axis=-1, keepdims=True) + EPS)
    return (y * g.astype(jnp.float32)).astype(x.dtype)

def layer_norm(x, g, b):
    xf = x.astype(jnp.float32)
    mu = jnp.mean(xf, axis=-1, keepdims=True)
    var = jnp.mean(jnp.square(xf - mu), axis=-1, keepdims=True)
    y = (xf - mu) * lax.rsqrt(var + EPS)
    return (y * g.astype(jnp.float32) + b.astype(jnp.float32)).astype(x.dtype)

def swiglu(x, w_gate, w_up, w_down):
    return (jax.nn.silu(x @ w_gate) * (x @ w_up)) @ w_down

def rope_tables(pos):
    inv = ROPE_THETA ** (-jnp.arange(0, HEAD_DIM, 2, dtype=jnp.float32) / HEAD_DIM)
    ang = pos.astype(jnp.float32)[..., None] * inv
    return jnp.cos(ang), jnp.sin(ang)

def apply_rope(x, cos, sin):
    x1, x2 = jnp.split(x, 2, axis=-1)
    c = cos[:, :, None, :]
    s = sin[:, :, None, :]
    return jnp.concatenate([x1 * c - x2 * s, x2 * c + x1 * s], axis=-1).astype(x.dtype)

def split_cols(z, sizes):
    out, off = [], 0
    for n in sizes:
        out.append(z[..., off:off + n])
        off += n
    return out

def to_blocks(x):
    b, s = x.shape[:2]
    return jnp.moveaxis(x.reshape(b, s // Q_BLOCK, Q_BLOCK, *x.shape[2:]), 1, 0)

def from_blocks(y):
    nb, b, q = y.shape[:3]
    return jnp.moveaxis(y, 0, 1).reshape(b, nb * q, *y.shape[3:])

def dsa_attention(q, k, v_lat, iq, ik, iw, w_uv):
    s_len = q.shape[1]
    top_k = min(TOPK_MAX, s_len // 4)
    key_chunk = jnp.arange(s_len) // CHUNK
    scale = HEAD_DIM ** -0.5
    gather = jax.vmap(lambda a, i: a[i])

    def block(args):
        qb, iqb, iwb, j = args
        q_chunk = (j * Q_BLOCK + jnp.arange(Q_BLOCK)) // CHUNK
        mask = key_chunk[None, :] <= q_chunk[:, None]
        dots = jnp.einsum('bqhe,bse->bqhs', iqb, ik).astype(jnp.float32)
        score = jnp.einsum('bqh,bqhs->bqs', iwb.astype(jnp.float32), jax.nn.relu(dots))
        score = jnp.where(mask, score, -jnp.inf)
        _, sel = lax.top_k(score, top_k)
        valid = (sel // CHUNK) <= q_chunk[None, :, None]
        k_sel = gather(k, sel)
        v_sel = gather(v_lat, sel)
        logits = jnp.einsum('bqhd,bqkd->bhqk', qb, k_sel).astype(jnp.float32) * scale
        logits = jnp.where(valid[:, None], logits, -jnp.inf)
        prob = jax.nn.softmax(logits, axis=-1).astype(v_lat.dtype)
        o_lat = jnp.einsum('bhqk,bqkl->bqhl', prob, v_sel)
        return jnp.einsum('bqhl,hld->bqhd', o_lat, w_uv)

    nb = s_len // Q_BLOCK
    o = lax.map(block, (to_blocks(q), to_blocks(iq), to_blocks(iw), jnp.arange(nb)))
    return from_blocks(o)

def diff_attention(q, k, v, lam, subln_g, lam_init):
    s_len = q.shape[1]
    key_chunk = jnp.arange(s_len) // CHUNK
    scale = HEAD_DIM ** -0.5

    def block(args):
        qb, j = args
        q_chunk = (j * Q_BLOCK + jnp.arange(Q_BLOCK)) // CHUNK
        mask = key_chunk[None, :] <= q_chunk[:, None]
        s = jnp.einsum('bqhcd,bshcd->cbhqs', qb, k).astype(jnp.float32) * scale
        prob = jax.nn.softmax(jnp.where(mask, s, -jnp.inf), axis=-1)
        a = (prob[0] - lam * prob[1]).astype(v.dtype)
        return jnp.einsum('bhqs,bshe->bqhe', a, v)

    nb = s_len // Q_BLOCK
    o = from_blocks(lax.map(block, (to_blocks(q), jnp.arange(nb))))
    return rms_norm(o, subln_g) * (1.0 - lam_init)

def even_mixer(xn, cos, sin, w_in, w_out, a_q_g, a_k_g, a_w_uv, b_q_g, b_k_g,
               lq1, lk1, lq2, lk2, subln_g, lam_init):
    bsz, s_len = xn.shape[:2]
    aq, ak, av, iq, ik, iw, bq, bk, bv = split_cols(xn @ w_in, EVEN_SIZES)
    aq = apply_rope(rms_norm(aq.reshape(bsz, s_len, A_HEADS, HEAD_DIM), a_q_g), cos, sin)
    ak = apply_rope(rms_norm(ak, a_k_g)[:, :, None], cos, sin)[:, :, 0]
    iq = apply_rope(iq.reshape(bsz, s_len, IDX_HEADS, IDX_DIM), cos, sin)
    ik = apply_rope(ik[:, :, None], cos, sin)[:, :, 0]
    a_out = dsa_attention(aq, ak, av, iq, ik, iw, a_w_uv).reshape(bsz, s_len, A_HEADS * HEAD_DIM)
    bq = rms_norm(bq.reshape(bsz, s_len, B_HEADS * 2, HEAD_DIM), b_q_g)
    bk = rms_norm(bk.reshape(bsz, s_len, B_HEADS * 2, HEAD_DIM), b_k_g)
    bq = apply_rope(bq, cos, sin).reshape(bsz, s_len, B_HEADS, 2, HEAD_DIM)
    bk = apply_rope(bk, cos, sin).reshape(bsz, s_len, B_HEADS, 2, HEAD_DIM)
    bv = bv.reshape(bsz, s_len, B_HEADS, B_VDIM)
    lam = (jnp.exp(jnp.sum(lq1.astype(jnp.float32) * lk1.astype(jnp.float32)))
           - jnp.exp(jnp.sum(lq2.astype(jnp.float32) * lk2.astype(jnp.float32))) + lam_init)
    b_out = diff_attention(bq, bk, bv, lam, subln_g, lam_init).reshape(bsz, s_len, B_HEADS * B_VDIM)
    return jnp.concatenate([a_out, b_out], axis=-1) @ w_out

def odd_mixer(xn, w_in, w_out, c_ln_g, c_ln_b, c_w_s, c_b_s, d_conv_w, d_conv_b, d_ln_g, d_ln_b):
    bsz, s_len = xn.shape[:2]
    zc, zd = split_cols(xn @ w_in, (2 * C_WIDTH, 2 * D_WIDTH))
    u, v = jnp.split(jax.nn.gelu(zc), 2, axis=-1)
    v = layer_norm(v, c_ln_g, c_ln_b)
    vb = v.reshape(bsz, s_len // SGU_BLOCK, SGU_BLOCK, C_GROUPS, C_WIDTH // C_GROUPS)
    pc = jnp.arange(SGU_BLOCK) // CHUNK
    w_s = jnp.where((pc[:, None] >= pc[None, :])[None], c_w_s, 0.0)
    sg = jnp.einsum('gij,bnjgc->bnigc', w_s, vb) + c_b_s.T[None, None, :, :, None]
    c_out = u * sg.reshape(bsz, s_len, C_WIDTH)
    a, g = jnp.split(zd, 2, axis=-1)
    hd = a * jax.nn.sigmoid(g)
    hd = lax.conv_general_dilated(hd, d_conv_w[:, None, :], window_strides=(1,),
                                  padding=[(CONV_W - 1, 0)],
                                  dimension_numbers=('NWC', 'WIO', 'NWC'),
                                  feature_group_count=D_WIDTH) + d_conv_b
    d_out = jax.nn.silu(layer_norm(hd, d_ln_g, d_ln_b))
    return jnp.concatenate([c_out, d_out], axis=-1) @ w_out

def first_inputs(seed: int = 0) -> dict:
    key = jax.random.key(seed)
    ks = list(jax.random.split(key, 48))

    def nrm(shape, scale):
        return jax.random.normal(ks.pop(), shape, jnp.float32) * scale

    def gain(shape):
        return 1.0 + nrm(shape, 0.02)

    D = D_MODEL
    return {
        "x": nrm((BATCH, SEQ, D), 1.0),
        "p": nrm((DEPTH, BATCH, SEQ, PLE_DIM), 1.0),
        "pos": (jax.random.randint(ks.pop(), (BATCH, 1), 0, 4096, dtype=jnp.int32)
                + jnp.arange(SEQ, dtype=jnp.int32)[None, :]).astype(jnp.int32),
        "ffn1_g": gain((DEPTH, D)),
        "ffn1_wg": nrm((DEPTH, D, D_FF), D ** -0.5),
        "ffn1_wu": nrm((DEPTH, D, D_FF), D ** -0.5),
        "ffn1_wd": nrm((DEPTH, D_FF, D), D_FF ** -0.5),
        "mix_g": gain((DEPTH, D)),
        "ffn2_g": gain((DEPTH, D)),
        "ffn2_wg": nrm((DEPTH, D, D_FF), D ** -0.5),
        "ffn2_wu": nrm((DEPTH, D, D_FF), D ** -0.5),
        "ffn2_wd": nrm((DEPTH, D_FF, D), D_FF ** -0.5),
        "ple_g": gain((DEPTH, D)),
        "ple_wgate": nrm((DEPTH, D, D), D ** -0.5),
        "ple_wproj": nrm((DEPTH, PLE_DIM, D), PLE_DIM ** -0.5),
        "ev_w_in": nrm((N_EVEN, D, EVEN_IN), D ** -0.5),
        "ev_w_out": nrm((N_EVEN, EVEN_OUT, D), EVEN_OUT ** -0.5),
        "a_q_g": gain((N_EVEN, HEAD_DIM)),
        "a_k_g": gain((N_EVEN, HEAD_DIM)),
        "a_w_uv": nrm((N_EVEN, A_HEADS, A_LAT, HEAD_DIM), A_LAT ** -0.5),
        "b_q_g": gain((N_EVEN, HEAD_DIM)),
        "b_k_g": gain((N_EVEN, HEAD_DIM)),
        "b_lam_q1": nrm((N_EVEN, HEAD_DIM), 0.1),
        "b_lam_k1": nrm((N_EVEN, HEAD_DIM), 0.1),
        "b_lam_q2": nrm((N_EVEN, HEAD_DIM), 0.1),
        "b_lam_k2": nrm((N_EVEN, HEAD_DIM), 0.1),
        "b_subln_g": gain((N_EVEN, B_VDIM)),
        "od_w_in": nrm((N_ODD, D, ODD_IN), D ** -0.5),
        "od_w_out": nrm((N_ODD, ODD_OUT, D), ODD_OUT ** -0.5),
        "c_ln_g": gain((N_ODD, C_WIDTH)),
        "c_ln_b": nrm((N_ODD, C_WIDTH), 0.02),
        "c_w_s": nrm((N_ODD, C_GROUPS, SGU_BLOCK, SGU_BLOCK), SGU_BLOCK ** -0.5),
        "c_b_s": 1.0 + nrm((N_ODD, C_GROUPS, SGU_BLOCK), 0.1),
        "d_conv_w": nrm((N_ODD, CONV_W, D_WIDTH), CONV_W ** -0.5),
        "d_conv_b": nrm((N_ODD, D_WIDTH), 0.02),
        "d_ln_g": gain((N_ODD, D_WIDTH)),
        "d_ln_b": nrm((N_ODD, D_WIDTH), 0.02),
    }

def first_block(x, p, pos, ffn1_g, ffn1_wg, ffn1_wu, ffn1_wd, mix_g, ffn2_g, ffn2_wg, ffn2_wu,
              ffn2_wd, ple_g, ple_wgate, ple_wproj, ev_w_in, ev_w_out, a_q_g, a_k_g, a_w_uv,
              b_q_g, b_k_g, b_lam_q1, b_lam_k1, b_lam_q2, b_lam_k2, b_subln_g, od_w_in,
              od_w_out, c_ln_g, c_ln_b, c_w_s, c_b_s, d_conv_w, d_conv_b, d_ln_g, d_ln_b):
    cos, sin = rope_tables(pos)
    h = x
    for layer in range(DEPTH):
        h = h + 0.5 * swiglu(rms_norm(h, ffn1_g[layer]), ffn1_wg[layer], ffn1_wu[layer], ffn1_wd[layer])
        xn = rms_norm(h, mix_g[layer])
        if layer % 2 == 0:
            e = layer // 2
            lam_init = 0.8 - 0.6 * math.exp(-0.3 * layer)
            mix = even_mixer(xn, cos, sin, ev_w_in[e], ev_w_out[e], a_q_g[e], a_k_g[e], a_w_uv[e],
                             b_q_g[e], b_k_g[e], b_lam_q1[e], b_lam_k1[e], b_lam_q2[e],
                             b_lam_k2[e], b_subln_g[e], lam_init)
        else:
            o = layer // 2
            mix = odd_mixer(xn, od_w_in[o], od_w_out[o], c_ln_g[o], c_ln_b[o], c_w_s[o], c_b_s[o],
                            d_conv_w[o], d_conv_b[o], d_ln_g[o], d_ln_b[o])
        h = h + mix
        h = h + 0.5 * swiglu(rms_norm(h, ffn2_g[layer]), ffn2_wg[layer], ffn2_wu[layer], ffn2_wd[layer])
        gate = jax.nn.sigmoid(rms_norm(h, ple_g[layer]) @ ple_wgate[layer])
        h = h + gate * (p[layer] @ ple_wproj[layer])
    return h


_first_inputs = first_inputs


def first_inputs(seed=0):
    import zlib

    import numpy as np

    out = dict(_first_inputs(seed))
    spreads = {}
    factors = {'ffn1_g': 4.116,
     'ffn2_g': 6.495,
     'ple_g': 200.0,
     'a_q_g': 33.234,
     'a_k_g': 39.271,
     'b_q_g': 5.699,
     'b_k_g': 6.502,
     'b_lam_q1': 64.0,
     'b_lam_k1': 48.082,
     'b_lam_q2': 200.0,
     'b_lam_k2': 4.175,
     'b_subln_g': 19.194,
     'c_ln_g': 200.0,
     'c_ln_b': 200.0,
     'd_conv_b': 5.454,
     'd_ln_g': 200.0,
     'd_ln_b': 200.0,
     'c_b_s': 54.334}
    for name, (base, spread) in spreads.items():
        noise = np.random.default_rng([zlib.crc32(name.encode()), seed]).standard_normal(out[name].shape)
        drawn = base * np.exp(spread * noise) if base else spread * noise
        out[name] = __import__('jax').numpy.asarray(drawn.astype(out[name].dtype))
    for name, factor in factors.items():
        out[name] = (out[name] * factor).astype(out[name].dtype)
    return out


_narrow_inputs = first_inputs


def first_inputs(seed=0):

    out = dict(_narrow_inputs(seed))
    wider = {'ple_g': 12.0,
     'c_ln_g': 5.5,
     'c_ln_b': 5.61,
     'c_b_s': 3.36,
     'd_ln_g': 4.26,
     'd_ln_b': 4.14}
    for name, times in wider.items():
        mean = out[name].mean()
        out[name] = (mean + times * (out[name] - mean)).astype(out[name].dtype)
    return out


EXPAND = 2
D_INNER = EXPAND * D_MODEL
N_MEM = 256
NEG = -1e30
BIG = 1e30

POOL_WINDOWS = (2, 4, 8, 16)
POOL_WIDTH = 3 * D_INNER // 8
POOL_GROUP = POOL_WIDTH // len(POOL_WINDOWS)

RET_HEADS = 4
RET_DK = 128
RET_DV = 192
RET_CHUNK = 128
ROPE_BASE = 10000.0

MEM_HEADS = 4
MEM_DH = 128
MEM_WIDTH = MEM_HEADS * MEM_DH

NSA_HEADS = 12
NSA_KV = 2
NSA_HPG = NSA_HEADS // NSA_KV
NSA_DH = 128
CMP_BLOCK = 32
CMP_STRIDE = 16
CMP_HIDDEN = 256
SLC_BLOCK = 64
SLC_TOPK = 8
WINDOW = 512
NSA_QBLOCK = 32

REL_BUCKETS = 32
REL_MAX_DIST = 128

EVEN_SPLITS = (POOL_WIDTH, RET_HEADS * RET_DK, RET_HEADS * RET_DK, RET_HEADS * RET_DV, MEM_WIDTH, D_INNER)
ODD_SPLITS = (NSA_HEADS * NSA_DH,) + (NSA_KV * NSA_DH,) * 6 + (3 * NSA_HEADS, MEM_WIDTH, D_INNER)
EVEN_COLS = sum(EVEN_SPLITS)
ODD_COLS = sum(ODD_SPLITS)


def rmsnorm(x, g):
    xf = x.astype(jnp.float32)
    y = xf * lax.rsqrt(jnp.mean(xf * xf, axis=-1, keepdims=True) + EPS)
    return (y * g.astype(jnp.float32)).astype(x.dtype)

def split_cols_2(z, sizes):
    return jnp.split(z, np.cumsum(sizes)[:-1].tolist(), axis=-1)

def t5_bucket(rel):
    n = jnp.maximum(rel, 0)
    max_exact = REL_BUCKETS // 2
    nf = jnp.maximum(n, 1).astype(jnp.float32)
    large = max_exact + (jnp.log(nf / max_exact) / math.log(REL_MAX_DIST / max_exact)
                         * (REL_BUCKETS - max_exact)).astype(jnp.int32)
    large = jnp.minimum(large, REL_BUCKETS - 1)
    return jnp.where(n < max_exact, n, large)

def pool_mixer(u, w_grp, scale):
    B_, S, W = u.shape
    uf = u.astype(jnp.float32)
    cs = jnp.concatenate([jnp.zeros((B_, 1, W), jnp.float32), jnp.cumsum(uf, axis=1)], axis=1)
    t = jnp.arange(S)
    outs = []
    for gi, w in enumerate(POOL_WINDOWS):
        sl = slice(gi * POOL_GROUP, (gi + 1) * POOL_GROUP)
        lo = jnp.maximum(t + 1 - w, 0)
        cnt = (t + 1 - lo).astype(jnp.float32)[None, :, None]
        outs.append((cs[:, 1:, sl] - cs[:, lo, sl]) / cnt - uf[..., sl])
    pooled = jnp.stack(outs, axis=2)
    y = jnp.einsum('bsgc,gcd->bsgd', pooled, w_grp.astype(jnp.float32)).reshape(B_, S, W)
    return y * scale.astype(jnp.float32)

def rotary(x):
    S, Dh = x.shape[-2], x.shape[-1]
    half = Dh // 2
    inv = ROPE_BASE ** (-jnp.arange(half, dtype=jnp.float32) / half)
    ang = jnp.arange(S, dtype=jnp.float32)[:, None] * inv[None, :]
    cos, sin = jnp.cos(ang), jnp.sin(ang)
    x1 = x[..., :half].astype(jnp.float32)
    x2 = x[..., half:].astype(jnp.float32)
    return jnp.concatenate([x1 * cos - x2 * sin, x1 * sin + x2 * cos], axis=-1)

def retention(q, k, v):
    B_, S, _ = q.shape
    H, C = RET_HEADS, RET_CHUNK
    N = S // C
    qh = rotary(q.reshape(B_, S, H, RET_DK).transpose(0, 2, 1, 3)) * (RET_DK ** -0.5)
    kh = rotary(k.reshape(B_, S, H, RET_DK).transpose(0, 2, 1, 3))
    vh = v.reshape(B_, S, H, RET_DV).transpose(0, 2, 1, 3).astype(jnp.float32)
    log_g = jnp.log(1.0 - jnp.exp2(-5.0 - jnp.arange(H, dtype=jnp.float32)))
    n = jnp.arange(C, dtype=jnp.float32)
    diff = n[:, None] - n[None, :]
    decay_in = jnp.where(diff >= 0, jnp.exp(log_g[:, None, None] * jnp.maximum(diff, 0.0)), 0.0)
    xi = jnp.exp(log_g[:, None] * (n + 1.0))
    zeta = jnp.exp(log_g[:, None] * (C - 1.0 - n))
    g_chunk = jnp.exp(log_g * C)
    qc = qh.reshape(B_, H, N, C, RET_DK)
    kc = kh.reshape(B_, H, N, C, RET_DK)
    vc = vh.reshape(B_, H, N, C, RET_DV)
    att = jnp.einsum('bhncd,bhnmd->bhncm', qc, kc) * decay_in[None, :, None]
    o_inner = jnp.einsum('bhncm,bhnmv->bhncv', att, vc)
    kv = jnp.einsum('bhnmd,bhnmv->bhndv', kc * zeta[None, :, None, :, None], vc)

    def step(R, kv_n):
        return R * g_chunk[None, :, None, None] + kv_n, R

    _, R_prev = lax.scan(step, jnp.zeros((B_, H, RET_DK, RET_DV), jnp.float32), kv.transpose(2, 0, 1, 3, 4))
    R_prev = R_prev.transpose(1, 2, 0, 3, 4)
    o_cross = jnp.einsum('bhncd,bhndv->bhncv', qc * xi[None, :, None, :, None], R_prev)
    o = (o_inner + o_cross).reshape(B_, H, S, RET_DV)
    mu = jnp.mean(o, axis=-1, keepdims=True)
    var = jnp.mean((o - mu) ** 2, axis=-1, keepdims=True)
    o = (o - mu) * lax.rsqrt(var + EPS)
    return o.transpose(0, 2, 1, 3).reshape(B_, S, H * RET_DV)

def mem_attention(xq, mem_n, w_mem_kv):
    B_, S, _ = xq.shape
    M = mem_n.shape[1]
    mk, mv = jnp.split(mem_n @ w_mem_kv, 2, axis=-1)
    mk = mk.reshape(B_, M, MEM_HEADS, MEM_DH)
    mv = mv.reshape(B_, M, MEM_HEADS, MEM_DH)
    qh = xq.reshape(B_, S, MEM_HEADS, MEM_DH).astype(jnp.float32) * (MEM_DH ** -0.5)
    p = jax.nn.softmax(jnp.einsum('bshd,bmhd->bhsm', qh, mk), axis=-1)
    o = jnp.einsum('bhsm,bmhd->bshd', p, mv)
    return o.reshape(B_, S, MEM_WIDTH)

def compress(k, pe, w1, b1, w2):
    B_, S = k.shape[:2]
    n_cmp = (S - CMP_BLOCK) // CMP_STRIDE + 1
    idx = jnp.arange(n_cmp)[:, None] * CMP_STRIDE + jnp.arange(CMP_BLOCK)[None, :]
    blocks = k[:, idx] + pe[:, None, :]
    flat = blocks.transpose(0, 1, 3, 2, 4).reshape(B_, n_cmp, NSA_KV, CMP_BLOCK * NSA_DH)
    return jax.nn.silu(flat @ w1 + b1) @ w2

def cmp_to_slc_matrix(n_cmp, n_slc):
    cst = np.arange(n_cmp)[:, None] * CMP_STRIDE
    sst = np.arange(n_slc)[None, :] * SLC_BLOCK
    ov = np.clip(np.minimum(cst + CMP_BLOCK, sst + SLC_BLOCK) - np.maximum(cst, sst), 0, None)
    return jnp.asarray(ov / CMP_STRIDE, dtype=jnp.float32)

def nsa_attention(q, kc, vc, ks, vs, kw, vw, gate_logits, cmp_pe, cmp_w1, cmp_b1, cmp_w2, rel_bias):
    B_, S = q.shape[:2]
    QB = NSA_QBLOCK
    qh = q.reshape(B_, S, NSA_KV, NSA_HPG, NSA_DH).transpose(0, 2, 3, 1, 4).astype(jnp.float32) * (NSA_DH ** -0.5)

    def kv_heads(t):
        return t.reshape(B_, S, NSA_KV, NSA_DH)

    kcmp = compress(kv_heads(kc), cmp_pe[0], cmp_w1[0], cmp_b1[0], cmp_w2[0]).transpose(0, 2, 1, 3)
    vcmp = compress(kv_heads(vc), cmp_pe[1], cmp_w1[1], cmp_b1[1], cmp_w2[1]).transpose(0, 2, 1, 3)
    n_cmp = kcmp.shape[2]
    n_slc = S // SLC_BLOCK
    kslc = kv_heads(ks).reshape(B_, n_slc, SLC_BLOCK, NSA_KV, NSA_DH).transpose(0, 3, 1, 2, 4)
    vslc = kv_heads(vs).reshape(B_, n_slc, SLC_BLOCK, NSA_KV, NSA_DH).transpose(0, 3, 1, 2, 4)
    pad = ((0, 0), (0, 0), (WINDOW, 0), (0, 0))
    kwin = jnp.pad(kv_heads(kw).transpose(0, 2, 1, 3), pad)
    vwin = jnp.pad(kv_heads(vw).transpose(0, 2, 1, 3), pad)
    gates = jax.nn.sigmoid(gate_logits.astype(jnp.float32)).reshape(B_, S, 3, NSA_KV, NSA_HPG).transpose(0, 2, 3, 4, 1)
    overlap = cmp_to_slc_matrix(n_cmp, n_slc)
    cend = jnp.arange(n_cmp) * CMP_STRIDE + CMP_BLOCK - 1
    table = rel_bias.astype(jnp.float32)
    table_g = table.reshape(REL_BUCKETS, NSA_KV, NSA_HPG)
    k_sel = min(SLC_TOPK, n_slc)
    b_idx = jnp.arange(B_)[:, None, None, None]
    g_idx = jnp.arange(NSA_KV)[None, :, None, None]

    def head_bias(rel):
        return table[t5_bucket(rel)].transpose(2, 0, 1).reshape(NSA_KV, NSA_HPG, rel.shape[0], rel.shape[1])

    def masked_softmax(s, mask):
        return jax.nn.softmax(jnp.where(mask, s, NEG), axis=-1)

    def block(s0):
        tpos = s0 + jnp.arange(QB)
        qb = lax.dynamic_slice_in_dim(qh, s0, QB, axis=3)
        gb = lax.dynamic_slice_in_dim(gates, s0, QB, axis=4)
        rel_c = tpos[:, None] - cend[None, :]
        sc = jnp.einsum('bghqd,bgjd->bghqj', qb, kcmp) + head_bias(rel_c)
        pc = masked_softmax(sc, rel_c >= 0) * (tpos >= CMP_BLOCK - 1).astype(jnp.float32)[:, None]
        oc = jnp.einsum('bghqj,bgjd->bghqd', pc, vcmp)
        imp = jnp.einsum('bghqj,js->bgqs', pc, overlap)
        sblk = jnp.arange(n_slc)[None, :]
        cur = (tpos // SLC_BLOCK)[:, None]
        forced = (sblk == 0) | (sblk == cur) | (sblk == cur - 1)
        future = sblk * SLC_BLOCK > tpos[:, None]
        imp = jnp.where(forced, BIG, jnp.where(future, -BIG, imp))
        _, sel = lax.top_k(imp, k_sel)
        kg = kslc[b_idx, g_idx, sel].reshape(B_, NSA_KV, QB, k_sel * SLC_BLOCK, NSA_DH)
        vg = vslc[b_idx, g_idx, sel].reshape(B_, NSA_KV, QB, k_sel * SLC_BLOCK, NSA_DH)
        kpos_s = (sel[..., None] * SLC_BLOCK + jnp.arange(SLC_BLOCK)).reshape(B_, NSA_KV, QB, k_sel * SLC_BLOCK)
        rel_s = tpos[None, None, :, None] - kpos_s
        bias_s = table_g[t5_bucket(rel_s), g_idx].transpose(0, 1, 4, 2, 3)
        ss = jnp.einsum('bghqd,bgqkd->bghqk', qb, kg) + bias_s
        ps = masked_softmax(ss, (rel_s >= 0)[:, :, None])
        osel = jnp.einsum('bghqk,bgqkd->bghqd', ps, vg)
        kwb = lax.dynamic_slice_in_dim(kwin, s0, WINDOW + QB, axis=2)
        vwb = lax.dynamic_slice_in_dim(vwin, s0, WINDOW + QB, axis=2)
        kpos_w = s0 - WINDOW + jnp.arange(WINDOW + QB)
        rel_w = tpos[:, None] - kpos_w[None, :]
        mask_w = (rel_w >= 0) & (rel_w < WINDOW) & (kpos_w >= 0)[None, :]
        sw = jnp.einsum('bghqd,bgkd->bghqk', qb, kwb) + head_bias(rel_w)
        pw = masked_softmax(sw, mask_w)
        ow = jnp.einsum('bghqk,bgkd->bghqd', pw, vwb)
        return gb[:, 0, ..., None] * oc + gb[:, 1, ..., None] * osel + gb[:, 2, ..., None] * ow

    outs = lax.map(block, jnp.arange(S // QB) * QB)
    return outs.transpose(1, 0, 4, 2, 3, 5).reshape(B_, S, NSA_HEADS * NSA_DH)

def even_layer(h, mem_n, g, w_in, pool_w, pool_scale, w_mem_kv, w_out):
    u = rmsnorm(h, g)
    za, rq, rk, rv, xq, gate = split_cols_2(u @ w_in, EVEN_SPLITS)
    a = pool_mixer(za, pool_w, pool_scale)
    r = retention(rq, rk, rv)
    m = mem_attention(xq, mem_n, w_mem_kv)
    y = jnp.concatenate([a, r, m], axis=-1) * jax.nn.silu(gate.astype(jnp.float32))
    return h + (y @ w_out).astype(h.dtype)

def odd_layer(h, mem_n, g, w_in, cmp_pe, cmp_w1, cmp_b1, cmp_w2, w_mem_kv, w_out, rel_bias):
    u = rmsnorm(h, g)
    q, kc, vc, ks, vs, kw, vw, gl, xq, gate = split_cols_2(u @ w_in, ODD_SPLITS)
    c = nsa_attention(q, kc, vc, ks, vs, kw, vw, gl, cmp_pe, cmp_w1, cmp_b1, cmp_w2, rel_bias)
    m = mem_attention(xq, mem_n, w_mem_kv)
    y = jnp.concatenate([c, m], axis=-1) * jax.nn.silu(gate.astype(jnp.float32))
    return h + (y @ w_out).astype(h.dtype)

def second_inputs(seed: int = 0) -> dict:
    key = jax.random.key(seed)
    ks = jax.random.split(key, 20)
    n_even = (DEPTH + 1) // 2
    n_odd = DEPTH // 2

    def nrm(k, shape, scale):
        return scale * jax.random.normal(k, shape, jnp.float32)

    return {
        'x': nrm(ks[0], (BATCH, SEQ, D_MODEL), 1.0),
        'mem': nrm(ks[1], (BATCH, N_MEM, D_MODEL), 1.0),
        'norm_g': 1.0 + nrm(ks[2], (DEPTH, D_MODEL), 0.05),
        'final_g': 1.0 + nrm(ks[3], (D_MODEL,), 0.05),
        'mem_norm_g': 1.0 + nrm(ks[4], (D_MODEL,), 0.05),
        'rel_bias': nrm(ks[5], (REL_BUCKETS, NSA_HEADS), 0.5),
        'ev_w_in': nrm(ks[6], (n_even, D_MODEL, EVEN_COLS), D_MODEL ** -0.5),
        'ev_pool_w': nrm(ks[7], (n_even, len(POOL_WINDOWS), POOL_GROUP, POOL_GROUP), POOL_GROUP ** -0.5),
        'ev_pool_scale': 1.0 + nrm(ks[8], (n_even, POOL_WIDTH), 0.1),
        'ev_w_mem_kv': nrm(ks[9], (n_even, D_MODEL, 2 * MEM_WIDTH), D_MODEL ** -0.5),
        'ev_w_out': nrm(ks[10], (n_even, D_INNER, D_MODEL), D_INNER ** -0.5),
        'od_w_in': nrm(ks[11], (n_odd, D_MODEL, ODD_COLS), D_MODEL ** -0.5),
        'od_cmp_pe': nrm(ks[12], (n_odd, 2, CMP_BLOCK, NSA_DH), 0.1),
        'od_cmp_w1': nrm(ks[13], (n_odd, 2, CMP_BLOCK * NSA_DH, CMP_HIDDEN), (CMP_BLOCK * NSA_DH) ** -0.5),
        'od_cmp_b1': nrm(ks[14], (n_odd, 2, CMP_HIDDEN), 0.01),
        'od_cmp_w2': nrm(ks[15], (n_odd, 2, CMP_HIDDEN, NSA_DH), CMP_HIDDEN ** -0.5),
        'od_w_mem_kv': nrm(ks[16], (n_odd, D_MODEL, 2 * MEM_WIDTH), D_MODEL ** -0.5),
        'od_w_out': nrm(ks[17], (n_odd, D_INNER, D_MODEL), D_INNER ** -0.5),
    }

def second_block(x, mem, norm_g, final_g, mem_norm_g, rel_bias, ev_w_in, ev_pool_w, ev_pool_scale, ev_w_mem_kv, ev_w_out,
              od_w_in, od_cmp_pe, od_cmp_w1, od_cmp_b1, od_cmp_w2, od_w_mem_kv, od_w_out):
    mem_n = rmsnorm(mem, mem_norm_g)
    h = x
    for i in range(DEPTH):
        j = i // 2
        if i % 2 == 0:
            h = even_layer(h, mem_n, norm_g[i], ev_w_in[j], ev_pool_w[j], ev_pool_scale[j], ev_w_mem_kv[j], ev_w_out[j])
        else:
            h = odd_layer(h, mem_n, norm_g[i], od_w_in[j], od_cmp_pe[j], od_cmp_w1[j], od_cmp_b1[j], od_cmp_w2[j],
                          od_w_mem_kv[j], od_w_out[j], rel_bias)
    return rmsnorm(h, final_g)


def setup_inputs(seed=0):
    out = dict(first_inputs(seed))
    for name, value in second_inputs(seed + 1).items():
        if name != "x":
            out[name + "_2"] = value
    return out


def reference(
    x, p, pos, ffn1_g, ffn1_wg, ffn1_wu, ffn1_wd, mix_g, ffn2_g, ffn2_wg, ffn2_wu, ffn2_wd,
    ple_g, ple_wgate, ple_wproj, ev_w_in, ev_w_out, a_q_g, a_k_g, a_w_uv, b_q_g, b_k_g,
    b_lam_q1, b_lam_k1, b_lam_q2, b_lam_k2, b_subln_g, od_w_in, od_w_out, c_ln_g, c_ln_b, c_w_s,
    c_b_s, d_conv_w, d_conv_b, d_ln_g, d_ln_b, mem_2, norm_g_2, final_g_2, mem_norm_g_2,
    rel_bias_2, ev_w_in_2, ev_pool_w_2, ev_pool_scale_2, ev_w_mem_kv_2, ev_w_out_2, od_w_in_2,
    od_cmp_pe_2, od_cmp_w1_2, od_cmp_b1_2, od_cmp_w2_2, od_w_mem_kv_2, od_w_out_2,
):
    x = first_block(
        x, p, pos, ffn1_g, ffn1_wg, ffn1_wu, ffn1_wd, mix_g, ffn2_g, ffn2_wg, ffn2_wu, ffn2_wd,
        ple_g, ple_wgate, ple_wproj, ev_w_in, ev_w_out, a_q_g, a_k_g, a_w_uv, b_q_g, b_k_g,
        b_lam_q1, b_lam_k1, b_lam_q2, b_lam_k2, b_subln_g, od_w_in, od_w_out, c_ln_g, c_ln_b,
        c_w_s, c_b_s, d_conv_w, d_conv_b, d_ln_g, d_ln_b,
    )
    return second_block(
        x, mem_2, norm_g_2, final_g_2, mem_norm_g_2, rel_bias_2, ev_w_in_2, ev_pool_w_2,
        ev_pool_scale_2, ev_w_mem_kv_2, ev_w_out_2, od_w_in_2, od_cmp_pe_2, od_cmp_w1_2,
        od_cmp_b1_2, od_cmp_w2_2, od_w_mem_kv_2, od_w_out_2,
    )


_drawn_inputs = setup_inputs


def setup_inputs(seed=0):
    import zlib

    import numpy as np

    out = dict(_drawn_inputs(seed))
    spreads = {}
    factors = {'ple_g': 3.066,
     'mem_2': 8.0,
     'norm_g_2': 8.0,
     'mem_norm_g_2': 8.0,
     'rel_bias_2': 200.0,
     'ev_w_in_2': 8.0,
     'ev_pool_w_2': 8.0,
     'ev_pool_scale_2': 8.0,
     'ev_w_mem_kv_2': 8.0,
     'ev_w_out_2': 8.0,
     'od_w_in_2': 8.0,
     'od_cmp_pe_2': 8.0,
     'od_cmp_w1_2': 8.0,
     'od_cmp_b1_2': 168.401,
     'od_cmp_w2_2': 8.0,
     'od_w_mem_kv_2': 8.0,
     'od_w_out_2': 8.0}
    for name, (base, spread) in spreads.items():
        noise = np.random.default_rng([zlib.crc32(name.encode()), seed]).standard_normal(out[name].shape)
        drawn = base * np.exp(spread * noise) if base else spread * noise
        out[name] = __import__('jax').numpy.asarray(drawn.astype(out[name].dtype))
    for name, factor in factors.items():
        out[name] = (out[name] * factor).astype(out[name].dtype)
    return out
```

```python
from contextlib import ExitStack

import numpy as np

import concourse.bass as bass
from concourse import mybir
from concourse.alu_op_type import AluOpType as ALU

F32 = mybir.dt.float32
I32 = mybir.dt.int32
ACT = mybir.ActivationFunctionType
AX = mybir.AxisListType

P = 128
SEQ = 512
TT = SEQ // P
D = 1024
KT = D // P
DFF = 2816
FT = DFF // P
EPS = 1e-6
BIG = 1e30
RING = 6
SLAB = 2048
NMEM = 256
POOL_W = (2, 4, 8, 16)
RET_H, RET_DV = 4, 192
NSA_H, NSA_G, NSA_D = 12, 2, 128
NCMP = (SEQ - 32) // 16 + 1
BIASW = 896
FREV = 1024
TOPK = 128
SHRINK = 2.0 ** -40
OVERFLOW = 3.4028235e38 * SHRINK ** 2


def t5_bucket(rel):
    n = np.maximum(rel, 0)
    nf = np.maximum(n, 1).astype(np.float32)
    large = 16 + (np.log(nf / np.float32(16)) / np.float32(np.log(8.0)) * np.float32(16)).astype(np.int32)
    return np.where(n < 16, n, np.minimum(large, 31))


def constant_pack():
    p = np.arange(P)
    f = np.float32
    out = {}
    out["ident"] = np.eye(P, dtype=f)
    out["flip"] = np.eye(P, dtype=f)[::-1]
    out["ones"] = np.ones((P, P), f)
    out["ones64"] = (p[:, None] // 64 == p[None, :] // 64).astype(f)
    for name, half in (("rot64", 32), ("rot128", 64)):
        r = np.zeros((P, P), f)
        for m in range(P):
            if m % (2 * half) < half:
                r[m + half, m] = -1.0
            else:
                r[m - half, m] = 1.0
        out[name] = r
    y = np.arange(SEQ)
    out["chunkmask"] = np.where((y[None, :] >= 448) & (p[:, None] < 64), f(BIG), f(0)).astype(f)
    inv = (10000.0 ** (-np.arange(0, 64, 2) / 64)).astype(f)
    out["inv64"] = inv[p % 32][:, None]
    out["seen"] = (p >= 31).astype(f)[:, None]
    out["eps"] = np.full((P, 1), EPS, f)
    out["eps_small"] = np.full((P, 1), EPS * SHRINK ** 2, f)
    return out


def rotary_tables():
    f = np.float32
    inv = (10000.0 ** (-np.arange(64) / 64)).astype(f)
    ang = (np.arange(SEQ, dtype=f)[None, :] * inv[:, None]).astype(f)
    c, s = np.cos(ang), np.sin(ang)
    return np.concatenate([np.tile(c, (2, 1)), np.tile(s, (2, 1))], axis=1).astype(f)


def decay_tables():
    m, x = np.arange(P)[:, None], np.arange(SEQ)[None, :]
    out = []
    for h in range(RET_H):
        lg = np.log(1.0 - 2.0 ** (-5.0 - h))
        out.append(np.where(x >= m, np.exp(lg * np.maximum(x - m, 0)), 0.0))
    return np.concatenate(out, axis=1).astype(np.float32)


def pool_tables():
    t = np.arange(SEQ)
    return np.tile(np.concatenate([1.0 / np.minimum(t + 1, w) for w in POOL_W])[None], (P, 1)).astype(np.float32)


def bucket_table():
    z = np.arange(FREV)
    rel = 511 - z
    out = np.zeros((33, FREV), np.float32)
    b = t5_bucket(rel)
    out[b[z <= 511], z[z <= 511]] = 1.0
    out[32, z > 511] = 1.0
    return out


CONSTS = constant_pack()
CONST_AT = {}
_at = 0
for _n, _a in CONSTS.items():
    CONST_AT[_n] = (_at, _a.shape[1])
    _at += _a.shape[1]
CONST_N = _at

def tiles(lo, n, w=P):
    return [(lo + i * w, w) for i in range(n)]


EV = dict(aq=0, ak=512, av=576, iq=704, ik=960, iw=1024, bq=1028, bk=1540, bv=2052)
EV_F = (tiles(EV["aq"], 4) + [(EV["ak"], 64, 2)] + tiles(EV["iq"], 2) + [(EV["ik"], 64, 2)]
        + tiles(EV["bq"], 4) + tiles(EV["bk"], 4))
EV_T = [(EV["av"], P), (EV["iw"], 4)] + tiles(EV["bv"], 4)
OD_F = tiles(0, 4) + tiles(1024, 8)
OD_T = tiles(512, 4)
E2 = dict(za=0, rq=768, rk=1280, rv=1792, xq=2560, gate=3072)
O2 = dict(q=0, kc=1536, vc=1792, ks=2048, vs=2304, kw=2560, vw=2816, gl=3072, xq=3108, gate=3620)


def stream_plan():
    plan = []
    for l in range(2):
        for n in ("ffn1", "mix", "ffn2"):
            if n == "mix":
                if l == 0:
                    plan += [("ev_f", "ev_w_in", 0, "cols", EV_F), ("ev_t", "ev_w_in", 0, "cols", EV_T),
                             ("ev_out", "ev_w_out", 0, "cols", tiles(0, KT))]
                else:
                    plan += [("od_f", "od_w_in", 0, "cols", OD_F), ("od_t", "od_w_in", 0, "cols", OD_T),
                             ("od_out", "od_w_out", 0, "cols", tiles(0, KT))]
                continue
            plan += [(f"{n}_up{l}", (f"{n}_wg", f"{n}_wu"), l, "pair", tiles(0, FT)),
                     (f"{n}_down{l}", f"{n}_wd", l, "rows", tiles(0, FT))]
        plan += [(f"ple_p{l}", "ple_wproj", l, "rows", tiles(0, 2)),
                 (f"ple_g{l}", "ple_wgate", l, "cols", tiles(0, KT))]
    for l, (w, c, kv, wo) in enumerate((("ev_w_in_2", E2, "ev_w_mem_kv_2", "ev_w_out_2"),
                                        ("od_w_in_2", O2, "od_w_mem_kv_2", "od_w_out_2"))):
        plan += [(f"mk{l}", kv, 0, "cols", tiles(0, 4)), (f"mv{l}", kv, 0, "cols", tiles(512, 4)),
                 (f"xq{l}", w, 0, "cols", tiles(c["xq"], 4))]
        if l == 0:
            plan += [("za", w, 0, "cols", tiles(c["za"], 8, 96)),
                     ("rqk", w, 0, "cols", tiles(c["rq"], 8)), ("rv", w, 0, "cols", tiles(c["rv"], 6)),
                     ("gate0", w, 0, "cols", tiles(c["gate"], 16, 96) + tiles(c["gate"] + 1536, 4)),
                     ("wo0", wo, 0, "rows", tiles(0, 16, 96) + tiles(1536, 4))]
        else:
            plan += [("kvc", w, 0, "cols", tiles(c["kc"], 4)),
                     ("cmp0", "od_cmp_w1_2", 0, "rows4", tiles(0, 32)),
                     ("cmp1", "od_cmp_w1_2", 1, "rows4", tiles(0, 32)),
                     ("nsaq", w, 0, "cols", tiles(c["q"], 12)),
                     ("nsak", w, 0, "cols", tiles(c["ks"], 2) + tiles(c["kw"], 2)),
                     ("nsav", w, 0, "cols", tiles(c["vs"], 2) + tiles(c["vw"], 2) + [(c["gl"], 36)]),
                     ("gate1", w, 0, "cols", tiles(c["gate"], 16)),
                     ("wo1", wo, 0, "rows", tiles(0, 16))]
    return plan


def slab_count(kind, t):
    if kind == "pair":
        return len(t)
    if kind == "rows4":
        return len(t) // 8
    return (len(t) + 1) // 2


PLAN = stream_plan()
STREAM_AT = {}
_at = 0
for _s, _w, _l, _k, _t in PLAN:
    STREAM_AT[_s] = (_at, slab_count(_k, _t))
    _at += slab_count(_k, _t)
NSLAB = _at


def lay_stream(inputs):
    out = np.zeros((NSLAB, P, SLAB), np.float32)

    def column_slabs(w, t, at, step):
        w3 = w.reshape(KT, P, -1).transpose(1, 0, 2)
        for i, tile in enumerate(t):
            lo, n = tile[:2]
            view = out[at + (i // 2) * step].reshape(P, KT, 2, P)
            for r in range(tile[2] if len(tile) > 2 else 1):
                view[:, :, i % 2, r * n:(r + 1) * n] = w3[:, :, lo:lo + n]

    for stage, name, layer, kind, t in PLAN:
        at, _ = STREAM_AT[stage]
        if kind == "pair":
            for j in range(2):
                column_slabs(inputs[name[j]][layer], t, at + j, 2)
        elif kind == "cols":
            column_slabs(inputs[name][layer], t, at, 1)
        elif kind == "rows":
            for i, (lo, n) in enumerate(t):
                out[at + i // 2].reshape(P, 2, D)[:n, i % 2] = inputs[name][layer][lo:lo + n]
        else:
            w = inputs[name][0, layer].reshape(4, 8, P, 256)
            out[at:at + 4] = w.transpose(0, 2, 1, 3).reshape(4, P, SLAB)
    return out


VEC = []
for _l in range(2):
    VEC += [(f"ffn1_g{_l}", "ffn1_g", _l, P), (f"mix_g{_l}", "mix_g", _l, P), (f"ffn2_g{_l}", "ffn2_g", _l, P),
            (f"ple_g{_l}", "ple_g", _l, P), (f"norm2_g{_l}", "norm_g_2", _l, P)]
VEC += [("final_g", "final_g_2", None, P), ("memnorm_g", "mem_norm_g_2", None, P),
        ("subln_g", "b_subln_g", 0, P), ("conv_b", "d_conv_b", 0, P),
        ("dln_g", "d_ln_g", 0, P), ("dln_b", "d_ln_b", 0, P), ("pool_scale", "ev_pool_scale_2", 0, 96)]
VEC_N = {"ffn1_g": 8, "mix_g": 8, "ffn2_g": 8, "ple_g": 8, "norm_g_2": 8, "final_g_2": 8, "mem_norm_g_2": 8,
         "b_subln_g": 1, "d_conv_b": 4, "d_ln_g": 4, "d_ln_b": 4, "ev_pool_scale_2": 8}
VEC_AT = {}
_at = 0
for _n, _a, _i, _w in VEC:
    VEC_AT[_n] = (_at, VEC_N[_a])
    _at += VEC_N[_a]
for _n, _c in (("aq_g", 1), ("ak_g", 1), ("bq_g", 1), ("bk_g", 1), ("conv_w", 4 * 31), ("lams", 4),
               ("cmp_b1", 4), ("cmp_pe", 64)):
    VEC_AT[_n] = (_at, _c)
    _at += _c
VEC_TOTAL = _at


def lay_vectors(inputs):
    out = np.zeros((P, VEC_TOTAL), np.float32)
    for name, arr, idx, w in VEC:
        at, n = VEC_AT[name]
        a = inputs[arr] if idx is None else inputs[arr][idx]
        out[:w, at:at + n] = a.reshape(n, w).T
    for name, arr in (("aq_g", "a_q_g"), ("ak_g", "a_k_g"), ("bq_g", "b_q_g"), ("bk_g", "b_k_g")):
        out[0:64, VEC_AT[name][0]] = inputs[arr][0]
        out[64:128, VEC_AT[name][0]] = inputs[arr][0]
    at = VEC_AT["conv_w"][0]
    out[:, at:at + 124] = inputs["d_conv_w"][0].reshape(31, 4, P).transpose(2, 1, 0).reshape(P, 124)
    at = VEC_AT["lams"][0]
    for j, arr in enumerate(("b_lam_q1", "b_lam_k1", "b_lam_q2", "b_lam_k2")):
        out[0:64, at + j] = inputs[arr][0]
    at = VEC_AT["cmp_b1"][0]
    out[:, at:at + 4] = inputs["od_cmp_b1_2"][0].reshape(4, P).T
    at = VEC_AT["cmp_pe"][0]
    out[:, at:at + 64] = inputs["od_cmp_pe_2"][0].reshape(64, P).T
    return out


class Signal:

    def __init__(self, handle):
        self.handle, self.base = handle, 0

    def at(self, n):
        return self.base + n

    def advance(self, n):
        self.base += n


class Core:

    def __init__(self, nc, ctx, dram):
        self.nc, self.dram = nc, dram
        self.ctx = ctx
        sb = lambda n, s, dt=F32: ctx.enter_context(nc.sbuf_tensor(n, s, dt))
        self.ring = sb("ring", [P, RING, SLAB])
        self.h = sb("h", [P, KT, SEQ])
        self.xn = sb("xn", [P, KT, SEQ])
        self.cst = sb("cst", [P, CONST_N])
        self.vec = sb("vec", [P, VEC_TOTAL])
        self.arena_n = (nc.sbuf_top - nc.sbuf_base) // 4 - 8
        self.arena = sb("arena", [P, self.arena_n])
        self.ps = ctx.enter_context(nc.psum_tensor("ps", [P, 8, SEQ], F32))
        names = ("slab_free", "product_done", "evacuated", "squares_done", "sum_done", "root_done", "root_read",
                 "vec_chain", "act_chain", "pool_chain", "act_step", "dve_step", "pe_step", "dve_read", "act_read",
                 "scores_done", "biased", "exp_done", "diag_done", "turned", "turned_copied", "out_done",
                 "out_copied", "pool_step", "pe_step2", "tmp_ready")
        self.s = {n: Signal(ctx.enter_context(nc.semaphore(n))) for n in names}
        self.slab_loaded = [ctx.enter_context(nc.semaphore(f"slab_loaded{i}")) for i in range(RING)]
        self.aux = Signal(ctx.enter_context(nc.semaphore("aux_loaded")))
        self.stored = Signal(ctx.enter_context(nc.semaphore("stored")))
        self.loaded = 0
        self.slab_end = []

    def c(self, name):
        a, n = CONST_AT[name]
        return self.cst[:, a:a + n]

    def v(self, name, j=0, rows=P):
        a, _ = VEC_AT[name]
        return self.vec[0:rows, a + j:a + j + 1]

    def at(self, off, *shape):
        n = int(np.prod(shape))
        assert off + n <= self.arena_n, (off, shape, self.arena_n)
        a = self.arena[:, off:off + n]
        if len(shape) == 2:
            a = a.rearrange("p (a b) -> p a b", b=shape[1])
        elif len(shape) == 3:
            a = a.rearrange("p (a b c) -> p a b c", b=shape[1], c=shape[2])
        return a

    def vlink(self, ins):
        s = self.s["vec_chain"]
        ins.then_inc(s.handle, 1)
        s.advance(1)
        self.nc.vector.wait_ge(s.handle, s.base)

    def alink(self, ins):
        s = self.s["act_chain"]
        ins.then_inc(s.handle, 1)
        s.advance(1)
        self.nc.scalar.wait_ge(s.handle, s.base)

    def plink(self, ins):
        s = self.s["pool_chain"]
        ins.then_inc(s.handle, 1)
        s.advance(1)
        self.nc.gpsimd.wait_ge(s.handle, s.base)

    def slabs_end(self, signal, values):
        self.slab_end += [(signal.handle, v) for v in values]

    def stream(self, sp):
        while self.loaded < min(NSLAB, len(self.slab_end) + RING):
            n = self.loaded
            if n >= RING:
                sp.wait_ge(*self.slab_end[n - RING])
            sp.dma_start(self.ring[:, n % RING, :], self.dram["stream"][n]).then_inc(self.slab_loaded[n % RING], 16)
            self.loaded += 1

    def slab(self, pe, n):
        pe.wait_ge(self.slab_loaded[n % RING], 16 * (n // RING + 1))
        return self.ring[:, n % RING, :]


def start(k):
    nc = k.nc

    with nc.Block() as block:
        @block.sync
        def _(sp):
            sp.dma_start(k.h[:, :, :], k.dram["x"]).then_inc(k.aux.handle, 16)
            sp.dma_start(k.vec[:, :], k.dram["vec"]).then_inc(k.aux.handle, 16)
            sp.dma_start(k.cst[:, :], k.dram["cst"]).then_inc(k.aux.handle, 16)
            k.stream(sp)
            sp.wait_ge(k.aux.handle, k.aux.at(48))
    k.aux.advance(48)


def load(k, pairs):
    with k.nc.Block() as block:
        @block.sync
        def _(sp):
            for dst, src in pairs:
                sp.dma_start(dst, src).then_inc(k.aux.handle, 16)
            sp.wait_ge(k.aux.handle, k.aux.at(16 * len(pairs)))
    k.aux.advance(16 * len(pairs))


def rms(k, src, dst, gain, nk=KT, n=SEQ, scratch=0):
    nc, s = k.nc, k.s
    sq = k.at(scratch, 2, SEQ)
    root = k.at(scratch + 2 * SEQ, SEQ)
    inv = k.at(scratch + 3 * SEQ, SEQ)

    with nc.Block() as block:
        @block.scalar
        def _(act):
            for c in range(nk):
                if c >= 2:
                    act.wait_ge(s["sum_done"].handle, s["sum_done"].at(c - 1))
                nc.scalar.activation(sq[:, c % 2, 0:n], src[:, c, 0:n], ACT.Square).then_inc(s["squares_done"].handle, 1)
            act.wait_ge(s["sum_done"].handle, s["sum_done"].at(nk))
            nc.scalar.activation(root[:, 0:n], k.ps[:, 0, 0:n], ACT.Sqrt, bias=k.c("eps"),
                                 scale=1.0 / (nk * P)).then_inc(s["root_done"].handle, 1)

        @block.tensor
        def _(pe):
            for c in range(nk):
                pe.wait_ge(s["squares_done"].handle, s["squares_done"].at(c + 1))
                nc.tensor.matmul(k.ps[:, 0, 0:n], k.c("ones"), sq[:, c % 2, 0:n], start=(c == 0),
                                 stop=(c == nk - 1)).then_inc(s["sum_done"].handle, 1)

        @block.vector
        def _(dve):
            dve.wait_ge(s["root_done"].handle, s["root_done"].at(1))
            k.vlink(nc.vector.reciprocal(inv[:, 0:n], root[:, 0:n]))
            for c in range(nk):
                nc.vector.scalar_tensor_tensor(dst[:, c, 0:n], src[:, c, 0:n], k.v(gain, c), inv[:, 0:n],
                                               ALU.mult, ALU.mult)
    s["squares_done"].advance(nk)
    s["sum_done"].advance(nk)
    s["root_done"].advance(1)


def dense_f(k, stage, x, widths, evacuate, engine="scalar", nk=KT, n=SEQ):
    nc, s = k.nc, k.s
    first, slabs = STREAM_AT[stage]
    per = 2 if nk == KT else KT
    done, read = s["product_done"], s["evacuated"]
    k.slabs_end(done, [done.at(min(per * (j + 1), len(widths))) for j in range(slabs)])

    with nc.Block() as block:
        @block.sync
        def _(sp):
            k.stream(sp)

        @block.tensor
        def _(pe):
            for m, w in enumerate(widths):
                slab = k.slab(pe, first + m // per).rearrange("p (k m j) -> p k m j", k=nk, j=P)[:, :, m % per, :]
                if m >= 8:
                    pe.wait_ge(read.handle, read.at(m - 7))
                for c in range(nk):
                    ins = nc.tensor.matmul(k.ps[0:w, m % 8, 0:n], slab[:, c, 0:w], x[:, c, 0:n],
                                           start=(c == 0), stop=(c == nk - 1))
                ins.then_inc(done.handle, 1)

        def evac(eng):
            for m, w in enumerate(widths):
                eng.wait_ge(done.handle, done.at(m + 1))
                evacuate(m, k.ps[0:w, m % 8, 0:n]).then_inc(read.handle, 1)

        (block.scalar if engine == "scalar" else block.vector)(evac)
    done.advance(len(widths))
    read.advance(len(widths))


def dense_t(k, stage, x, widths, evacuate, tts=TT):
    nc, s = k.nc, k.s
    first, slabs = STREAM_AT[stage]
    done, read = s["product_done"], s["evacuated"]
    assert slabs == len(widths)
    k.slabs_end(done, [done.at(tts * (j + 1)) for j in range(slabs)])

    with nc.Block() as block:
        @block.sync
        def _(sp):
            k.stream(sp)

        @block.tensor
        def _(pe):
            for j, w in enumerate(widths):
                slab = k.slab(pe, first + j).rearrange("p (k n) -> p k n", k=KT)
                for t in range(tts):
                    u = j * tts + t
                    if u >= 8:
                        pe.wait_ge(read.handle, read.at(u - 7))
                    for c in range(KT):
                        ins = nc.tensor.matmul(k.ps[:, u % 8, 0:w], x[:, c, t * P:(t + 1) * P], slab[:, c, 0:w],
                                               start=(c == 0), stop=(c == KT - 1))
                    ins.then_inc(done.handle, 1)

        @block.scalar
        def _(act):
            for j, w in enumerate(widths):
                for t in range(tts):
                    u = j * tts + t
                    act.wait_ge(done.handle, done.at(u + 1))
                    evacuate(j, t, k.ps[:, u % 8, 0:w]).then_inc(read.handle, 1)
    done.advance(tts * slabs)
    read.advance(tts * slabs)


def dense_gated(k, stage, x, widths, func, finish, scratch):
    nc, s = k.nc, k.s
    first, slabs = STREAM_AT[stage]
    done, gate, read = s["product_done"], s["act_step"], s["evacuated"]
    buf = k.at(scratch, 4, SEQ)
    n = len(widths)
    k.slabs_end(done, [done.at(min(2 * (j + 1), n)) for j in range(slabs)])

    with nc.Block() as block:
        @block.sync
        def _(sp):
            k.stream(sp)

        @block.tensor
        def _(pe):
            for m, w in enumerate(widths):
                slab = k.slab(pe, first + m // 2).rearrange("p (k m j) -> p k m j", k=KT, j=P)[:, :, m % 2, :]
                if m >= 8:
                    pe.wait_ge(gate.handle, gate.at(m - 7))
                for c in range(KT):
                    ins = nc.tensor.matmul(k.ps[0:w, m % 8, :], slab[:, c, 0:w], x[:, c, :],
                                           start=(c == 0), stop=(c == KT - 1))
                ins.then_inc(done.handle, 1)

        @block.scalar
        def _(act):
            for m, w in enumerate(widths):
                act.wait_ge(done.handle, done.at(m + 1))
                if m >= 4:
                    act.wait_ge(read.handle, read.at(m - 3))
                nc.scalar.activation(buf[0:w, m % 4, :], k.ps[0:w, m % 8, :], func).then_inc(gate.handle, 1)

        @block.vector
        def _(dve):
            for m, w in enumerate(widths):
                dve.wait_ge(gate.handle, gate.at(m + 1))
                finish(m, buf[0:w, m % 4, :]).then_inc(read.handle, 1)
    for g in (done, gate, read):
        g.advance(n)


def rows_add(k, stage, x, heights, scale):
    nc, s = k.nc, k.s
    first, slabs = STREAM_AT[stage]
    n = len(heights)
    part, done, read = s["pe_step"], s["product_done"], s["evacuated"]
    k.slabs_end(part, [part.at(j + 1) for j in range(slabs - 1)])
    k.slabs_end(done, [done.at(KT)])

    with nc.Block() as block:
        @block.sync
        def _(sp):
            k.stream(sp)

        @block.tensor
        def _(pe):
            for j in range(slabs):
                slab = k.slab(pe, first + j).rearrange("p (k m j) -> p k m j", k=2, j=P)
                for i in range(2 * j, min(2 * j + 2, n)):
                    w = heights[i]
                    for m in range(KT):
                        ins = nc.tensor.matmul(k.ps[:, m, :], slab[0:w, i % 2, m, :], x[0:w, i, :],
                                               start=(i == 0), stop=(i == n - 1))
                        if i == n - 1:
                            ins.then_inc(done.handle, 1)
                if j < slabs - 1:
                    ins.then_inc(part.handle, 1)

        @block.vector
        def _(dve):
            for m in range(KT):
                dve.wait_ge(done.handle, done.at(m + 1))
                nc.vector.scalar_tensor_tensor(k.h[:, m, :], k.ps[:, m, :], scale, k.h[:, m, :],
                                               ALU.mult, ALU.add)
    part.advance(slabs - 1)
    done.advance(KT)


def ffn(k, name, layer):
    nc, s = k.nc, k.s
    hidden = k.at(0, FT, SEQ)
    rms(k, k.h, k.xn, f"{name}_g{layer}", scratch=FT * SEQ)
    first, slabs = STREAM_AT[f"{name}_up{layer}"]
    done, gate, read = s["product_done"], s["act_step"], s["evacuated"]
    k.slabs_end(done, [done.at(2 * (j // 2) + 2) for j in range(slabs)])

    with nc.Block() as block:
        @block.sync
        def _(sp):
            k.stream(sp)

        @block.tensor
        def _(pe):
            for f in range(FT):
                if f >= 4:
                    pe.wait_ge(read.handle, read.at(f - 3))
                for j in range(2):
                    slab = k.slab(pe, first + 2 * (f // 2) + j).rearrange("p (k m j) -> p k m j", k=KT, j=P)
                    for c in range(KT):
                        ins = nc.tensor.matmul(k.ps[:, (2 * f + j) % 8, :], slab[:, c, f % 2, :], k.xn[:, c, :],
                                               start=(c == 0), stop=(c == KT - 1))
                ins.then_inc(done.handle, 1)

        @block.scalar
        def _(act):
            for f in range(FT):
                act.wait_ge(done.handle, done.at(f + 1))
                nc.scalar.activation(hidden[:, f, :], k.ps[:, (2 * f) % 8, :], ACT.Silu).then_inc(gate.handle, 1)

        @block.vector
        def _(dve):
            for f in range(FT):
                dve.wait_ge(gate.handle, gate.at(f + 1))
                nc.vector.tensor_tensor(hidden[:, f, :], hidden[:, f, :], k.ps[:, (2 * f + 1) % 8, :],
                                        ALU.mult).then_inc(read.handle, 1)
    for g in (done, gate, read):
        g.advance(FT)
    rows_add(k, f"{name}_down{layer}", hidden, [P] * FT, 0.5)


def ple(k, layer):
    nc = k.nc
    pt = k.at(0, 2, SEQ)
    proj = k.at(1024, KT, SEQ)
    load(k, [(pt[:, :, :], k.dram["p"][layer])])
    rms(k, k.h, k.xn, f"ple_g{layer}", scratch=8192)
    dense_f(k, f"ple_p{layer}", pt, [P] * KT, lambda m, ps: nc.scalar.copy(proj[:, m, :], ps), nk=2)

    def finish(m, gate):
        k.vlink(nc.vector.tensor_tensor(gate, gate, proj[:, m, :], ALU.mult))
        return nc.vector.tensor_tensor(k.h[:, m, :], k.h[:, m, :], gate, ALU.add)

    dense_gated(k, f"ple_g{layer}", k.xn, [P] * KT, ACT.Sigmoid, finish, 8192)


class Unit:

    def __init__(self, q, key, bias, v, gate=None, first=True, last=True, dst=None):
        self.q, self.key, self.bias, self.v, self.gate = q, key, bias, v, gate
        self.first, self.last, self.dst = first, last, dst
        self.w = key.shape[-1]


def attention(k, units, scratch):
    nc, s = k.nc, k.s
    n = len(units)
    sc = k.at(scratch, 3, SEQ)
    ex = k.at(scratch + 1536, 3, SEQ)
    pt = k.at(scratch + 3072, 2, SEQ)
    dg = k.at(scratch + 4096, 3, P)
    low = k.at(scratch + 4480, 4)
    tot = k.at(scratch + 4484, 4)
    inv = k.at(scratch + 4488, 4)
    scored, biased, expd = s["scores_done"], s["biased"], s["exp_done"]
    diag, turned, copied = s["diag_done"], s["turned"], s["turned_copied"]
    summed, stored = s["out_done"], s["out_copied"]
    group = np.cumsum([u.first for u in units]) - 1
    last_of = {int(group[i]): i for i in range(n)}

    with nc.Block() as block:
        @block.tensor
        def _(pe):
            def scores(i):
                u = units[i]
                if i >= 3:
                    pe.wait_ge(biased.handle, biased.at(i - 2))
                nc.tensor.matmul(k.ps[:, i % 3, 0:u.w], u.q, u.key, start=True, stop=True).then_inc(scored.handle, 1)

            def turn(i):
                u = units[i]
                pe.wait_ge(diag.handle, diag.at(i + 1))
                if i >= 2:
                    pe.wait_ge(copied.handle, copied.at(i - 1))
                for j, (rows, _) in enumerate(u.v):
                    ins = nc.tensor.matmul(k.ps[0:rows, 3 + i % 2, j * P:(j + 1) * P],
                                           ex[:, i % 3, j * P:j * P + rows], dg[:, i % 3, :], start=True, stop=True)
                ins.then_inc(turned.handle, 1)

            def values(i):
                u = units[i]
                g = int(group[i])
                pe.wait_ge(copied.handle, copied.at(i + 1))
                if u.first and g >= 2:
                    pe.wait_ge(stored.handle, stored.at(g - 1))
                for j, (rows, v) in enumerate(u.v):
                    ins = nc.tensor.matmul(k.ps[0:v.shape[-1], 5 + g % 2, 0:P], v, pt[0:rows, i % 2, j * P:(j + 1) * P],
                                           start=(u.first and j == 0), stop=(u.last and j == len(u.v) - 1))
                ins.then_inc(summed.handle, 1)

            for i in range(n + 3):
                if i < n:
                    scores(i)
                if 2 <= i < n + 2:
                    turn(i - 2)
                if i >= 3:
                    values(i - 3)

        @block.vector
        def _(dve):
            def bias(i):
                u = units[i]
                dve.wait_ge(scored.handle, scored.at(i + 1))
                if i >= 3:
                    dve.wait_ge(expd.handle, expd.at(i - 2))
                nc.vector.tensor_tensor_reduce(sc[:, i % 3, 0:u.w], k.ps[:, i % 3, 0:u.w], u.bias, 1.0, 3e38,
                                               ALU.add, ALU.min, low[:, i % 4:i % 4 + 1]).then_inc(biased.handle, 1)

            def diagonal(i):
                u = units[i]
                dve.wait_ge(expd.handle, expd.at(i + 1))
                k.vlink(nc.vector.reciprocal(inv[:, i % 4:i % 4 + 1], tot[:, i % 4:i % 4 + 1]))
                if i >= 3:
                    dve.wait_ge(turned.handle, turned.at(i - 2))
                if u.gate is None:
                    ins = nc.vector.tensor_scalar(dg[:, i % 3, :], k.c("ident"), inv[:, i % 4:i % 4 + 1], None, ALU.mult)
                else:
                    ins = nc.vector.tensor_scalar(dg[:, i % 3, :], k.c("ident"), inv[:, i % 4:i % 4 + 1], u.gate,
                                                  ALU.mult, ALU.mult)
                ins.then_inc(diag.handle, 1)

            def store(g):
                u = units[last_of[g]]
                dve.wait_ge(summed.handle, summed.at(last_of[g] + 1))
                e = u.v[0][1].shape[-1]
                nc.vector.tensor_copy(u.dst, k.ps[0:e, 5 + g % 2, 0:P]).then_inc(stored.handle, 1)

            for i in range(n + 5):
                if i < n:
                    bias(i)
                if 1 <= i < n + 1:
                    diagonal(i - 1)
                if i >= 5 and units[i - 5].last:
                    store(int(group[i - 5]))

        @block.scalar
        def _(act):
            def exponentials(i):
                u = units[i]
                act.wait_ge(biased.handle, biased.at(i + 1))
                if i >= 3:
                    act.wait_ge(turned.handle, turned.at(i - 2))
                nc.scalar.activation(ex[:, i % 3, 0:u.w], sc[:, i % 3, 0:u.w], ACT.Exp, bias=low[:, i % 4:i % 4 + 1],
                                     scale=-1.0, accum_out=tot[:, i % 4:i % 4 + 1]).then_inc(expd.handle, 1)

            def copy(i):
                u = units[i]
                rows, m = u.v[0][0], len(u.v)
                act.wait_ge(turned.handle, turned.at(i + 1))
                if i >= 2:
                    act.wait_ge(summed.handle, summed.at(i - 1))
                nc.scalar.copy(pt[0:rows, i % 2, 0:m * P], k.ps[0:rows, 3 + i % 2, 0:m * P]).then_inc(copied.handle, 1)

            for i in range(n + 2):
                if i < n:
                    exponentials(i)
                if i >= 2:
                    copy(i - 2)
    for g in (scored, biased, expd, diag, turned, copied, summed):
        g.advance(n)
    stored.advance(len(last_of))


def rotary_cos_sin(k, cos, sin, pos_i, pos_f, tmp):
    nc, s = k.nc, k.s
    two_pi = 2 * np.pi
    c1 = 6.28125
    c2 = float(np.float32(np.round((two_pi - c1) * 2 ** 20) / 2 ** 20))
    c3 = float(np.float32(two_pi - c1 - c2))
    magic = 1.5 * 2.0 ** 23
    edge = 3.1415925
    ready = s["dve_step"]
    ang, turns = tmp[:, 0, :], tmp[:, 1, :]
    load(k, [(pos_i, k.dram["pos"].partition_broadcast(P))])

    with nc.Block() as block:
        @block.vector
        def _(dve):
            k.vlink(nc.vector.tensor_copy(pos_f, pos_i))
            k.vlink(nc.vector.tensor_scalar(ang, pos_f, k.c("inv64"), None, ALU.mult))
            for dst, quarter in ((sin, 0.0), (cos, 0.25)):
                k.vlink(nc.vector.tensor_scalar(turns, ang, 1.0 / two_pi, quarter, ALU.mult, ALU.add))
                k.vlink(nc.vector.tensor_scalar(turns, turns, magic, None, ALU.add))
                k.vlink(nc.vector.tensor_scalar(turns, turns, -magic, None, ALU.add))
                k.vlink(nc.vector.scalar_tensor_tensor(dst, turns, -c1, ang, ALU.mult, ALU.add))
                k.vlink(nc.vector.scalar_tensor_tensor(dst, turns, -c2, dst, ALU.mult, ALU.add))
                k.vlink(nc.vector.scalar_tensor_tensor(dst, turns, -c3, dst, ALU.mult, ALU.add))
                if quarter:
                    k.vlink(nc.vector.tensor_scalar(dst, dst, float(np.pi / 2), None, ALU.add))
                nc.vector.tensor_scalar(dst, dst, -edge, edge, ALU.max, ALU.min).then_inc(ready.handle, 1)

        @block.scalar
        def _(act):
            for i, dst in enumerate((sin, cos)):
                act.wait_ge(ready.handle, ready.at(i + 1))
                nc.scalar.activation(dst, dst, ACT.Sin)
    ready.advance(2)


def norm_rope(k, jobs, rot, ones, dim, cos, sin, scratch):
    nc, s = k.nc, k.s
    n = len(jobs)
    sq = k.at(scratch, 2, SEQ)
    root = k.at(scratch + 1024, SEQ)
    t1 = k.at(scratch + 1536, SEQ)
    t2 = k.at(scratch + 2048, SEQ)
    squared, sums, rooted, normed, rotated, used = (s["squares_done"], s["sum_done"], s["root_done"], s["dve_step"],
                                                    s["pe_step2"], s["dve_read"])
    normal = [i for i, (_, g, _) in enumerate(jobs) if g is not None]

    with nc.Block() as block:
        @block.scalar
        def _(act):
            for a, i in enumerate(normal):
                if a >= 2:
                    act.wait_ge(sums.handle, sums.at(a - 1))
                nc.scalar.activation(sq[:, a % 2, :], jobs[i][0], ACT.Square).then_inc(squared.handle, 1)
                act.wait_ge(sums.handle, sums.at(a + 1))
                if a >= 1:
                    act.wait_ge(normed.handle, normed.at(normal[a - 1] + 1))
                nc.scalar.activation(root, k.ps[:, a % 2, :], ACT.Sqrt, bias=k.c("eps"),
                                     scale=1.0 / dim).then_inc(rooted.handle, 1)

        @block.tensor
        def _(pe):
            a = 0
            for i, (x, g, _) in enumerate(jobs):
                if g is not None:
                    pe.wait_ge(squared.handle, squared.at(a + 1))
                    nc.tensor.matmul(k.ps[:, a % 2, :], k.c(ones), sq[:, a % 2, :], start=True,
                                     stop=True).then_inc(sums.handle, 1)
                    a += 1
                pe.wait_ge(normed.handle, normed.at(i + 1))
                if i >= 2:
                    pe.wait_ge(used.handle, used.at(i - 1))
                nc.tensor.matmul(k.ps[:, 2 + i % 2, :], k.c(rot), x, start=True, stop=True).then_inc(rotated.handle, 1)

        @block.vector
        def _(dve):
            a = 0
            for i, (x, g, scale) in enumerate(jobs):
                if g is not None:
                    dve.wait_ge(rooted.handle, rooted.at(a + 1))
                    k.vlink(nc.vector.reciprocal(t1, root))
                    nc.vector.scalar_tensor_tensor(x, x, k.v(g), t1, ALU.mult, ALU.mult).then_inc(normed.handle, 1)
                    a += 1
                else:
                    k.vlink(nc.vector.memset(t1[:, 0:1], 0.0))
                    nc.vector.memset(t1[:, 0:1], 0.0).then_inc(normed.handle, 1)
                dve.wait_ge(rotated.handle, rotated.at(i + 1))
                nc.vector.scalar_tensor_tensor(t1, x, scale, cos, ALU.mult, ALU.mult)
                nc.vector.scalar_tensor_tensor(t2, k.ps[:, 2 + i % 2, :], scale, sin, ALU.mult,
                                               ALU.mult).then_inc(used.handle, 1)
                dve.wait_ge(used.handle, used.at(i + 1))
                k.vlink(nc.vector.tensor_tensor(x, t1, t2, ALU.add))
    for g, v in ((squared, len(normal)), (sums, len(normal)), (rooted, len(normal)), (normed, n), (rotated, n), (used, n)):
        g.advance(v)


def select_keys(k, iq, ik, iw, negmask, scratch):
    nc, s = k.nc, k.s
    dots = k.at(scratch, 2, SEQ)
    work = k.at(scratch + 1024, SEQ)
    top = k.at(scratch + 1536, 8)
    done, cut, used = s["product_done"], s["act_step"], s["dve_read"]
    gone = -3e38

    with nc.Block() as block:
        @block.tensor
        def _(pe):
            for i in range(1, TT):
                for h in range(4):
                    u = (i - 1) * 4 + h
                    lo = 64 * (h % 2)
                    if u >= 2:
                        pe.wait_ge(cut.handle, cut.at(u - 1))
                    nc.tensor.matmul(k.ps[:, u % 2, 0:P * (i + 1)], iq[lo:lo + 64, h // 2, i * P:(i + 1) * P],
                                     ik[lo:lo + 64, 0:P * (i + 1)], start=True, stop=True).then_inc(done.handle, 1)

        @block.scalar
        def _(act):
            for i in range(1, TT):
                for h in range(4):
                    u = (i - 1) * 4 + h
                    act.wait_ge(done.handle, done.at(u + 1))
                    if u >= 2:
                        act.wait_ge(used.handle, used.at(u - 1))
                    nc.scalar.activation(dots[:, u % 2, 0:P * (i + 1)], k.ps[:, u % 2, 0:P * (i + 1)],
                                         ACT.Relu).then_inc(cut.handle, 1)

        @block.vector
        def _(dve):
            k.vlink(nc.vector.tensor_copy(negmask[:, 0, 0:P], k.c("chunkmask")[:, SEQ - P:SEQ]))
            for i in range(1, TT):
                w = P * (i + 1)
                for h in range(4):
                    u = (i - 1) * 4 + h
                    dve.wait_ge(cut.handle, cut.at(u + 1))
                    wt = iw[:, i, h:h + 1]
                    if h == 0:
                        ins = nc.vector.tensor_scalar(work[:, 0:w], dots[:, u % 2, 0:w], wt, None, ALU.mult)
                    else:
                        ins = nc.vector.scalar_tensor_tensor(work[:, 0:w], dots[:, u % 2, 0:w], wt, work[:, 0:w],
                                                             ALU.mult, ALU.add)
                    ins.then_inc(used.handle, 1)
                    dve.wait_ge(used.handle, used.at(u + 1))
                k.vlink(nc.vector.tensor_tensor(work[:, 0:w], work[:, 0:w], k.c("chunkmask")[:, SEQ - w:SEQ],
                                                ALU.subtract))
                for _ in range(TOPK // 8):
                    k.vlink(nc.vector.max(top, work[:, 0:w]))
                    k.vlink(nc.vector.match_replace(work[:, 0:w], top, work[:, 0:w], gone))
                k.vlink(nc.vector.tensor_scalar(negmask[:, i, 0:w], work[:, 0:w], gone, BIG, ALU.not_equal, ALU.mult))
    for g in (done, cut, used):
        g.advance(4 * (TT - 1))


def even_mixer(k):
    nc, s = k.nc, k.s
    qk = k.at(0, 16, SEQ)
    vt = k.at(8192, TT, 132)
    bv = k.at(8720, TT, 512)
    o = k.at(10768, KT, SEQ)
    olat = k.at(14864, KT, SEQ)
    cos, sin = k.at(18960, SEQ), k.at(19472, SEQ)
    negmask = k.at(19984, TT, SEQ)
    uv = k.at(22032, 512)
    small = k.at(22544, 16)
    scr = 22560
    aq, ak, iq, ik = qk[:, 0:4], qk[:, 4], qk[:, 5:7], qk[:, 7]
    bq, bk = qk[:, 8:12], qk[:, 12:16]

    load(k, [(uv, k.dram["w_uv"])])
    rms(k, k.h, k.xn, "mix_g0", scratch=scr)
    dense_f(k, "ev_f", k.xn, [P] * 16, lambda m, ps: nc.scalar.copy(qk[:, m, :], ps))

    def token_major(j, t, ps):
        dst = vt[:, t, :] if j == 0 else bv[:, t, (j - 1) * 256:j * 256]
        return nc.scalar.copy(dst, ps)

    dense_t(k, "ev_t", k.xn, [132, 256, 256], token_major)
    rotary_cos_sin(k, cos, sin, k.at(scr, SEQ).bitcast(I32), k.at(scr + 512, SEQ), k.at(scr + 1024, 2, SEQ))
    scale = -(64 ** -0.5)
    jobs = ([(aq[:, m, :], "aq_g", scale) for m in range(4)] + [(ak, "ak_g", 1.0)]
            + [(iq[:, m, :], None, 1.0) for m in range(2)] + [(ik, None, 1.0)]
            + [(bq[:, m, :], "bq_g", scale) for m in range(4)] + [(bk[:, m, :], "bk_g", 1.0) for m in range(4)])
    norm_rope(k, jobs, "rot64", "ones64", 64, cos, sin, scr)
    select_keys(k, iq, ik, vt[:, :, 128:132], negmask, scr)

    lams = k.vec[:, VEC_AT["lams"][0]:VEC_AT["lams"][0] + 4]
    with nc.Block() as block:
        @block.vector
        def _(dve):
            nc.vector.tensor_tensor(small[:, 0:2], lams[:, 0:4:2], lams[:, 1:4:2], ALU.mult).then_inc(s["dve_step"].handle, 1)
            dve.wait_ge(s["act_step"].handle, s["act_step"].at(1))
            k.vlink(nc.vector.tensor_tensor(small[:, 4:5], small[:, 3:4], small[:, 2:3], ALU.subtract))
            k.vlink(nc.vector.tensor_scalar(small[:, 5:6], small[:, 4:5], -0.2, None, ALU.add))

        @block.tensor
        def _(pe):
            pe.wait_ge(s["dve_step"].handle, s["dve_step"].at(1))
            nc.tensor.matmul(k.ps[:, 0, 0:2], k.c("ones"), small[:, 0:2], start=True,
                             stop=True).then_inc(s["pe_step"].handle, 1)

        @block.scalar
        def _(act):
            act.wait_ge(s["pe_step"].handle, s["pe_step"].at(1))
            nc.scalar.activation(small[:, 2:4], k.ps[:, 0, 0:2], ACT.Exp).then_inc(s["act_step"].handle, 1)
    for g in ("dve_step", "act_step", "pe_step"):
        s[g].advance(1)

    units = []
    for i in range(TT):
        q = slice(i * P, (i + 1) * P)
        w = P * (i + 1)
        for h in range(8):
            lo = 64 * (h % 2)
            units.append(Unit(aq[lo:lo + 64, h // 2, q], ak[lo:lo + 64, 0:w], negmask[:, i, 0:w],
                              [(P, vt[:, j, 0:P]) for j in range(i + 1)], dst=olat[:, h, q]))
        for h in range(4):
            for c in range(2):
                units.append(Unit(bq[64 * c:64 * c + 64, h, q], bk[64 * c:64 * c + 64, h, 0:w],
                                  k.c("chunkmask")[:, SEQ - w:SEQ],
                                  [(P, bv[:, j, h * P:(h + 1) * P]) for j in range(i + 1)],
                                  gate=small[:, 5:6] if c else None, first=(c == 0), last=(c == 1),
                                  dst=o[:, 4 + h, q]))
    attention(k, units, scr)

    sq = k.at(scr, 2, SEQ)
    root = k.at(scr + 1024, 2, SEQ)
    inv, fin = k.at(scr + 2048, SEQ), k.at(scr + 2560, SEQ)
    lifted, copied, squared, sums, rooted, used = (s["product_done"], s["evacuated"], s["squares_done"], s["sum_done"],
                                                   s["root_done"], s["dve_read"])
    with nc.Block() as block:
        @block.tensor
        def _(pe):
            for h in range(8):
                if h >= 4:
                    pe.wait_ge(copied.handle, copied.at(h - 3))
                nc.tensor.matmul(k.ps[0:64, h % 4, :], uv[:, h * 64:(h + 1) * 64], olat[:, h, :], start=True,
                                 stop=True).then_inc(lifted.handle, 1)
            for h in range(4):
                pe.wait_ge(squared.handle, squared.at(h + 1))
                nc.tensor.matmul(k.ps[:, 4 + h, :], k.c("ones"), sq[:, h % 2, :], start=True,
                                 stop=True).then_inc(sums.handle, 1)

        @block.scalar
        def _(act):
            for h in range(8):
                act.wait_ge(lifted.handle, lifted.at(h + 1))
                lo = 64 * (h % 2)
                nc.scalar.copy(o[lo:lo + 64, h // 2, :], k.ps[0:64, h % 4, :]).then_inc(copied.handle, 1)
            for h in range(4):
                if h >= 2:
                    act.wait_ge(sums.handle, sums.at(h - 1))
                act.wait_ge(s["dve_step"].handle, s["dve_step"].at(h + 1))
                nc.scalar.activation(sq[:, h % 2, :], o[:, 4 + h, :], ACT.Square, scale=SHRINK).then_inc(squared.handle, 1)
            for h in range(4):
                act.wait_ge(sums.handle, sums.at(h + 1))
                if h >= 2:
                    act.wait_ge(used.handle, used.at(h - 1))
                nc.scalar.activation(root[:, h % 2, :], k.ps[:, 4 + h, :], ACT.Sqrt, bias=k.c("eps_small"),
                                     scale=1.0 / P).then_inc(rooted.handle, 1)

        @block.vector
        def _(dve):
            for h in range(4):
                nc.vector.tensor_scalar(o[:, 4 + h, :], o[:, 4 + h, :], -BIG, BIG, ALU.max,
                                        ALU.min).then_inc(s["dve_step"].handle, 1)
            k.vlink(nc.vector.tensor_scalar(small[:, 6:7], k.v("subln_g"), 1.0 - 0.2, None, ALU.mult))
            for h in range(4):
                dve.wait_ge(rooted.handle, rooted.at(h + 1))
                nc.vector.reciprocal(inv, root[:, h % 2, :])
                nc.vector.tensor_scalar(fin, k.ps[:, 4 + h, :], OVERFLOW, SHRINK, ALU.is_lt,
                                        ALU.mult).then_inc(used.handle, 1)
                dve.wait_ge(used.handle, used.at(h + 1))
                k.vlink(nc.vector.tensor_tensor(inv, inv, fin, ALU.mult))
                k.vlink(nc.vector.scalar_tensor_tensor(o[:, 4 + h, :], o[:, 4 + h, :], small[:, 6:7], inv,
                                                       ALU.mult, ALU.mult))
    for g, v in ((lifted, 8), (copied, 8), (squared, 4), (sums, 4), (rooted, 4), (used, 4),
                 (s["dve_step"], 4)):
        g.advance(v)
    dense_f(k, "ev_out", o, [P] * KT,
            lambda m, ps: nc.vector.tensor_tensor(k.h[:, m, :], ps, k.h[:, m, :], ALU.add), engine="vector")


def layer_norm_f(k, groups, rows, scratch):
    nc, s = k.nc, k.s
    sq = k.at(scratch, 2, SEQ)
    root = k.at(scratch + 1024, 2, SEQ)
    inv = k.at(scratch + 2048, SEQ)
    summed, centred, squared, sums, rooted, used = (s["product_done"], s["dve_step"], s["squares_done"], s["sum_done"],
                                                    s["root_done"], s["dve_read"])
    per = len(groups[0])
    dim = per * rows
    n = len(groups)

    with nc.Block() as block:
        @block.tensor
        def _(pe):
            for g, tl in enumerate(groups):
                if g >= 2:
                    pe.wait_ge(centred.handle, centred.at((g - 1) * per))
                for j, x in enumerate(tl):
                    ins = nc.tensor.matmul(k.ps[0:rows, g % 2, :], k.c("ones")[0:rows, 0:rows], x, start=(j == 0),
                                           stop=(j == per - 1))
                ins.then_inc(summed.handle, 1)
                if g >= 2:
                    pe.wait_ge(rooted.handle, rooted.at(g - 1))
                for j in range(per):
                    pe.wait_ge(squared.handle, squared.at(g * per + j + 1))
                    nc.tensor.matmul(k.ps[0:rows, 2 + g % 2, :], k.c("ones")[0:rows, 0:rows],
                                     sq[0:rows, (g * per + j) % 2, :], start=(j == 0),
                                     stop=(j == per - 1)).then_inc(sums.handle, 1)

        @block.scalar
        def _(act):
            for g, tl in enumerate(groups):
                for j, x in enumerate(tl):
                    u = g * per + j
                    act.wait_ge(centred.handle, centred.at(u + 1))
                    if u >= 2:
                        act.wait_ge(sums.handle, sums.at(u - 1))
                    nc.scalar.activation(sq[0:rows, u % 2, :], x, ACT.Square).then_inc(squared.handle, 1)
                act.wait_ge(sums.handle, sums.at((g + 1) * per))
                if g >= 2:
                    act.wait_ge(used.handle, used.at(g - 1))
                nc.scalar.activation(root[0:rows, g % 2, :], k.ps[0:rows, 2 + g % 2, :], ACT.Sqrt,
                                     bias=k.c("eps")[0:rows, :], scale=1.0 / dim).then_inc(rooted.handle, 1)

        @block.vector
        def _(dve):
            for g, tl in enumerate(groups):
                dve.wait_ge(summed.handle, summed.at(g + 1))
                for x in tl:
                    nc.vector.scalar_tensor_tensor(x, k.ps[0:rows, g % 2, :], -1.0 / dim, x, ALU.mult,
                                                   ALU.add).then_inc(centred.handle, 1)
                dve.wait_ge(rooted.handle, rooted.at(g + 1))
                nc.vector.reciprocal(inv[0:rows, :], root[0:rows, g % 2, :]).then_inc(used.handle, 1)
                dve.wait_ge(used.handle, used.at(g + 1))
                for x in tl:
                    ins = nc.vector.tensor_tensor(x, x, inv[0:rows, :], ALU.mult)
                k.vlink(ins)
    for g, v in ((summed, n), (centred, n * per), (squared, n * per), (sums, n * per), (rooted, n), (used, n)):
        g.advance(v)


def odd_mixer(k):
    nc, s = k.nc, k.s
    o = k.at(0, KT, SEQ)
    a = k.at(4096, 4, SEQ)
    g = k.at(6144, 4, 30 + SEQ)
    vt = k.at(8312, TT, 512)
    ws = k.at(10360, 8, P)
    bs = k.at(11384, 4, P)
    lng, lnb = k.at(11896, 512), k.at(12408, 512)
    acc = k.at(12920, 4, SEQ)
    stats, aggr, sm = k.at(14968, TT, 6), k.at(14992, TT, 2), k.at(15000, 16)
    scr = 15016
    load(k, [(ws, k.dram["w_s"]), (bs, k.dram["b_s"]), (lng, k.dram["cln"][0:1].partition_broadcast(P)),
             (lnb, k.dram["cln"][1:2].partition_broadcast(P))])
    rms(k, k.h, k.xn, "mix_g1", scratch=scr)

    def evac(m, ps):
        if m < 4:
            return nc.scalar.activation(o[:, m, :], ps, ACT.Gelu_apprx_tanh)
        if m < 8:
            return nc.scalar.copy(a[:, m - 4, :], ps)
        return nc.scalar.activation(g[:, m - 8, 30:], ps, ACT.Sigmoid)

    dense_f(k, "od_f", k.xn, [P] * 12, evac)
    dense_t(k, "od_t", k.xn, [256, 256],
            lambda j, t, ps: nc.scalar.activation(vt[:, t, j * 256:(j + 1) * 256], ps, ACT.Gelu_apprx_tanh))

    rooted, normed, mixed = s["root_done"], s["dve_step"], s["product_done"]
    with nc.Block() as block:
        @block.gpsimd
        def _(pool):
            nc.gpsimd.memset(g[:, :, 0:30], 0.0)
            k.plink(nc.gpsimd.tensor_tensor(g[:, :, 30:], g[:, :, 30:], a[:, :, :], ALU.mult))
            nc.gpsimd.memset(ws[64:128, :, 0:64], 0.0).then_inc(s["pool_step"].handle, 1)

        @block.scalar
        def _(act):
            act.wait_ge(s["tmp_ready"].handle, s["tmp_ready"].at(1))
            nc.scalar.activation(sm[:, 0:4], aggr[:, :, 1], ACT.Sqrt, bias=k.c("eps")).then_inc(rooted.handle, 1)

        @block.vector
        def _(dve):
            for t in range(TT):
                k.vlink(nc.vector.bn_stats(stats[:, t, :], vt[:, t, :]))
            for t in range(TT):
                ins = nc.vector.bn_aggr(aggr[:, t, :], stats[:, t, :])
            ins.then_inc(s["tmp_ready"].handle, 1)
            dve.wait_ge(rooted.handle, rooted.at(1))
            k.vlink(nc.vector.reciprocal(sm[:, 4:8], sm[:, 0:4]))
            for t in range(TT):
                k.vlink(nc.vector.tensor_scalar(vt[:, t, :], vt[:, t, :], aggr[:, t, 0:1], sm[:, 4 + t:5 + t],
                                                ALU.subtract, ALU.mult))
                k.vlink(nc.vector.tensor_tensor(vt[:, t, :], vt[:, t, :], lng, ALU.mult))
                nc.vector.tensor_tensor(vt[:, t, :], vt[:, t, :], lnb, ALU.add).then_inc(normed.handle, 1)
            for t in range(TT):
                for gp in range(4):
                    u = t * 4 + gp
                    dve.wait_ge(mixed.handle, mixed.at(u + 1))
                    for half in range(2):
                        lo = 64 * half
                        dst = o[lo:lo + 64, gp, t * P:(t + 1) * P]
                        tmp = acc[lo:lo + 64, half, 0:P]
                        k.vlink(nc.vector.tensor_tensor(tmp, k.ps[lo:lo + 64, u % 8, half * P:(half + 1) * P],
                                                        bs[lo:lo + 64, gp, :], ALU.add))
                        ins = nc.vector.tensor_tensor(dst, dst, tmp, ALU.mult)
                        if half:
                            ins.then_inc(s["dve_read"].handle, 1)
                            dve.wait_ge(s["dve_read"].handle, s["dve_read"].at(u + 1))
                        else:
                            k.vlink(ins)

        @block.tensor
        def _(pe):
            pe.wait_ge(s["pool_step"].handle, s["pool_step"].at(1))
            for t in range(TT):
                pe.wait_ge(normed.handle, normed.at(t + 1))
                for gp in range(4):
                    u = t * 4 + gp
                    if u >= 8:
                        pe.wait_ge(s["dve_read"].handle, s["dve_read"].at(u - 7))
                    nc.tensor.matmul(k.ps[:, u % 8, 0:256], vt[:, t, gp * P:(gp + 1) * P],
                                     ws[:, 2 * gp:2 * gp + 2, :], start=True, stop=True).then_inc(mixed.handle, 1)
    for n, v in (("pool_step", 1), ("tmp_ready", 1), ("root_done", 1), ("dve_step", 4), ("product_done", 16),
                 ("dve_read", 16)):
        s[n].advance(v)

    at = VEC_AT["conv_w"][0]
    with nc.Block() as block:
        @block.vector
        def _(dve):
            for tap in range(31):
                for c in range(4):
                    wt = k.vec[:, at + c * 31 + tap:at + c * 31 + tap + 1]
                    src = g[:, c, tap:tap + SEQ]
                    dst = o[:, 4 + c, :]
                    if tap == 0:
                        ins = nc.vector.tensor_scalar(dst, src, wt, k.v("conv_b", c), ALU.mult, ALU.add)
                    else:
                        ins = nc.vector.scalar_tensor_tensor(dst, src, wt, dst, ALU.mult, ALU.add)
                k.vlink(ins)
    layer_norm_f(k, [[o[:, 4 + c, :] for c in range(4)]], P, scr)
    with nc.Block() as block:
        @block.scalar
        def _(act):
            for c in range(4):
                nc.scalar.activation(o[:, 4 + c, :], o[:, 4 + c, :], ACT.Silu, bias=k.v("dln_b", c),
                                     scale=k.v("dln_g", c))
    dense_f(k, "od_out", o, [P] * KT,
            lambda m, ps: nc.vector.tensor_tensor(k.h[:, m, :], ps, k.h[:, m, :], ALU.add), engine="vector")


def mem_attention(k, layer, memn, out, base):
    nc = k.nc
    mk = k.at(base, 4, NMEM)
    mv = k.at(base + 1024, 2, 512)
    xq = k.at(base + 2048, 4, SEQ)
    zero = k.c("chunkmask")[:, 0:NMEM]
    dense_f(k, f"mk{layer}", memn, [P] * 4, lambda m, ps: nc.scalar.copy(mk[:, m, :], ps), n=NMEM)
    dense_t(k, f"mv{layer}", memn, [256, 256],
            lambda j, t, ps: nc.scalar.copy(mv[:, t, j * 256:(j + 1) * 256], ps), tts=2)
    dense_f(k, f"xq{layer}", k.xn, [P] * 4, lambda m, ps: nc.scalar.mul(xq[:, m, :], ps, -(P ** -0.5)))
    attention(k, [Unit(xq[:, h, i * P:(i + 1) * P], mk[:, h, :], zero,
                       [(P, mv[:, j, h * P:(h + 1) * P]) for j in range(2)], dst=out[:, h, i * P:(i + 1) * P])
                  for i in range(TT) for h in range(4)], base + 4096)


def pool_mixer(k, za, out, scr):
    nc, s = k.nc, k.s
    recip = k.at(scr, 4, SEQ)
    wg = k.at(scr + 2048, 8, 192)
    buf = k.at(scr + 3584, 2, 2 * SEQ)
    load(k, [(recip, k.dram["pool_recip"]), (wg[0:96], k.dram["pool_w"])])
    ready, done = s["dve_step"], s["product_done"]

    with nc.Block() as block:
        @block.vector
        def _(dve):
            for g, w in enumerate(POOL_W):
                src = za[0:96, 2 * g:2 * g + 2, :]
                step, b = 1, 0
                while step < w:
                    dst = buf[0:96, b, :].rearrange("p (a t) -> p a t", a=2)
                    nc.vector.tensor_copy(dst[:, :, 0:step], src[:, :, 0:step])
                    k.vlink(nc.vector.tensor_tensor(dst[:, :, step:], src[:, :, step:], src[:, :, 0:SEQ - step], ALU.add))
                    src, step, b = dst, 2 * step, 1 - b
                for a in range(2):
                    k.vlink(nc.vector.tensor_tensor(src[:, a, :], src[:, a, :], recip[0:96, g, :], ALU.mult))
                z = za[0:96, 2 * g:2 * g + 2, :]
                ins = nc.vector.tensor_tensor(z, src, z, ALU.subtract)
                ins.then_inc(ready.handle, 1)
                dve.wait_ge(ready.handle, ready.at(g + 1))

        @block.tensor
        def _(pe):
            for g in range(4):
                pe.wait_ge(ready.handle, ready.at(g + 1))
                for m in range(2):
                    for c in range(2):
                        ins = nc.tensor.matmul(k.ps[0:96, 2 * g + m, :], wg[0:96, 2 * g + c, m * 96:(m + 1) * 96],
                                               za[0:96, 2 * g + c, :], start=(c == 0), stop=(c == 1))
                    ins.then_inc(done.handle, 1)

        @block.scalar
        def _(act):
            for m in range(8):
                act.wait_ge(done.handle, done.at(m + 1))
                nc.scalar.activation(out[0:96, m, :], k.ps[0:96, m, :], ACT.Copy, scale=k.v("pool_scale", m, 96))
    ready.advance(4)
    done.advance(8)


def retention(k, q, key, v, out, decay, scr):
    nc, s = k.nc, k.s
    att = k.at(scr, 2, SEQ)
    scored, decayed, summed, copied = s["scores_done"], s["biased"], s["out_done"], s["out_copied"]

    with nc.Block() as block:
        @block.tensor
        def _(pe):
            def scores(u):
                h, j = u // TT, u % TT
                if u >= 2:
                    pe.wait_ge(decayed.handle, decayed.at(u - 1))
                nc.tensor.matmul(k.ps[:, u % 2, 0:SEQ - j * P], key[:, h, j * P:(j + 1) * P], q[:, h, j * P:],
                                 start=True, stop=True).then_inc(scored.handle, 1)

            def values(u):
                h, j = u // TT, u % TT
                pe.wait_ge(decayed.handle, decayed.at(u + 1))
                if j == 0 and h >= 2:
                    pe.wait_ge(copied.handle, copied.at(2 * (h - 1)))
                for m in range(2):
                    c = h * RET_DV + m * 96
                    ins = nc.tensor.matmul(k.ps[0:96, 2 + 2 * (h % 2) + m, j * P:SEQ], v[:, j, c:c + 96],
                                           att[:, u % 2, 0:SEQ - j * P], start=(j == 0), stop=(j == TT - 1))
                ins.then_inc(summed.handle, 1)

            for u in range(RET_H * TT + 1):
                if u < RET_H * TT:
                    scores(u)
                if u >= 1:
                    values(u - 1)

        @block.vector
        def _(dve):
            for u in range(RET_H * TT):
                h, j = u // TT, u % TT
                dve.wait_ge(scored.handle, scored.at(u + 1))
                if u >= 2:
                    dve.wait_ge(summed.handle, summed.at(u - 1))
                nc.vector.tensor_tensor(att[:, u % 2, 0:SEQ - j * P], k.ps[:, u % 2, 0:SEQ - j * P],
                                        decay[:, h, 0:SEQ - j * P], ALU.mult).then_inc(decayed.handle, 1)

        @block.scalar
        def _(act):
            for h in range(RET_H):
                act.wait_ge(summed.handle, summed.at((h + 1) * TT))
                for m in range(2):
                    nc.scalar.copy(out[0:96, 2 * h + m, :], k.ps[0:96, 2 + 2 * (h % 2) + m, :]).then_inc(copied.handle, 1)
    for g in (scored, decayed, summed):
        g.advance(RET_H * TT)
    copied.advance(2 * RET_H)
    layer_norm_f(k, [[out[0:96, 2 * h + m, :] for m in range(2)] for h in range(RET_H)], 96, scr)


def gate_and_project(k, layer, y, heights, scratch):
    nc = k.nc
    dense_gated(k, f"gate{layer}", k.xn, heights, ACT.Silu,
                lambda m, gate: nc.vector.tensor_tensor(y[0:heights[m], m, :], y[0:heights[m], m, :], gate, ALU.mult),
                scratch)
    rows_add(k, f"wo{layer}", y, heights, 1.0)


def second_even(k):
    nc = k.nc
    y = k.at(0, 20, SEQ)
    base = 10240
    memn = k.at(base, KT, NMEM)
    load(k, [(memn, k.dram["mem"])])
    rms(k, memn, memn, "memnorm_g", n=NMEM, scratch=base + 2048)
    rms(k, k.h, k.xn, "norm2_g0", scratch=base + 2048)
    mem_attention(k, 0, memn, y[:, 16:20], base + 2048)
    za = k.at(base + 2048, 8, SEQ)
    dense_f(k, "za", k.xn, [96] * 8, lambda m, ps: nc.scalar.copy(za[0:96, m, :], ps))
    pool_mixer(k, za, y[:, 0:8], base + 6144)
    qk = k.at(base + 2048, 8, SEQ)
    v = k.at(base + 6144, TT, 768)
    tab = k.at(base + 9216, 2, SEQ)
    decay = k.at(base + 10240, 4, SEQ)
    scr = base + 12288
    load(k, [(tab, k.dram["rotary"]), (decay, k.dram["decay"])])
    dense_f(k, "rqk", k.xn, [P] * 8, lambda m, ps: nc.scalar.copy(qk[:, m, :], ps))
    dense_t(k, "rv", k.xn, [256] * 3, lambda j, t, ps: nc.scalar.copy(v[:, t, j * 256:(j + 1) * 256], ps))
    norm_rope(k, [(qk[:, m, :], None, P ** -0.5 if m < 4 else 1.0) for m in range(8)], "rot128", "ones", P,
              tab[:, 0, :], tab[:, 1, :], scr)
    retention(k, qk[:, 0:4], qk[:, 4:8], v, y[:, 8:16], decay, scr)
    gate_and_project(k, 0, y, [96] * 16 + [P] * 4, scr)


def compress(k, kc, vc, kcmp, vcmp, scr):
    nc, s = k.nc, k.s
    m2 = NSA_G * NCMP
    x = k.at(scr, 64, 64)
    hid = k.at(scr + 4096, 4, 64)
    w2 = k.at(scr + 4352, 4, P)
    load(k, [(w2, k.dram["cmp_w2"])])
    ready, done, part, act_done = s["dve_step"], s["product_done"], s["pe_step"], s["act_step"]
    k.slabs_end(part, [part.at(j + 1) for j in range(8)])

    with nc.Block() as block:
        @block.sync
        def _(sp):
            k.stream(sp)

        @block.vector
        def _(dve):
            for kind, src in enumerate((kc, vc)):
                for l in range(32):
                    u = kind * 32 + l
                    dst = x[:, u, 0:m2].rearrange("p (g j) -> p g j", g=2)
                    nc.vector.tensor_scalar(dst, src[:, :, l:l + 16 * (NCMP - 1) + 1:16], k.v("cmp_pe", u), None,
                                            ALU.add).then_inc(ready.handle, 1)

        @block.tensor
        def _(pe):
            for kind in range(2):
                for j in range(4):
                    slab = k.slab(pe, STREAM_AT[f"cmp{kind}"][0] + j).rearrange("p (l m c) -> p l m c", l=8, c=P)
                    pe.wait_ge(ready.handle, ready.at(kind * 32 + 8 * (j + 1)))
                    for li in range(8):
                        for m in range(2):
                            l = 8 * j + li
                            ins = nc.tensor.matmul(k.ps[:, 2 * kind + m, 0:m2], slab[:, li, m, :],
                                                   x[:, kind * 32 + l, 0:m2], start=(l == 0), stop=(l == 31))
                    ins.then_inc(part.handle, 1)
            pe.wait_ge(act_done.handle, act_done.at(4))
            for c in range(2):
                ins = nc.tensor.matmul(k.ps[:, 4, 0:m2], w2[:, c, :], hid[:, c, 0:m2], start=(c == 0), stop=(c == 1))
            ins.then_inc(done.handle, 1)
            for g in range(2):
                for c in range(2):
                    ins = nc.tensor.matmul(k.ps[0:NCMP, 5 + g, 0:P], hid[:, 2 + c, g * NCMP:(g + 1) * NCMP], w2[:, 2 + c, :],
                                           start=(c == 0), stop=(c == 1))
                ins.then_inc(done.handle, 1)

        @block.scalar
        def _(act):
            for kind in range(2):
                act.wait_ge(part.handle, part.at(4 * (kind + 1)))
                for m in range(2):
                    nc.scalar.activation(hid[:, 2 * kind + m, 0:m2], k.ps[:, 2 * kind + m, 0:m2], ACT.Silu,
                                         bias=k.v("cmp_b1", 2 * kind + m)).then_inc(act_done.handle, 1)
            act.wait_ge(done.handle, done.at(1))
            nc.scalar.copy(kcmp[:, 0:m2], k.ps[:, 4, 0:m2])
            for g in range(2):
                act.wait_ge(done.handle, done.at(2 + g))
                nc.scalar.copy(vcmp[0:NCMP, g, :], k.ps[0:NCMP, 5 + g, 0:P])
    for g, v in ((ready, 64), (part, 8), (act_done, 4), (done, 3)):
        g.advance(v)


def distance_bias(k, bias, scr):
    nc, s = k.nc, k.s
    tab = k.at(scr, NSA_H)
    hot = k.at(scr + 16, FREV)
    frev = k.at(scr + 1040, FREV)
    half = BIASW // 2
    load(k, [(tab[0:32, :], k.dram["rel"]), (hot[0:33, :], k.dram["buckets"])])

    with nc.Block() as block:
        @block.vector
        def _(dve):
            nc.vector.tensor_scalar(tab[0:32, :], tab[0:32, :], -1.0, None, ALU.mult)
            nc.vector.memset(tab[32:33, :], BIG).then_inc(s["dve_step"].handle, 1)

        @block.tensor
        def _(pe):
            pe.wait_ge(s["dve_step"].handle, s["dve_step"].at(1))
            for j in range(2):
                nc.tensor.matmul(k.ps[0:NSA_H, j, :], tab[0:33, :], hot[0:33, j * SEQ:(j + 1) * SEQ], start=True,
                                 stop=True).then_inc(s["pe_step"].handle, 1)
            pe.wait_ge(k.aux.handle, k.aux.at(16))
            for h in range(NSA_H):
                if h >= 3:
                    pe.wait_ge(s["act_step"].handle, s["act_step"].at(2 + 2 * (h - 2)))
                for j in range(2):
                    ins = nc.tensor.matmul(k.ps[:, 2 + 2 * (h % 3) + j, 0:half], k.c("flip"),
                                           bias[:, h, j * half:(j + 1) * half], start=True, stop=True)
                ins.then_inc(s["pe_step"].handle, 1)

        @block.scalar
        def _(act):
            for j in range(2):
                act.wait_ge(s["pe_step"].handle, s["pe_step"].at(j + 1))
                nc.scalar.copy(frev[0:NSA_H, j * SEQ:(j + 1) * SEQ], k.ps[0:NSA_H, j, :]).then_inc(s["act_step"].handle, 1)
            for h in range(NSA_H):
                act.wait_ge(s["pe_step"].handle, s["pe_step"].at(h + 3))
                for j in range(2):
                    nc.scalar.copy(bias[:, h, j * half:(j + 1) * half],
                                   k.ps[:, 2 + 2 * (h % 3) + j, 0:half]).then_inc(s["act_step"].handle, 1)

        @block.sync
        def _(sp):
            sp.wait_ge(s["act_step"].handle, s["act_step"].at(2))
            sp.dma_start(k.dram["frev"], frev[0:NSA_H, :]).then_inc(k.stored.handle, 16)
            sp.wait_ge(k.stored.handle, k.stored.at(16))
            rows = bass.AP(k.dram["frev"].tensor, 0, [[1, P], [FREV, NSA_H], [1, BIASW]])
            sp.dma_start(bias, rows).then_inc(k.aux.handle, 16)
            sp.wait_ge(k.aux.handle, k.aux.at(16))
    s["dve_step"].advance(1)
    s["pe_step"].advance(2 + NSA_H)
    s["act_step"].advance(2 + 2 * NSA_H)
    k.stored.advance(16)
    k.aux.advance(16)


def second_odd(k):
    nc, s = k.nc, k.s
    y = k.at(0, 16, SEQ)
    base = 8192
    memn = k.at(base, KT, NMEM)
    small = k.at(base, 384)
    load(k, [(memn, k.dram["mem"])])
    rms(k, memn, memn, "memnorm_g", n=NMEM, scratch=base + 2048)
    rms(k, k.h, k.xn, "norm2_g1", scratch=base + 2048)
    mem_attention(k, 1, memn, y[:, 12:16], base + 2048)
    kcmp = k.at(base, 64)
    vcmp = k.at(base + 64, 2, P)
    gl = k.at(base + 320, TT, 36)
    seen = k.at(base + 464, TT, NSA_H)
    kvc = k.at(base + 512, 4, SEQ)
    dense_f(k, "kvc", k.xn, [P] * 4, lambda m, ps: nc.scalar.copy(kvc[:, m, :], ps))
    compress(k, kvc[:, 0:2], kvc[:, 2:4], kcmp, vcmp, base + 2560)

    keys = k.at(base + 512, 4, SEQ)
    vals = k.at(base + 2560, TT, 512)
    bias = k.at(base + 4608, NSA_H, BIASW)
    scr = base + 4608 + NSA_H * BIASW
    distance_bias(k, bias, scr)
    dense_f(k, "nsaq", k.xn, [P] * 12, lambda m, ps: nc.scalar.mul(y[:, m, :], ps, -(P ** -0.5)))
    dense_f(k, "nsak", k.xn, [P] * 4, lambda m, ps: nc.scalar.copy(keys[:, m, :], ps))

    def evac(j, t, ps):
        if j == 2:
            return nc.scalar.activation(gl[:, t, :], ps, ACT.Sigmoid)
        return nc.scalar.copy(vals[:, t, j * 256:(j + 1) * 256], ps)

    dense_t(k, "nsav", k.xn, [256, 256, 36], evac)
    with nc.Block() as block:
        @block.vector
        def _(dve):
            nc.vector.tensor_scalar(gl[:, 0, 0:NSA_H], gl[:, 0, 0:NSA_H], k.c("seen"), None, ALU.mult)

    units = []
    for i in range(TT):
        q = slice(i * P, (i + 1) * P)
        w = P * (i + 1)
        for h in range(NSA_H):
            g = h // 6
            qh = y[:, h, q]
            c0 = 415 - P * i
            units.append(Unit(qh, kcmp[:, g * NCMP:(g + 1) * NCMP], bias[:, h, c0:c0 + 16 * (NCMP - 1) + 1:16],
                              [(NCMP, vcmp[0:NCMP, g, :])], gate=gl[:, i, h:h + 1], last=False))
            for b in range(2):
                units.append(Unit(qh, keys[:, 2 * b + g, 0:w], bias[:, h, SEQ - w:SEQ],
                                  [(P, vals[:, j, b * 256 + g * P:b * 256 + (g + 1) * P]) for j in range(i + 1)],
                                  gate=gl[:, i, NSA_H * (b + 1) + h:NSA_H * (b + 1) + h + 1], first=False,
                                  last=(b == 1), dst=qh))
    attention(k, units, scr)
    gate_and_project(k, 1, y, [P] * 16, scr)


def finish(k):
    nc = k.nc
    rms(k, k.h, k.xn, "final_g", scratch=0)
    with nc.Block() as block:
        @block.sync
        def _(sp):
            sp.dma_start(k.dram["out"], k.xn[:, :, :]).then_inc(k.stored.handle, 16)
            sp.wait_ge(k.stored.handle, k.stored.at(16))
    k.stored.advance(16)


def build(nc, dram):
    with ExitStack() as ctx:
        k = Core(nc, ctx, dram)
        start(k)
        for layer in range(2):
            ffn(k, "ffn1", layer)
            (odd_mixer if layer else even_mixer)(k)
            ffn(k, "ffn2", layer)
            ple(k, layer)
        second_even(k)
        second_odd(k)
        finish(k)


def kernel(**inputs):
    import concourse.bacc as bacc
    from concourse.bass_utils import run_bass_kernel_spmd as run

    a = {n: np.asarray(v) for n, v in inputs.items()}

    def feature_major(x):
        return np.ascontiguousarray(x.T.reshape(-1, P, x.shape[0]).transpose(1, 0, 2))

    arrays = {
        "x": feature_major(a["x"][0]),
        "p": np.stack([feature_major(a["p"][l, 0]) for l in range(2)]),
        "mem": feature_major(a["mem_2"][0]),
        "pos": np.ascontiguousarray(a["pos"].reshape(1, SEQ)),
        "stream": lay_stream(a),
        "vec": lay_vectors(a),
        "cst": np.concatenate([CONSTS[n] for n in CONST_AT], axis=1),
        "w_uv": np.ascontiguousarray(a["a_w_uv"][0].transpose(1, 0, 2).reshape(P, 512)),
        "w_s": np.ascontiguousarray(a["c_w_s"][0].transpose(2, 0, 1)),
        "b_s": np.ascontiguousarray(np.repeat(a["c_b_s"][0], 64, axis=0).reshape(4, P, P).transpose(1, 0, 2)),
        "cln": np.concatenate([a["c_ln_g"], a["c_ln_b"]], axis=0),
        "pool_w": np.ascontiguousarray(a["ev_pool_w_2"][0].reshape(8, 96, 192).transpose(1, 0, 2)),
        "pool_recip": pool_tables().reshape(P, 4, SEQ),
        "rotary": rotary_tables().reshape(P, 2, SEQ),
        "decay": decay_tables().reshape(P, 4, SEQ),
        "cmp_w2": np.ascontiguousarray(a["od_cmp_w2_2"][0].reshape(4, P, P).transpose(1, 0, 2)),
        "rel": np.ascontiguousarray(a["rel_bias_2"]),
        "buckets": bucket_table(),
    }
    nc = bacc.Bacc("TRN2", target_bir_lowering=False, num_devices=1)
    dram = {n: nc.dram_tensor(f"in_{n}", v.shape, mybir.dt.from_np(v.dtype), kind="ExternalInput").ap()
            for n, v in arrays.items()}
    dram["frev"] = nc.dram_tensor("frev", (NSA_H, FREV), F32, kind="Internal").ap()
    dram["out"] = nc.dram_tensor("out_0", (P, KT, SEQ), F32, kind="ExternalOutput").ap()
    build(nc, dram)
    r = run(nc, [{f"in_{n}": v for n, v in arrays.items()}], core_ids=[0])
    got = r.results[0]["out_0"]
    return np.ascontiguousarray(got.transpose(2, 1, 0).reshape(1, SEQ, D))
```

```python
from contextlib import ExitStack

import numpy as np

import concourse.bass as bass
from concourse import mybir
from concourse.alu_op_type import AluOpType as ALU

F32 = mybir.dt.float32
F32R = mybir.dt.float32r
I32 = mybir.dt.int32
ACT = mybir.ActivationFunctionType
AX = mybir.AxisListType

P = 128
SEQ = 512
TT = SEQ // P
D = 1024
KT = D // P
DFF = 2816
FT = DFF // P
EPS = 1e-6
BIG = 1e30
RING = 3
SPLIT = 3
SLAB = 1024
NMEM = 256
POOL_W = (2, 4, 8, 16)
RET_H, RET_DV = 4, 192
NSA_H, NSA_G, NSA_D = 12, 2, 128
NCMP = (SEQ - 32) // 16 + 1
BIASW = 896
FREV = 1024
TOPK = 128
SHRINK = 2.0 ** -40
OVERFLOW = 3.4028235e38 * SHRINK ** 2


def t5_bucket(rel):
    n = np.maximum(rel, 0)
    nf = np.maximum(n, 1).astype(np.float32)
    large = 16 + (np.log(nf / np.float32(16)) / np.float32(np.log(8.0)) * np.float32(16)).astype(np.int32)
    return np.where(n < 16, n, np.minimum(large, 31))


def constant_pack():
    p = np.arange(P)
    f = np.float32
    out = {}
    out["ident"] = np.eye(P, dtype=f)
    out["flip"] = np.eye(P, dtype=f)[::-1]
    out["ones"] = np.ones((P, P), f)
    out["ones64"] = (p[:, None] // 64 == p[None, :] // 64).astype(f)
    for name, half in (("rot64", 32), ("rot128", 64)):
        r = np.zeros((P, P), f)
        for m in range(P):
            if m % (2 * half) < half:
                r[m + half, m] = -1.0
            else:
                r[m - half, m] = 1.0
        out[name] = r
    y = np.arange(SEQ)
    out["chunkmask"] = np.where((y[None, :] >= 448) & (p[:, None] < 64), f(BIG), f(0)).astype(f)
    inv = (10000.0 ** (-np.arange(0, 64, 2) / 64)).astype(f)
    out["inv64"] = inv[p % 32][:, None]
    out["seen"] = (p >= 31).astype(f)[:, None]
    out["eps"] = np.full((P, 1), EPS, f)
    out["eps_small"] = np.full((P, 1), EPS * SHRINK ** 2, f)
    return out


def rotary_tables():
    f = np.float32
    inv = (10000.0 ** (-np.arange(64) / 64)).astype(f)
    ang = (np.arange(SEQ, dtype=f)[None, :] * inv[:, None]).astype(f)
    c, s = np.cos(ang), np.sin(ang)
    return np.concatenate([np.tile(c, (2, 1)), np.tile(s, (2, 1))], axis=1).astype(f)


def decay_tables():
    m, x = np.arange(P)[:, None], np.arange(SEQ)[None, :]
    out = []
    for h in range(RET_H):
        lg = np.log(1.0 - 2.0 ** (-5.0 - h))
        out.append(np.where(x >= m, np.exp(lg * np.maximum(x - m, 0)), 0.0))
    return np.concatenate(out, axis=1).astype(np.float32)


def pool_tables():
    t = np.arange(SEQ)
    return np.tile(np.concatenate([1.0 / np.minimum(t + 1, w) for w in POOL_W])[None], (P, 1)).astype(np.float32)


def bucket_table():
    z = np.arange(FREV)
    rel = 511 - z
    out = np.zeros((33, FREV), np.float32)
    b = t5_bucket(rel)
    out[b[z <= 511], z[z <= 511]] = 1.0
    out[32, z > 511] = 1.0
    return out


CONSTS = constant_pack()
CONST_AT = {}
_at = 0
for _n, _a in CONSTS.items():
    CONST_AT[_n] = (_at, _a.shape[1])
    _at += _a.shape[1]
CONST_N = _at

def tiles(lo, n, w=P):
    return [(lo + i * w, w) for i in range(n)]


EV = dict(aq=0, ak=512, av=576, iq=704, ik=960, iw=1024, bq=1028, bk=1540, bv=2052)
EV_F = (tiles(EV["aq"], 4) + [(EV["ak"], 64, 2)] + tiles(EV["iq"], 2) + [(EV["ik"], 64, 2)]
        + tiles(EV["bq"], 4) + tiles(EV["bk"], 4))
EV_T = [(EV["av"], P), (EV["iw"], 4)] + tiles(EV["bv"], 4)
OD_F = tiles(0, 4) + tiles(1024, 8)
OD_T = tiles(512, 4)
E2 = dict(za=0, rq=768, rk=1280, rv=1792, xq=2560, gate=3072)
O2 = dict(q=0, kc=1536, vc=1792, ks=2048, vs=2304, kw=2560, vw=2816, gl=3072, xq=3108, gate=3620)


def stream_plan():
    plan = []
    for l in range(2):
        for n in ("ffn1", "mix", "ffn2"):
            if n == "mix":
                if l == 0:
                    plan += [("ev_f", "ev_w_in", 0, "cols", EV_F), ("ev_t", "ev_w_in", 0, "tcols", EV_T),
                             ("ev_out", "ev_w_out", 0, "rows", tiles(0, KT))]
                else:
                    plan += [("od_f", "od_w_in", 0, "cols", OD_F), ("od_t", "od_w_in", 0, "tcols", OD_T),
                             ("od_out", "od_w_out", 0, "rows", tiles(0, KT))]
                continue
            plan += [(f"{n}_up{l}", (f"{n}_wg", f"{n}_wu"), l, "pair", tiles(0, FT)),
                     (f"{n}_down{l}", f"{n}_wd", l, "rows", tiles(0, FT))]
        plan += [(f"ple_p{l}", "ple_wproj", l, "rows", tiles(0, 2)),
                 (f"ple_g{l}", "ple_wgate", l, "cols", tiles(0, KT))]
    for l, (w, c, kv, wo) in enumerate((("ev_w_in_2", E2, "ev_w_mem_kv_2", "ev_w_out_2"),
                                        ("od_w_in_2", O2, "od_w_mem_kv_2", "od_w_out_2"))):
        plan += [(f"mk{l}", kv, 0, "cols", tiles(0, 4)), (f"mv{l}", kv, 0, "tcols", tiles(512, 4)),
                 (f"xq{l}", w, 0, "cols", tiles(c["xq"], 4))]
        if l == 0:
            plan += [("za", w, 0, "cols", tiles(c["za"], 8, 96)),
                     ("rqk", w, 0, "cols", tiles(c["rq"], 8)), ("rv", w, 0, "tcols", tiles(c["rv"], 6)),
                     ("gate0", w, 0, "cols", tiles(c["gate"], 16, 96) + tiles(c["gate"] + 1536, 4)),
                     ("wo0", wo, 0, "rows", tiles(0, 16, 96) + tiles(1536, 4))]
        else:
            plan += [("kvc", w, 0, "cols", tiles(c["kc"], 4)),
                     ("cmp0", "od_cmp_w1_2", 0, "rows4", tiles(0, 32)),
                     ("cmp1", "od_cmp_w1_2", 1, "rows4", tiles(0, 32)),
                     ("nsaq", w, 0, "cols", tiles(c["q"], 12)),
                     ("nsak", w, 0, "cols", tiles(c["ks"], 2) + tiles(c["kw"], 2)),
                     ("nsav", w, 0, "tcols", tiles(c["vs"], 2) + tiles(c["vw"], 2) + [(c["gl"], 36)]),
                     ("gate1", w, 0, "cols", tiles(c["gate"], 16)),
                     ("wo1", wo, 0, "rows", tiles(0, 16))]
    return plan


def slab_count(kind, t):
    return {"cols": len(t), "tcols": 2 * ((len(t) + 1) // 2), "pair": 2 * len(t), "rows": len(t),
            "rows4": len(t) // 4}[kind]


PLAN = stream_plan()
STREAM_AT = {}
_at = 0
for _s, _w, _l, _k, _t in PLAN:
    STREAM_AT[_s] = (_at, slab_count(_k, _t))
    _at += slab_count(_k, _t)
NSLAB = _at


def lay_stream(inputs):
    out = np.zeros((NSLAB, P, SLAB), np.float32)

    def column_slabs(w, t, at, step):
        w3 = w.reshape(KT, P, -1).transpose(1, 0, 2)
        for i, tile in enumerate(t):
            lo, n = tile[:2]
            view = out[at + i * step].reshape(P, KT, P)
            for r in range(tile[2] if len(tile) > 2 else 1):
                view[:, :, r * n:(r + 1) * n] = w3[:, :, lo:lo + n]

    for stage, name, layer, kind, t in PLAN:
        at, _ = STREAM_AT[stage]
        if kind == "pair":
            for j in range(2):
                column_slabs(inputs[name[j]][layer], t, at + j, 2)
        elif kind == "cols":
            column_slabs(inputs[name][layer], t, at, 1)
        elif kind == "tcols":
            w3 = inputs[name][layer].reshape(KT, P, -1).transpose(1, 0, 2)
            for i, (lo, n) in enumerate(t):
                for half in range(2):
                    view = out[at + 2 * (i // 2) + half].reshape(P, 4, 2, P)
                    view[:, :, i % 2, 0:n] = w3[:, 4 * half:4 * half + 4, lo:lo + n]
        elif kind == "rows":
            for i, (lo, n) in enumerate(t):
                out[at + i, :n] = inputs[name][layer][lo:lo + n]
        else:
            w = inputs[name][0, layer].reshape(8, 4, P, 256)
            out[at:at + 8] = w.transpose(0, 2, 1, 3).reshape(8, P, SLAB)
    return out


VEC = []
for _l in range(2):
    VEC += [(f"ffn1_g{_l}", "ffn1_g", _l, P), (f"mix_g{_l}", "mix_g", _l, P), (f"ffn2_g{_l}", "ffn2_g", _l, P),
            (f"ple_g{_l}", "ple_g", _l, P), (f"norm2_g{_l}", "norm_g_2", _l, P)]
VEC += [("final_g", "final_g_2", None, P), ("memnorm_g", "mem_norm_g_2", None, P),
        ("subln_g", "b_subln_g", 0, P), ("conv_b", "d_conv_b", 0, P),
        ("dln_g", "d_ln_g", 0, P), ("dln_b", "d_ln_b", 0, P), ("pool_scale", "ev_pool_scale_2", 0, 96)]
VEC_N = {"ffn1_g": 8, "mix_g": 8, "ffn2_g": 8, "ple_g": 8, "norm_g_2": 8, "final_g_2": 8, "mem_norm_g_2": 8,
         "b_subln_g": 1, "d_conv_b": 4, "d_ln_g": 4, "d_ln_b": 4, "ev_pool_scale_2": 8}
VEC_AT = {}
_at = 0
for _n, _a, _i, _w in VEC:
    VEC_AT[_n] = (_at, VEC_N[_a])
    _at += VEC_N[_a]
for _n, _c in (("aq_g", 1), ("ak_g", 1), ("bq_g", 1), ("bk_g", 1), ("conv_w", 4 * 31), ("lams", 4),
               ("cmp_b1", 4), ("cmp_pe", 64)):
    VEC_AT[_n] = (_at, _c)
    _at += _c
VEC_TOTAL = _at


def lay_vectors(inputs):
    out = np.zeros((P, VEC_TOTAL), np.float32)
    for name, arr, idx, w in VEC:
        at, n = VEC_AT[name]
        a = inputs[arr] if idx is None else inputs[arr][idx]
        out[:w, at:at + n] = a.reshape(n, w).T
    for name, arr in (("aq_g", "a_q_g"), ("ak_g", "a_k_g"), ("bq_g", "b_q_g"), ("bk_g", "b_k_g")):
        out[0:64, VEC_AT[name][0]] = inputs[arr][0]
        out[64:128, VEC_AT[name][0]] = inputs[arr][0]
    at = VEC_AT["conv_w"][0]
    out[:, at:at + 124] = inputs["d_conv_w"][0].reshape(31, 4, P).transpose(2, 1, 0).reshape(P, 124)
    at = VEC_AT["lams"][0]
    for j, arr in enumerate(("b_lam_q1", "b_lam_k1", "b_lam_q2", "b_lam_k2")):
        out[0:64, at + j] = inputs[arr][0]
    at = VEC_AT["cmp_b1"][0]
    out[:, at:at + 4] = inputs["od_cmp_b1_2"][0].reshape(4, P).T
    at = VEC_AT["cmp_pe"][0]
    out[:, at:at + 64] = inputs["od_cmp_pe_2"][0].reshape(64, P).T
    return out


class Signal:

    def __init__(self, handle):
        self.handle, self.base = handle, 0

    def at(self, n):
        return self.base + n

    def advance(self, n):
        self.base += n


class Core:

    def __init__(self, nc, ctx, dram):
        self.nc, self.dram = nc, dram
        self.ctx = ctx
        sb = lambda n, s, dt=F32: ctx.enter_context(nc.sbuf_tensor(n, s, dt))
        self.ring = sb("ring", [P, RING, SLAB])
        self.w_hi = sb("w_hi", [P, SPLIT, SLAB], F32R)
        self.w_lo = sb("w_lo", [P, SPLIT, SLAB], F32R)
        self.h = sb("h", [P, KT, SEQ])
        self.x_hi = sb("x_hi", [P, KT, SEQ], F32R)
        self.x_lo = sb("x_lo", [P, KT, SEQ], F32R)
        self.r_hi = sb("r_hi", [P, 2, SEQ], F32R)
        self.r_lo = sb("r_lo", [P, 2, SEQ], F32R)
        self.cst = sb("cst", [P, CONST_N])
        self.vec = sb("vec", [P, VEC_TOTAL])
        self.arena_n = (nc.sbuf_top - nc.sbuf_base) // 4 - 8
        self.arena = sb("arena", [P, self.arena_n])
        self.ps = ctx.enter_context(nc.psum_tensor("ps", [P, 8, SEQ], F32))
        names = ("slab_free", "product_done", "evacuated", "squares_done", "sum_done", "root_done", "root_read",
                 "vec_chain", "act_chain", "pool_chain", "act_step", "dve_step", "pe_step", "dve_read", "act_read",
                 "scores_done", "biased", "exp_done", "diag_done", "turned", "turned_copied", "out_done",
                 "out_copied", "pool_step", "pe_step2", "tmp_ready", "split_done", "high_done", "hi_done", "lo_done", "raw_done")
        self.s = {n: Signal(ctx.enter_context(nc.semaphore(n))) for n in names}
        self.slab_loaded = [ctx.enter_context(nc.semaphore(f"slab_loaded{i}")) for i in range(RING)]
        self.aux = Signal(ctx.enter_context(nc.semaphore("aux_loaded")))
        self.stored = Signal(ctx.enter_context(nc.semaphore("stored")))
        self.loaded = self.highs = self.lows = 0
        self.slab_end = []

    def c(self, name):
        a, n = CONST_AT[name]
        return self.cst[:, a:a + n]

    def v(self, name, j=0, rows=P):
        a, _ = VEC_AT[name]
        return self.vec[0:rows, a + j:a + j + 1]

    def at(self, off, *shape):
        n = int(np.prod(shape))
        assert off + n <= self.arena_n, (off, shape, self.arena_n)
        a = self.arena[:, off:off + n]
        if len(shape) == 2:
            a = a.rearrange("p (a b) -> p a b", b=shape[1])
        elif len(shape) == 3:
            a = a.rearrange("p (a b c) -> p a b c", b=shape[1], c=shape[2])
        return a

    def vlink(self, ins):
        s = self.s["vec_chain"]
        ins.then_inc(s.handle, 1)
        s.advance(1)
        self.nc.vector.wait_ge(s.handle, s.base)

    def alink(self, ins):
        s = self.s["act_chain"]
        ins.then_inc(s.handle, 1)
        s.advance(1)
        self.nc.scalar.wait_ge(s.handle, s.base)

    def plink(self, ins):
        s = self.s["pool_chain"]
        ins.then_inc(s.handle, 1)
        s.advance(1)
        self.nc.gpsimd.wait_ge(s.handle, s.base)

    def slabs_end(self, signal, values):
        self.slab_end += [(signal.handle, v) for v in values]

    def stream(self, sp):
        while self.loaded < min(NSLAB, len(self.slab_end) + SPLIT + RING):
            n = self.loaded
            if n >= RING:
                sp.wait_ge(self.s["split_done"].handle, n - RING + 1)
            sp.dma_start(self.ring[:, n % RING, :], self.dram["stream"][n]).then_inc(self.slab_loaded[n % RING], 16)
            self.loaded += 1

    def high(self, act, upto):
        while self.highs < min(NSLAB, upto):
            n = self.highs
            act.wait_ge(self.slab_loaded[n % RING], 16 * (n // RING + 1))
            if n >= SPLIT:
                act.wait_ge(*self.slab_end[n - SPLIT])
            self.nc.scalar.copy(self.w_hi[:, n % SPLIT, :],
                                self.ring[:, n % RING, :]).then_inc(self.s["high_done"].handle, 1)
            self.highs += 1

    def all_high(self, act):
        self.high(act, len(self.slab_end) + SPLIT)

    def low(self, pool):
        while self.lows < min(NSLAB, len(self.slab_end) + SPLIT):
            n = self.lows
            pool.wait_ge(self.s["high_done"].handle, n + 1)
            self.nc.gpsimd.tensor_tensor(self.w_lo[:, n % SPLIT, :], self.ring[:, n % RING, :],
                                         self.w_hi[:, n % SPLIT, :].bitcast(F32),
                                         ALU.subtract).then_inc(self.s["split_done"].handle, 1)
            self.lows += 1

    def slab(self, pe, n, *shape):
        pe.wait_ge(self.s["split_done"].handle, n + 1)
        parts = self.w_hi[:, n % SPLIT, :], self.w_lo[:, n % SPLIT, :]
        return [w.rearrange("p (a b) -> p a b", b=shape[-1]) for w in parts]

    def product(self, out, a, b, start, stop):
        nc = self.nc
        nc.tensor.matmul(out, a[0], b[0], start=start, stop=False)
        nc.tensor.matmul(out, a[0], b[1], start=False, stop=False)
        return nc.tensor.matmul(out, a[1], b[0], start=False, stop=stop)


def start(k):
    nc = k.nc

    with nc.Block() as block:
        @block.sync
        def _(sp):
            sp.dma_start(k.h[:, :, :], k.dram["x"]).then_inc(k.aux.handle, 16)
            sp.dma_start(k.vec[:, :], k.dram["vec"]).then_inc(k.aux.handle, 16)
            sp.dma_start(k.cst[:, :], k.dram["cst"]).then_inc(k.aux.handle, 16)
            k.stream(sp)
            sp.wait_ge(k.aux.handle, k.aux.at(48))

        @block.gpsimd
        def _(pool):
            k.low(pool)

        @block.scalar
        def _(act):
            k.all_high(act)
    k.aux.advance(48)


def load(k, pairs):
    with k.nc.Block() as block:
        @block.sync
        def _(sp):
            for dst, src in pairs:
                sp.dma_start(dst, src).then_inc(k.aux.handle, 16)
            sp.wait_ge(k.aux.handle, k.aux.at(16 * len(pairs)))
    k.aux.advance(16 * len(pairs))


def rms(k, src, gain, n=SEQ, scratch=0, dst=None):
    nc, s = k.nc, k.s
    sq = k.at(scratch, 2, SEQ)
    root = k.at(scratch + 2 * SEQ, SEQ)
    inv = k.at(scratch + 3 * SEQ, SEQ)
    raw = k.at(scratch + 4 * SEQ, 2, SEQ)
    raws, his = s["raw_done"], s["hi_done"]

    with nc.Block() as block:
        @block.scalar
        def _(act):
            for c in range(KT):
                if c >= 2:
                    act.wait_ge(s["sum_done"].handle, s["sum_done"].at(c - 1))
                nc.scalar.activation(sq[:, c % 2, 0:n], src[:, c, 0:n], ACT.Square).then_inc(s["squares_done"].handle, 1)
            act.wait_ge(s["sum_done"].handle, s["sum_done"].at(KT))
            nc.scalar.activation(root[:, 0:n], k.ps[:, 0, 0:n], ACT.Sqrt, bias=k.c("eps"),
                                 scale=1.0 / D).then_inc(s["root_done"].handle, 1)
            for c in range(KT if dst is None else 0):
                act.wait_ge(raws.handle, raws.at(c + 1))
                nc.scalar.copy(k.x_hi[:, c, 0:n], raw[:, c % 2, 0:n]).then_inc(his.handle, 1)

        @block.tensor
        def _(pe):
            for c in range(KT):
                pe.wait_ge(s["squares_done"].handle, s["squares_done"].at(c + 1))
                nc.tensor.matmul(k.ps[:, 0, 0:n], k.c("ones"), sq[:, c % 2, 0:n], start=(c == 0),
                                 stop=(c == KT - 1)).then_inc(s["sum_done"].handle, 1)

        @block.vector
        def _(dve):
            def low(c):
                dve.wait_ge(his.handle, his.at(c + 1))
                k.vlink(nc.vector.tensor_tensor(k.x_lo[:, c, 0:n], raw[:, c % 2, 0:n],
                                                k.x_hi[:, c, 0:n].bitcast(F32), ALU.subtract))

            dve.wait_ge(s["root_done"].handle, s["root_done"].at(1))
            k.vlink(nc.vector.reciprocal(inv[:, 0:n], root[:, 0:n]))
            for c in range(KT):
                out = raw[:, c % 2, 0:n] if dst is None else dst[:, c, 0:n]
                nc.vector.scalar_tensor_tensor(out, src[:, c, 0:n], k.v(gain, c), inv[:, 0:n],
                                               ALU.mult, ALU.mult).then_inc(raws.handle, 1)
                if dst is None and c >= 1:
                    low(c - 1)
            if dst is None:
                low(KT - 1)
    for g, v in (("squares_done", KT), ("sum_done", KT), ("root_done", 1), ("raw_done", KT),
                 ("hi_done", KT if dst is None else 0)):
        s[g].advance(v)


def dense_f(k, stage, widths, evacuate, n=SEQ):
    nc, s = k.nc, k.s
    first, slabs = STREAM_AT[stage]
    done, read = s["product_done"], s["evacuated"]
    assert slabs == len(widths)
    k.slabs_end(done, [done.at(m + 1) for m in range(slabs)])

    with nc.Block() as block:
        @block.sync
        def _(sp):
            k.stream(sp)

        @block.gpsimd
        def _(pool):
            k.low(pool)

        @block.tensor
        def _(pe):
            for m, w in enumerate(widths):
                hi, lo = k.slab(pe, first + m, P)
                if m >= 8:
                    pe.wait_ge(read.handle, read.at(m - 7))
                for c in range(KT):
                    ins = k.product(k.ps[0:w, m % 8, 0:n], (hi[:, c, 0:w], lo[:, c, 0:w]),
                                    (k.x_hi[:, c, 0:n], k.x_lo[:, c, 0:n]), c == 0, c == KT - 1)
                ins.then_inc(done.handle, 1)

        @block.scalar
        def _(act):
            for m, w in enumerate(widths):
                k.high(act, first + m + SPLIT)
                act.wait_ge(done.handle, done.at(m + 1))
                k.high(act, first + m + 1 + SPLIT)
                evacuate(m, k.ps[0:w, m % 8, 0:n]).then_inc(read.handle, 1)
    done.advance(slabs)
    read.advance(slabs)


def dense_t(k, stage, widths, evacuate, tts=TT):
    nc, s = k.nc, k.s
    first, slabs = STREAM_AT[stage]
    part, done, read = s["pe_step"], s["product_done"], s["evacuated"]
    assert slabs == 2 * len(widths)
    for j in range(len(widths)):
        k.slabs_end(part, [part.at(j + 1)])
        k.slabs_end(done, [done.at(tts * (j + 1))])

    with nc.Block() as block:
        @block.sync
        def _(sp):
            k.stream(sp)

        @block.gpsimd
        def _(pool):
            k.low(pool)

        @block.tensor
        def _(pe):
            for j, w in enumerate(widths):
                for half in range(2):
                    hi, lo = k.slab(pe, first + 2 * j + half, 256)
                    for t in range(tts):
                        u = j * tts + t
                        if u >= 8 and half == 0:
                            pe.wait_ge(read.handle, read.at(u - 7))
                        tok = slice(t * P, (t + 1) * P)
                        for ci in range(4):
                            c = 4 * half + ci
                            ins = k.product(k.ps[:, u % 8, 0:w], (k.x_hi[:, c, tok], k.x_lo[:, c, tok]),
                                            (hi[:, ci, 0:w], lo[:, ci, 0:w]), c == 0, c == KT - 1)
                        if half:
                            ins.then_inc(done.handle, 1)
                    if half == 0:
                        ins.then_inc(part.handle, 1)

        @block.scalar
        def _(act):
            for j, w in enumerate(widths):
                for t in range(tts):
                    u = j * tts + t
                    k.high(act, first + 2 * j + 1 + SPLIT)
                    act.wait_ge(done.handle, done.at(u + 1))
                    evacuate(j, t, k.ps[:, u % 8, 0:w]).then_inc(read.handle, 1)
            k.all_high(act)
    part.advance(len(widths))
    done.advance(tts * len(widths))
    read.advance(tts * len(widths))


def dense_gated(k, stage, widths, func, finish, scratch):
    nc, s = k.nc, k.s
    first, slabs = STREAM_AT[stage]
    done, gate, read = s["product_done"], s["act_step"], s["evacuated"]
    buf = k.at(scratch, 4, SEQ)
    n = len(widths)
    k.slabs_end(done, [done.at(m + 1) for m in range(n)])

    with nc.Block() as block:
        @block.sync
        def _(sp):
            k.stream(sp)

        @block.gpsimd
        def _(pool):
            k.low(pool)

        @block.tensor
        def _(pe):
            for m, w in enumerate(widths):
                hi, lo = k.slab(pe, first + m, P)
                if m >= 8:
                    pe.wait_ge(gate.handle, gate.at(m - 7))
                for c in range(KT):
                    ins = k.product(k.ps[0:w, m % 8, :], (hi[:, c, 0:w], lo[:, c, 0:w]),
                                    (k.x_hi[:, c, :], k.x_lo[:, c, :]), c == 0, c == KT - 1)
                ins.then_inc(done.handle, 1)

        @block.scalar
        def _(act):
            for m, w in enumerate(widths):
                k.high(act, first + m + SPLIT)
                act.wait_ge(done.handle, done.at(m + 1))
                k.high(act, first + m + 1 + SPLIT)
                if m >= 4:
                    act.wait_ge(read.handle, read.at(m - 3))
                nc.scalar.activation(buf[0:w, m % 4, :], k.ps[0:w, m % 8, :], func).then_inc(gate.handle, 1)

        @block.vector
        def _(dve):
            for m, w in enumerate(widths):
                dve.wait_ge(gate.handle, gate.at(m + 1))
                finish(m, buf[0:w, m % 4, :]).then_inc(read.handle, 1)
    for g in (done, gate, read):
        g.advance(n)


def rows(k, stage, x, heights, evacuate):
    nc, s = k.nc, k.s
    first, slabs = STREAM_AT[stage]
    n = len(heights)
    part, done, his, los = s["pe_step"], s["product_done"], s["hi_done"], s["lo_done"]
    assert slabs == n
    k.slabs_end(part, [part.at(j + 1) for j in range(n - 1)])
    k.slabs_end(done, [done.at(KT)])

    with nc.Block() as block:
        @block.sync
        def _(sp):
            k.stream(sp)

        @block.gpsimd
        def _(pool):
            k.low(pool)

        @block.scalar
        def _(act):
            for i, w in enumerate(heights):
                if i >= 2:
                    k.high(act, first + i - 2 + SPLIT)
                    act.wait_ge(part.handle, part.at(i - 1))
                nc.scalar.copy(k.r_hi[0:w, i % 2, :], x[0:w, i, :]).then_inc(his.handle, 1)
            k.all_high(act)

        @block.tensor
        def _(pe):
            for i, w in enumerate(heights):
                hi, lo = k.slab(pe, first + i, P)
                pe.wait_ge(los.handle, los.at(i + 1))
                for m in range(KT):
                    ins = k.product(k.ps[:, m, :], (hi[0:w, m, :], lo[0:w, m, :]),
                                    (k.r_hi[0:w, i % 2, :], k.r_lo[0:w, i % 2, :]), i == 0, i == n - 1)
                    if i == n - 1:
                        ins.then_inc(done.handle, 1)
                if i < n - 1:
                    ins.then_inc(part.handle, 1)

        @block.vector
        def _(dve):
            for i, w in enumerate(heights):
                dve.wait_ge(his.handle, his.at(i + 1))
                nc.vector.tensor_tensor(k.r_lo[0:w, i % 2, :], x[0:w, i, :], k.r_hi[0:w, i % 2, :].bitcast(F32),
                                        ALU.subtract).then_inc(los.handle, 1)
            for m in range(KT):
                dve.wait_ge(done.handle, done.at(m + 1))
                evacuate(m, k.ps[:, m, :])
    part.advance(n - 1)
    done.advance(KT)
    his.advance(n)
    los.advance(n)


def rows_add(k, stage, x, heights, scale):
    rows(k, stage, x, heights,
         lambda m, ps: k.nc.vector.scalar_tensor_tensor(k.h[:, m, :], ps, scale, k.h[:, m, :], ALU.mult, ALU.add))


def ffn(k, name, layer):
    nc, s = k.nc, k.s
    hidden = k.at(0, FT, SEQ)
    rms(k, k.h, f"{name}_g{layer}", scratch=FT * SEQ)
    first, slabs = STREAM_AT[f"{name}_up{layer}"]
    part, done, gate, read = s["pe_step"], s["product_done"], s["act_step"], s["evacuated"]
    for f in range(FT):
        k.slabs_end(part, [part.at(f + 1)])
        k.slabs_end(done, [done.at(f + 1)])

    with nc.Block() as block:
        @block.sync
        def _(sp):
            k.stream(sp)

        @block.gpsimd
        def _(pool):
            k.low(pool)

        @block.tensor
        def _(pe):
            for f in range(FT):
                if f >= 4:
                    pe.wait_ge(read.handle, read.at(f - 3))
                for j, finished in enumerate((part, done)):
                    hi, lo = k.slab(pe, first + 2 * f + j, P)
                    for c in range(KT):
                        ins = k.product(k.ps[:, (2 * f + j) % 8, :], (hi[:, c, :], lo[:, c, :]),
                                        (k.x_hi[:, c, :], k.x_lo[:, c, :]), c == 0, c == KT - 1)
                    ins.then_inc(finished.handle, 1)

        @block.scalar
        def _(act):
            for f in range(FT):
                k.high(act, first + 2 * f + SPLIT)
                act.wait_ge(part.handle, part.at(f + 1))
                nc.scalar.activation(hidden[:, f, :], k.ps[:, (2 * f) % 8, :], ACT.Silu).then_inc(gate.handle, 1)
                k.high(act, first + 2 * f + 1 + SPLIT)
            k.all_high(act)

        @block.vector
        def _(dve):
            for f in range(FT):
                dve.wait_ge(gate.handle, gate.at(f + 1))
                dve.wait_ge(done.handle, done.at(f + 1))
                nc.vector.tensor_tensor(hidden[:, f, :], hidden[:, f, :], k.ps[:, (2 * f + 1) % 8, :],
                                        ALU.mult).then_inc(read.handle, 1)
    for g in (part, done, gate, read):
        g.advance(FT)
    rows_add(k, f"{name}_down{layer}", hidden, [P] * FT, 0.5)


def ple(k, layer):
    nc = k.nc
    pt = k.at(0, 2, SEQ)
    proj = k.at(1024, KT, SEQ)
    load(k, [(pt[:, :, :], k.dram["p"][layer])])
    rows(k, f"ple_p{layer}", pt, [P] * 2, lambda m, ps: nc.vector.tensor_copy(proj[:, m, :], ps))
    rms(k, k.h, f"ple_g{layer}", scratch=8192)

    def finish(m, gate):
        k.vlink(nc.vector.tensor_tensor(gate, gate, proj[:, m, :], ALU.mult))
        return nc.vector.tensor_tensor(k.h[:, m, :], k.h[:, m, :], gate, ALU.add)

    dense_gated(k, f"ple_g{layer}", [P] * KT, ACT.Sigmoid, finish, 8192)


class Unit:

    def __init__(self, q, key, bias, v, gate=None, first=True, last=True, dst=None):
        self.q, self.key, self.bias, self.v, self.gate = q, key, bias, v, gate
        self.first, self.last, self.dst = first, last, dst
        self.w = key.shape[-1]


def attention(k, units, scratch):
    nc, s = k.nc, k.s
    n = len(units)
    ex = k.at(scratch, 4, SEQ)
    pt = k.at(scratch + 2048, 2, SEQ)
    dg = k.at(scratch + 3072, 3, P)
    low = k.at(scratch + 3456, 4)
    tot = k.at(scratch + 3460, 4)
    inv = k.at(scratch + 3464, 4)
    scored, biased, expd = s["scores_done"], s["biased"], s["exp_done"]
    diag, turned, copied = s["diag_done"], s["turned"], s["turned_copied"]
    summed, stored = s["out_done"], s["out_copied"]
    group = np.cumsum([u.first for u in units]) - 1
    last_of = {int(group[i]): i for i in range(n)}

    with nc.Block() as block:
        @block.tensor
        def _(pe):
            def scores(i):
                u = units[i]
                if i >= 3:
                    pe.wait_ge(biased.handle, biased.at(i - 2))
                nc.tensor.matmul(k.ps[:, i % 3, 0:u.w], u.q, u.key, start=True, stop=True).then_inc(scored.handle, 1)

            def turn(i):
                u = units[i]
                pe.wait_ge(diag.handle, diag.at(i + 1))
                if i >= 2:
                    pe.wait_ge(copied.handle, copied.at(i - 1))
                for j, (rows, _) in enumerate(u.v):
                    ins = nc.tensor.matmul(k.ps[0:rows, 3 + i % 2, j * P:(j + 1) * P],
                                           ex[:, i % 4, j * P:j * P + rows], dg[:, i % 3, :], start=True, stop=True)
                ins.then_inc(turned.handle, 1)

            def values(i):
                u = units[i]
                g = int(group[i])
                pe.wait_ge(copied.handle, copied.at(i + 1))
                if u.first and g >= 2:
                    pe.wait_ge(stored.handle, stored.at(g - 1))
                for j, (rows, v) in enumerate(u.v):
                    ins = nc.tensor.matmul(k.ps[0:v.shape[-1], 5 + g % 2, 0:P], v, pt[0:rows, i % 2, j * P:(j + 1) * P],
                                           start=(u.first and j == 0), stop=(u.last and j == len(u.v) - 1))
                ins.then_inc(summed.handle, 1)

            for i in range(n + 3):
                if i < n:
                    scores(i)
                if 2 <= i < n + 2:
                    turn(i - 2)
                if i >= 3:
                    values(i - 3)

        @block.vector
        def _(dve):
            def bias(i):
                u = units[i]
                dve.wait_ge(scored.handle, scored.at(i + 1))
                if i >= 4:
                    dve.wait_ge(turned.handle, turned.at(i - 3))
                nc.vector.tensor_tensor_reduce(ex[:, i % 4, 0:u.w], k.ps[:, i % 3, 0:u.w], u.bias, 1.0, 3e38,
                                               ALU.add, ALU.min, low[:, i % 4:i % 4 + 1]).then_inc(biased.handle, 1)

            def diagonal(i):
                u = units[i]
                dve.wait_ge(expd.handle, expd.at(i + 1))
                k.vlink(nc.vector.reciprocal(inv[:, i % 4:i % 4 + 1], tot[:, i % 4:i % 4 + 1]))
                if i >= 3:
                    dve.wait_ge(turned.handle, turned.at(i - 2))
                if u.gate is None:
                    ins = nc.vector.tensor_scalar(dg[:, i % 3, :], k.c("ident"), inv[:, i % 4:i % 4 + 1], None, ALU.mult)
                else:
                    ins = nc.vector.tensor_scalar(dg[:, i % 3, :], k.c("ident"), inv[:, i % 4:i % 4 + 1], u.gate,
                                                  ALU.mult, ALU.mult)
                ins.then_inc(diag.handle, 1)

            def store(g):
                u = units[last_of[g]]
                dve.wait_ge(summed.handle, summed.at(last_of[g] + 1))
                e = u.v[0][1].shape[-1]
                nc.vector.tensor_copy(u.dst, k.ps[0:e, 5 + g % 2, 0:P]).then_inc(stored.handle, 1)

            for i in range(n + 5):
                if i < n:
                    bias(i)
                if 1 <= i < n + 1:
                    diagonal(i - 1)
                if i >= 5 and units[i - 5].last:
                    store(int(group[i - 5]))

        @block.scalar
        def _(act):
            def exponentials(i):
                u = units[i]
                act.wait_ge(biased.handle, biased.at(i + 1))
                nc.scalar.activation(ex[:, i % 4, 0:u.w], ex[:, i % 4, 0:u.w], ACT.Exp, bias=low[:, i % 4:i % 4 + 1],
                                     scale=-1.0, accum_out=tot[:, i % 4:i % 4 + 1]).then_inc(expd.handle, 1)

            def copy(i):
                u = units[i]
                rows, m = u.v[0][0], len(u.v)
                act.wait_ge(turned.handle, turned.at(i + 1))
                if i >= 2:
                    act.wait_ge(summed.handle, summed.at(i - 1))
                nc.scalar.copy(pt[0:rows, i % 2, 0:m * P], k.ps[0:rows, 3 + i % 2, 0:m * P]).then_inc(copied.handle, 1)

            for i in range(n + 2):
                if i < n:
                    exponentials(i)
                if i >= 2:
                    copy(i - 2)
    for g in (scored, biased, expd, diag, turned, copied, summed):
        g.advance(n)
    stored.advance(len(last_of))


def rotary_cos_sin(k, cos, sin, pos_i, pos_f, tmp):
    nc, s = k.nc, k.s
    two_pi = 2 * np.pi
    c1 = 6.28125
    c2 = float(np.float32(np.round((two_pi - c1) * 2 ** 20) / 2 ** 20))
    c3 = float(np.float32(two_pi - c1 - c2))
    magic = 1.5 * 2.0 ** 23
    edge = 3.1415925
    ready = s["dve_step"]
    ang, turns = tmp[:, 0, :], tmp[:, 1, :]
    load(k, [(pos_i, k.dram["pos"].partition_broadcast(P))])

    with nc.Block() as block:
        @block.vector
        def _(dve):
            k.vlink(nc.vector.tensor_copy(pos_f, pos_i))
            k.vlink(nc.vector.tensor_scalar(ang, pos_f, k.c("inv64"), None, ALU.mult))
            for dst, quarter in ((sin, 0.0), (cos, 0.25)):
                k.vlink(nc.vector.tensor_scalar(turns, ang, 1.0 / two_pi, quarter, ALU.mult, ALU.add))
                k.vlink(nc.vector.tensor_scalar(turns, turns, magic, None, ALU.add))
                k.vlink(nc.vector.tensor_scalar(turns, turns, -magic, None, ALU.add))
                k.vlink(nc.vector.scalar_tensor_tensor(dst, turns, -c1, ang, ALU.mult, ALU.add))
                k.vlink(nc.vector.scalar_tensor_tensor(dst, turns, -c2, dst, ALU.mult, ALU.add))
                k.vlink(nc.vector.scalar_tensor_tensor(dst, turns, -c3, dst, ALU.mult, ALU.add))
                if quarter:
                    k.vlink(nc.vector.tensor_scalar(dst, dst, float(np.pi / 2), None, ALU.add))
                nc.vector.tensor_scalar(dst, dst, -edge, edge, ALU.max, ALU.min).then_inc(ready.handle, 1)

        @block.scalar
        def _(act):
            for i, dst in enumerate((sin, cos)):
                act.wait_ge(ready.handle, ready.at(i + 1))
                nc.scalar.activation(dst, dst, ACT.Sin)
    ready.advance(2)


def norm_rope(k, jobs, rot, ones, dim, cos, sin, scratch):
    nc, s = k.nc, k.s
    n = len(jobs)
    sq = k.at(scratch, 2, SEQ)
    root = k.at(scratch + 1024, SEQ)
    t1 = k.at(scratch + 1536, SEQ)
    t2 = k.at(scratch + 2048, SEQ)
    squared, sums, rooted, normed, rotated, used = (s["squares_done"], s["sum_done"], s["root_done"], s["dve_step"],
                                                    s["pe_step2"], s["dve_read"])
    normal = [i for i, (_, g, _) in enumerate(jobs) if g is not None]

    with nc.Block() as block:
        @block.scalar
        def _(act):
            for a, i in enumerate(normal):
                if a >= 2:
                    act.wait_ge(sums.handle, sums.at(a - 1))
                nc.scalar.activation(sq[:, a % 2, :], jobs[i][0], ACT.Square).then_inc(squared.handle, 1)
                act.wait_ge(sums.handle, sums.at(a + 1))
                if a >= 1:
                    act.wait_ge(normed.handle, normed.at(normal[a - 1] + 1))
                nc.scalar.activation(root, k.ps[:, a % 2, :], ACT.Sqrt, bias=k.c("eps"),
                                     scale=1.0 / dim).then_inc(rooted.handle, 1)

        @block.tensor
        def _(pe):
            a = 0
            for i, (x, g, _) in enumerate(jobs):
                if g is not None:
                    pe.wait_ge(squared.handle, squared.at(a + 1))
                    nc.tensor.matmul(k.ps[:, a % 2, :], k.c(ones), sq[:, a % 2, :], start=True,
                                     stop=True).then_inc(sums.handle, 1)
                    a += 1
                pe.wait_ge(normed.handle, normed.at(i + 1))
                if i >= 2:
                    pe.wait_ge(used.handle, used.at(i - 1))
                nc.tensor.matmul(k.ps[:, 2 + i % 2, :], k.c(rot), x, start=True, stop=True).then_inc(rotated.handle, 1)

        @block.vector
        def _(dve):
            a = 0
            for i, (x, g, scale) in enumerate(jobs):
                if g is not None:
                    dve.wait_ge(rooted.handle, rooted.at(a + 1))
                    k.vlink(nc.vector.reciprocal(t1, root))
                    nc.vector.scalar_tensor_tensor(x, x, k.v(g), t1, ALU.mult, ALU.mult).then_inc(normed.handle, 1)
                    a += 1
                else:
                    k.vlink(nc.vector.memset(t1[:, 0:1], 0.0))
                    nc.vector.memset(t1[:, 0:1], 0.0).then_inc(normed.handle, 1)
                dve.wait_ge(rotated.handle, rotated.at(i + 1))
                nc.vector.scalar_tensor_tensor(t1, x, scale, cos, ALU.mult, ALU.mult)
                nc.vector.scalar_tensor_tensor(t2, k.ps[:, 2 + i % 2, :], scale, sin, ALU.mult,
                                               ALU.mult).then_inc(used.handle, 1)
                dve.wait_ge(used.handle, used.at(i + 1))
                k.vlink(nc.vector.tensor_tensor(x, t1, t2, ALU.add))
    for g, v in ((squared, len(normal)), (sums, len(normal)), (rooted, len(normal)), (normed, n), (rotated, n), (used, n)):
        g.advance(v)


def select_keys(k, iq, ik, iw, negmask, scratch):
    nc, s = k.nc, k.s
    dots = k.at(scratch, 2, SEQ)
    work = k.at(scratch + 1024, SEQ)
    top = k.at(scratch + 1536, 8)
    done, cut, used = s["product_done"], s["act_step"], s["dve_read"]
    gone = -3e38

    with nc.Block() as block:
        @block.tensor
        def _(pe):
            for i in range(1, TT):
                for h in range(4):
                    u = (i - 1) * 4 + h
                    lo = 64 * (h % 2)
                    if u >= 2:
                        pe.wait_ge(cut.handle, cut.at(u - 1))
                    nc.tensor.matmul(k.ps[:, u % 2, 0:P * (i + 1)], iq[lo:lo + 64, h // 2, i * P:(i + 1) * P],
                                     ik[lo:lo + 64, 0:P * (i + 1)], start=True, stop=True).then_inc(done.handle, 1)

        @block.scalar
        def _(act):
            for i in range(1, TT):
                for h in range(4):
                    u = (i - 1) * 4 + h
                    act.wait_ge(done.handle, done.at(u + 1))
                    if u >= 2:
                        act.wait_ge(used.handle, used.at(u - 1))
                    nc.scalar.activation(dots[:, u % 2, 0:P * (i + 1)], k.ps[:, u % 2, 0:P * (i + 1)],
                                         ACT.Relu).then_inc(cut.handle, 1)

        @block.vector
        def _(dve):
            k.vlink(nc.vector.tensor_copy(negmask[:, 0, 0:P], k.c("chunkmask")[:, SEQ - P:SEQ]))
            for i in range(1, TT):
                w = P * (i + 1)
                for h in range(4):
                    u = (i - 1) * 4 + h
                    dve.wait_ge(cut.handle, cut.at(u + 1))
                    wt = iw[:, i, h:h + 1]
                    if h == 0:
                        ins = nc.vector.tensor_scalar(work[:, 0:w], dots[:, u % 2, 0:w], wt, None, ALU.mult)
                    else:
                        ins = nc.vector.scalar_tensor_tensor(work[:, 0:w], dots[:, u % 2, 0:w], wt, work[:, 0:w],
                                                             ALU.mult, ALU.add)
                    ins.then_inc(used.handle, 1)
                    dve.wait_ge(used.handle, used.at(u + 1))
                k.vlink(nc.vector.tensor_tensor(work[:, 0:w], work[:, 0:w], k.c("chunkmask")[:, SEQ - w:SEQ],
                                                ALU.subtract))
                for _ in range(TOPK // 8):
                    k.vlink(nc.vector.max(top, work[:, 0:w]))
                    k.vlink(nc.vector.match_replace(work[:, 0:w], top, work[:, 0:w], gone))
                k.vlink(nc.vector.tensor_scalar(negmask[:, i, 0:w], work[:, 0:w], gone, BIG, ALU.not_equal, ALU.mult))
    for g in (done, cut, used):
        g.advance(4 * (TT - 1))


def even_mixer(k):
    nc, s = k.nc, k.s
    qk = k.at(0, 16, SEQ)
    vt = k.at(8192, TT, 132)
    bv = k.at(8720, TT, 512)
    o = k.at(10768, KT, SEQ)
    olat = k.at(14864, KT, SEQ)
    cos, sin = k.at(18960, SEQ), k.at(19472, SEQ)
    negmask = k.at(19984, TT, SEQ)
    uv = k.at(22032, 512)
    small = k.at(22544, 16)
    scr = 22560
    aq, ak, iq, ik = qk[:, 0:4], qk[:, 4], qk[:, 5:7], qk[:, 7]
    bq, bk = qk[:, 8:12], qk[:, 12:16]

    load(k, [(uv, k.dram["w_uv"])])
    rms(k, k.h, "mix_g0", scratch=scr)
    dense_f(k, "ev_f", [P] * 16, lambda m, ps: nc.scalar.copy(qk[:, m, :], ps))

    def token_major(j, t, ps):
        dst = vt[:, t, :] if j == 0 else bv[:, t, (j - 1) * 256:j * 256]
        return nc.scalar.copy(dst, ps)

    dense_t(k, "ev_t", [132, 256, 256], token_major)
    rotary_cos_sin(k, cos, sin, k.at(scr, SEQ).bitcast(I32), k.at(scr + 512, SEQ), k.at(scr + 1024, 2, SEQ))
    scale = -(64 ** -0.5)
    jobs = ([(aq[:, m, :], "aq_g", scale) for m in range(4)] + [(ak, "ak_g", 1.0)]
            + [(iq[:, m, :], None, 1.0) for m in range(2)] + [(ik, None, 1.0)]
            + [(bq[:, m, :], "bq_g", scale) for m in range(4)] + [(bk[:, m, :], "bk_g", 1.0) for m in range(4)])
    norm_rope(k, jobs, "rot64", "ones64", 64, cos, sin, scr)
    select_keys(k, iq, ik, vt[:, :, 128:132], negmask, scr)

    lams = k.vec[:, VEC_AT["lams"][0]:VEC_AT["lams"][0] + 4]
    with nc.Block() as block:
        @block.vector
        def _(dve):
            nc.vector.tensor_tensor(small[:, 0:2], lams[:, 0:4:2], lams[:, 1:4:2], ALU.mult).then_inc(s["dve_step"].handle, 1)
            dve.wait_ge(s["act_step"].handle, s["act_step"].at(1))
            k.vlink(nc.vector.tensor_tensor(small[:, 4:5], small[:, 3:4], small[:, 2:3], ALU.subtract))
            k.vlink(nc.vector.tensor_scalar(small[:, 5:6], small[:, 4:5], -0.2, None, ALU.add))

        @block.tensor
        def _(pe):
            pe.wait_ge(s["dve_step"].handle, s["dve_step"].at(1))
            nc.tensor.matmul(k.ps[:, 0, 0:2], k.c("ones"), small[:, 0:2], start=True,
                             stop=True).then_inc(s["pe_step"].handle, 1)

        @block.scalar
        def _(act):
            act.wait_ge(s["pe_step"].handle, s["pe_step"].at(1))
            nc.scalar.activation(small[:, 2:4], k.ps[:, 0, 0:2], ACT.Exp).then_inc(s["act_step"].handle, 1)
    for g in ("dve_step", "act_step", "pe_step"):
        s[g].advance(1)

    units = []
    for i in range(TT):
        q = slice(i * P, (i + 1) * P)
        w = P * (i + 1)
        for h in range(8):
            lo = 64 * (h % 2)
            units.append(Unit(aq[lo:lo + 64, h // 2, q], ak[lo:lo + 64, 0:w], negmask[:, i, 0:w],
                              [(P, vt[:, j, 0:P]) for j in range(i + 1)], dst=olat[:, h, q]))
        for h in range(4):
            for c in range(2):
                units.append(Unit(bq[64 * c:64 * c + 64, h, q], bk[64 * c:64 * c + 64, h, 0:w],
                                  k.c("chunkmask")[:, SEQ - w:SEQ],
                                  [(P, bv[:, j, h * P:(h + 1) * P]) for j in range(i + 1)],
                                  gate=small[:, 5:6] if c else None, first=(c == 0), last=(c == 1),
                                  dst=o[:, 4 + h, q]))
    attention(k, units, scr)

    sq = k.at(scr, 2, SEQ)
    root = k.at(scr + 1024, 2, SEQ)
    inv, fin = k.at(scr + 2048, SEQ), k.at(scr + 2560, SEQ)
    lifted, copied, squared, sums, rooted, used = (s["product_done"], s["evacuated"], s["squares_done"], s["sum_done"],
                                                   s["root_done"], s["dve_read"])
    with nc.Block() as block:
        @block.tensor
        def _(pe):
            for h in range(8):
                if h >= 4:
                    pe.wait_ge(copied.handle, copied.at(h - 3))
                nc.tensor.matmul(k.ps[0:64, h % 4, :], uv[:, h * 64:(h + 1) * 64], olat[:, h, :], start=True,
                                 stop=True).then_inc(lifted.handle, 1)
            for h in range(4):
                pe.wait_ge(squared.handle, squared.at(h + 1))
                nc.tensor.matmul(k.ps[:, 4 + h, :], k.c("ones"), sq[:, h % 2, :], start=True,
                                 stop=True).then_inc(sums.handle, 1)

        @block.scalar
        def _(act):
            for h in range(8):
                act.wait_ge(lifted.handle, lifted.at(h + 1))
                lo = 64 * (h % 2)
                nc.scalar.copy(o[lo:lo + 64, h // 2, :], k.ps[0:64, h % 4, :]).then_inc(copied.handle, 1)
            for h in range(4):
                if h >= 2:
                    act.wait_ge(sums.handle, sums.at(h - 1))
                act.wait_ge(s["dve_step"].handle, s["dve_step"].at(h + 1))
                nc.scalar.activation(sq[:, h % 2, :], o[:, 4 + h, :], ACT.Square, scale=SHRINK).then_inc(squared.handle, 1)
            for h in range(4):
                act.wait_ge(sums.handle, sums.at(h + 1))
                if h >= 2:
                    act.wait_ge(used.handle, used.at(h - 1))
                nc.scalar.activation(root[:, h % 2, :], k.ps[:, 4 + h, :], ACT.Sqrt, bias=k.c("eps_small"),
                                     scale=1.0 / P).then_inc(rooted.handle, 1)

        @block.vector
        def _(dve):
            for h in range(4):
                nc.vector.tensor_scalar(o[:, 4 + h, :], o[:, 4 + h, :], -BIG, BIG, ALU.max,
                                        ALU.min).then_inc(s["dve_step"].handle, 1)
            k.vlink(nc.vector.tensor_scalar(small[:, 6:7], k.v("subln_g"), 1.0 - 0.2, None, ALU.mult))
            for h in range(4):
                dve.wait_ge(rooted.handle, rooted.at(h + 1))
                nc.vector.reciprocal(inv, root[:, h % 2, :])
                nc.vector.tensor_scalar(fin, k.ps[:, 4 + h, :], OVERFLOW, SHRINK, ALU.is_lt,
                                        ALU.mult).then_inc(used.handle, 1)
                dve.wait_ge(used.handle, used.at(h + 1))
                k.vlink(nc.vector.tensor_tensor(inv, inv, fin, ALU.mult))
                k.vlink(nc.vector.scalar_tensor_tensor(o[:, 4 + h, :], o[:, 4 + h, :], small[:, 6:7], inv,
                                                       ALU.mult, ALU.mult))
    for g, v in ((lifted, 8), (copied, 8), (squared, 4), (sums, 4), (rooted, 4), (used, 4),
                 (s["dve_step"], 4)):
        g.advance(v)
    rows_add(k, "ev_out", o, [P] * KT, 1.0)


def layer_norm_f(k, groups, rows, scratch):
    nc, s = k.nc, k.s
    sq = k.at(scratch, 2, SEQ)
    root = k.at(scratch + 1024, 2, SEQ)
    inv = k.at(scratch + 2048, SEQ)
    summed, centred, squared, sums, rooted, used = (s["product_done"], s["dve_step"], s["squares_done"], s["sum_done"],
                                                    s["root_done"], s["dve_read"])
    per = len(groups[0])
    dim = per * rows
    n = len(groups)

    with nc.Block() as block:
        @block.tensor
        def _(pe):
            for g, tl in enumerate(groups):
                if g >= 2:
                    pe.wait_ge(centred.handle, centred.at((g - 1) * per))
                for j, x in enumerate(tl):
                    ins = nc.tensor.matmul(k.ps[0:rows, g % 2, :], k.c("ones")[0:rows, 0:rows], x, start=(j == 0),
                                           stop=(j == per - 1))
                ins.then_inc(summed.handle, 1)
                if g >= 2:
                    pe.wait_ge(rooted.handle, rooted.at(g - 1))
                for j in range(per):
                    pe.wait_ge(squared.handle, squared.at(g * per + j + 1))
                    nc.tensor.matmul(k.ps[0:rows, 2 + g % 2, :], k.c("ones")[0:rows, 0:rows],
                                     sq[0:rows, (g * per + j) % 2, :], start=(j == 0),
                                     stop=(j == per - 1)).then_inc(sums.handle, 1)

        @block.scalar
        def _(act):
            for g, tl in enumerate(groups):
                for j, x in enumerate(tl):
                    u = g * per + j
                    act.wait_ge(centred.handle, centred.at(u + 1))
                    if u >= 2:
                        act.wait_ge(sums.handle, sums.at(u - 1))
                    nc.scalar.activation(sq[0:rows, u % 2, :], x, ACT.Square).then_inc(squared.handle, 1)
                act.wait_ge(sums.handle, sums.at((g + 1) * per))
                if g >= 2:
                    act.wait_ge(used.handle, used.at(g - 1))
                nc.scalar.activation(root[0:rows, g % 2, :], k.ps[0:rows, 2 + g % 2, :], ACT.Sqrt,
                                     bias=k.c("eps")[0:rows, :], scale=1.0 / dim).then_inc(rooted.handle, 1)

        @block.vector
        def _(dve):
            for g, tl in enumerate(groups):
                dve.wait_ge(summed.handle, summed.at(g + 1))
                for x in tl:
                    nc.vector.scalar_tensor_tensor(x, k.ps[0:rows, g % 2, :], -1.0 / dim, x, ALU.mult,
                                                   ALU.add).then_inc(centred.handle, 1)
                dve.wait_ge(rooted.handle, rooted.at(g + 1))
                nc.vector.reciprocal(inv[0:rows, :], root[0:rows, g % 2, :]).then_inc(used.handle, 1)
                dve.wait_ge(used.handle, used.at(g + 1))
                for x in tl:
                    ins = nc.vector.tensor_tensor(x, x, inv[0:rows, :], ALU.mult)
                k.vlink(ins)
    for g, v in ((summed, n), (centred, n * per), (squared, n * per), (sums, n * per), (rooted, n), (used, n)):
        g.advance(v)


def odd_mixer(k):
    nc, s = k.nc, k.s
    o = k.at(0, KT, SEQ)
    a = k.at(4096, 4, SEQ)
    g = k.at(6144, 4, 30 + SEQ)
    vt = k.at(8312, TT, 512)
    ws = k.at(10360, 8, P)
    bs = k.at(11384, 4, P)
    lng, lnb = k.at(11896, 512), k.at(12408, 512)
    acc = k.at(12920, 4, SEQ)
    stats, aggr, sm = k.at(14968, TT, 6), k.at(14992, TT, 2), k.at(15000, 16)
    scr = 15016
    load(k, [(ws, k.dram["w_s"]), (bs, k.dram["b_s"]), (lng, k.dram["cln"][0:1].partition_broadcast(P)),
             (lnb, k.dram["cln"][1:2].partition_broadcast(P))])
    rms(k, k.h, "mix_g1", scratch=scr)

    def evac(m, ps):
        if m < 4:
            return nc.scalar.activation(o[:, m, :], ps, ACT.Gelu_apprx_tanh)
        if m < 8:
            return nc.scalar.copy(a[:, m - 4, :], ps)
        return nc.scalar.activation(g[:, m - 8, 30:], ps, ACT.Sigmoid)

    dense_f(k, "od_f", [P] * 12, evac)
    dense_t(k, "od_t", [256, 256],
            lambda j, t, ps: nc.scalar.activation(vt[:, t, j * 256:(j + 1) * 256], ps, ACT.Gelu_apprx_tanh))

    rooted, normed, mixed = s["root_done"], s["dve_step"], s["product_done"]
    with nc.Block() as block:
        @block.gpsimd
        def _(pool):
            nc.gpsimd.memset(g[:, :, 0:30], 0.0)
            k.plink(nc.gpsimd.tensor_tensor(g[:, :, 30:], g[:, :, 30:], a[:, :, :], ALU.mult))
            nc.gpsimd.memset(ws[64:128, :, 0:64], 0.0).then_inc(s["pool_step"].handle, 1)

        @block.scalar
        def _(act):
            act.wait_ge(s["tmp_ready"].handle, s["tmp_ready"].at(1))
            nc.scalar.activation(sm[:, 0:4], aggr[:, :, 1], ACT.Sqrt, bias=k.c("eps")).then_inc(rooted.handle, 1)

        @block.vector
        def _(dve):
            for t in range(TT):
                k.vlink(nc.vector.bn_stats(stats[:, t, :], vt[:, t, :]))
            for t in range(TT):
                ins = nc.vector.bn_aggr(aggr[:, t, :], stats[:, t, :])
            ins.then_inc(s["tmp_ready"].handle, 1)
            dve.wait_ge(rooted.handle, rooted.at(1))
            k.vlink(nc.vector.reciprocal(sm[:, 4:8], sm[:, 0:4]))
            for t in range(TT):
                k.vlink(nc.vector.tensor_scalar(vt[:, t, :], vt[:, t, :], aggr[:, t, 0:1], sm[:, 4 + t:5 + t],
                                                ALU.subtract, ALU.mult))
                k.vlink(nc.vector.tensor_tensor(vt[:, t, :], vt[:, t, :], lng, ALU.mult))
                nc.vector.tensor_tensor(vt[:, t, :], vt[:, t, :], lnb, ALU.add).then_inc(normed.handle, 1)
            for t in range(TT):
                for gp in range(4):
                    u = t * 4 + gp
                    dve.wait_ge(mixed.handle, mixed.at(u + 1))
                    for half in range(2):
                        lo = 64 * half
                        dst = o[lo:lo + 64, gp, t * P:(t + 1) * P]
                        tmp = acc[lo:lo + 64, half, 0:P]
                        k.vlink(nc.vector.tensor_tensor(tmp, k.ps[lo:lo + 64, u % 8, half * P:(half + 1) * P],
                                                        bs[lo:lo + 64, gp, :], ALU.add))
                        ins = nc.vector.tensor_tensor(dst, dst, tmp, ALU.mult)
                        if half:
                            ins.then_inc(s["dve_read"].handle, 1)
                            dve.wait_ge(s["dve_read"].handle, s["dve_read"].at(u + 1))
                        else:
                            k.vlink(ins)

        @block.tensor
        def _(pe):
            pe.wait_ge(s["pool_step"].handle, s["pool_step"].at(1))
            for t in range(TT):
                pe.wait_ge(normed.handle, normed.at(t + 1))
                for gp in range(4):
                    u = t * 4 + gp
                    if u >= 8:
                        pe.wait_ge(s["dve_read"].handle, s["dve_read"].at(u - 7))
                    nc.tensor.matmul(k.ps[:, u % 8, 0:256], vt[:, t, gp * P:(gp + 1) * P],
                                     ws[:, 2 * gp:2 * gp + 2, :], start=True, stop=True).then_inc(mixed.handle, 1)
    for n, v in (("pool_step", 1), ("tmp_ready", 1), ("root_done", 1), ("dve_step", 4), ("product_done", 16),
                 ("dve_read", 16)):
        s[n].advance(v)

    at = VEC_AT["conv_w"][0]
    with nc.Block() as block:
        @block.vector
        def _(dve):
            for tap in range(31):
                for c in range(4):
                    wt = k.vec[:, at + c * 31 + tap:at + c * 31 + tap + 1]
                    src = g[:, c, tap:tap + SEQ]
                    dst = o[:, 4 + c, :]
                    if tap == 0:
                        ins = nc.vector.tensor_scalar(dst, src, wt, k.v("conv_b", c), ALU.mult, ALU.add)
                    else:
                        ins = nc.vector.scalar_tensor_tensor(dst, src, wt, dst, ALU.mult, ALU.add)
                k.vlink(ins)
    layer_norm_f(k, [[o[:, 4 + c, :] for c in range(4)]], P, scr)
    with nc.Block() as block:
        @block.scalar
        def _(act):
            for c in range(4):
                nc.scalar.activation(o[:, 4 + c, :], o[:, 4 + c, :], ACT.Silu, bias=k.v("dln_b", c),
                                     scale=k.v("dln_g", c))
    rows_add(k, "od_out", o, [P] * KT, 1.0)


def mem_attention(k, layer, out, base):
    nc = k.nc
    mem = k.at(base + 4096, KT, NMEM)
    load(k, [(mem, k.dram["mem"])])
    rms(k, mem, "memnorm_g", n=NMEM, scratch=base + 6144)
    mk = k.at(base, 4, NMEM)
    mv = k.at(base + 1024, 2, 512)
    xq = k.at(base + 2048, 4, SEQ)
    zero = k.c("chunkmask")[:, 0:NMEM]
    dense_f(k, f"mk{layer}", [P] * 4, lambda m, ps: nc.scalar.copy(mk[:, m, :], ps), n=NMEM)
    dense_t(k, f"mv{layer}", [256, 256],
            lambda j, t, ps: nc.scalar.copy(mv[:, t, j * 256:(j + 1) * 256], ps), tts=2)
    rms(k, k.h, f"norm2_g{layer}", scratch=base + 4096)
    dense_f(k, f"xq{layer}", [P] * 4, lambda m, ps: nc.scalar.mul(xq[:, m, :], ps, -(P ** -0.5)))
    attention(k, [Unit(xq[:, h, i * P:(i + 1) * P], mk[:, h, :], zero,
                       [(P, mv[:, j, h * P:(h + 1) * P]) for j in range(2)], dst=out[:, h, i * P:(i + 1) * P])
                  for i in range(TT) for h in range(4)], base + 4096)


def pool_mixer(k, za, out, scr):
    nc, s = k.nc, k.s
    recip = k.at(scr, 4, SEQ)
    wg = k.at(scr + 2048, 8, 192)
    buf = k.at(scr + 3584, 2, 2 * SEQ)
    load(k, [(recip, k.dram["pool_recip"]), (wg[0:96], k.dram["pool_w"])])
    ready, done = s["dve_step"], s["product_done"]

    with nc.Block() as block:
        @block.vector
        def _(dve):
            for g, w in enumerate(POOL_W):
                src = za[0:96, 2 * g:2 * g + 2, :]
                step, b = 1, 0
                while step < w:
                    dst = buf[0:96, b, :].rearrange("p (a t) -> p a t", a=2)
                    nc.vector.tensor_copy(dst[:, :, 0:step], src[:, :, 0:step])
                    k.vlink(nc.vector.tensor_tensor(dst[:, :, step:], src[:, :, step:], src[:, :, 0:SEQ - step], ALU.add))
                    src, step, b = dst, 2 * step, 1 - b
                for a in range(2):
                    k.vlink(nc.vector.tensor_tensor(src[:, a, :], src[:, a, :], recip[0:96, g, :], ALU.mult))
                z = za[0:96, 2 * g:2 * g + 2, :]
                ins = nc.vector.tensor_tensor(z, src, z, ALU.subtract)
                ins.then_inc(ready.handle, 1)
                dve.wait_ge(ready.handle, ready.at(g + 1))

        @block.tensor
        def _(pe):
            for g in range(4):
                pe.wait_ge(ready.handle, ready.at(g + 1))
                for m in range(2):
                    for c in range(2):
                        ins = nc.tensor.matmul(k.ps[0:96, 2 * g + m, :], wg[0:96, 2 * g + c, m * 96:(m + 1) * 96],
                                               za[0:96, 2 * g + c, :], start=(c == 0), stop=(c == 1))
                    ins.then_inc(done.handle, 1)

        @block.scalar
        def _(act):
            for m in range(8):
                act.wait_ge(done.handle, done.at(m + 1))
                nc.scalar.activation(out[0:96, m, :], k.ps[0:96, m, :], ACT.Copy, scale=k.v("pool_scale", m, 96))
    ready.advance(4)
    done.advance(8)


def retention(k, q, key, v, out, decay, scr):
    nc, s = k.nc, k.s
    att = k.at(scr, 2, SEQ)
    scored, decayed, summed, copied = s["scores_done"], s["biased"], s["out_done"], s["out_copied"]

    with nc.Block() as block:
        @block.tensor
        def _(pe):
            def scores(u):
                h, j = u // TT, u % TT
                if u >= 2:
                    pe.wait_ge(decayed.handle, decayed.at(u - 1))
                nc.tensor.matmul(k.ps[:, u % 2, 0:SEQ - j * P], key[:, h, j * P:(j + 1) * P], q[:, h, j * P:],
                                 start=True, stop=True).then_inc(scored.handle, 1)

            def values(u):
                h, j = u // TT, u % TT
                pe.wait_ge(decayed.handle, decayed.at(u + 1))
                if j == 0 and h >= 2:
                    pe.wait_ge(copied.handle, copied.at(2 * (h - 1)))
                for m in range(2):
                    c = h * RET_DV + m * 96
                    ins = nc.tensor.matmul(k.ps[0:96, 2 + 2 * (h % 2) + m, j * P:SEQ], v[:, j, c:c + 96],
                                           att[:, u % 2, 0:SEQ - j * P], start=(j == 0), stop=(j == TT - 1))
                ins.then_inc(summed.handle, 1)

            for u in range(RET_H * TT + 1):
                if u < RET_H * TT:
                    scores(u)
                if u >= 1:
                    values(u - 1)

        @block.vector
        def _(dve):
            for u in range(RET_H * TT):
                h, j = u // TT, u % TT
                dve.wait_ge(scored.handle, scored.at(u + 1))
                if u >= 2:
                    dve.wait_ge(summed.handle, summed.at(u - 1))
                nc.vector.tensor_tensor(att[:, u % 2, 0:SEQ - j * P], k.ps[:, u % 2, 0:SEQ - j * P],
                                        decay[:, h, 0:SEQ - j * P], ALU.mult).then_inc(decayed.handle, 1)

        @block.scalar
        def _(act):
            for h in range(RET_H):
                act.wait_ge(summed.handle, summed.at((h + 1) * TT))
                for m in range(2):
                    nc.scalar.copy(out[0:96, 2 * h + m, :], k.ps[0:96, 2 + 2 * (h % 2) + m, :]).then_inc(copied.handle, 1)
    for g in (scored, decayed, summed):
        g.advance(RET_H * TT)
    copied.advance(2 * RET_H)
    layer_norm_f(k, [[out[0:96, 2 * h + m, :] for m in range(2)] for h in range(RET_H)], 96, scr)


def gate_and_project(k, layer, y, heights, scratch):
    nc = k.nc
    dense_gated(k, f"gate{layer}", heights, ACT.Silu,
                lambda m, gate: nc.vector.tensor_tensor(y[0:heights[m], m, :], y[0:heights[m], m, :], gate, ALU.mult),
                scratch)
    rows_add(k, f"wo{layer}", y, heights, 1.0)


def second_even(k):
    nc = k.nc
    y = k.at(0, 20, SEQ)
    base = 10240
    mem_attention(k, 0, y[:, 16:20], base)
    za = k.at(base, 8, SEQ)
    dense_f(k, "za", [96] * 8, lambda m, ps: nc.scalar.copy(za[0:96, m, :], ps))
    pool_mixer(k, za, y[:, 0:8], base + 4096)
    qk = k.at(base, 8, SEQ)
    v = k.at(base + 4096, TT, 768)
    tab = k.at(base + 7168, 2, SEQ)
    decay = k.at(base + 8192, 4, SEQ)
    scr = base + 10240
    load(k, [(tab, k.dram["rotary"]), (decay, k.dram["decay"])])
    dense_f(k, "rqk", [P] * 8, lambda m, ps: nc.scalar.copy(qk[:, m, :], ps))
    dense_t(k, "rv", [256] * 3, lambda j, t, ps: nc.scalar.copy(v[:, t, j * 256:(j + 1) * 256], ps))
    norm_rope(k, [(qk[:, m, :], None, P ** -0.5 if m < 4 else 1.0) for m in range(8)], "rot128", "ones", P,
              tab[:, 0, :], tab[:, 1, :], scr)
    retention(k, qk[:, 0:4], qk[:, 4:8], v, y[:, 8:16], decay, scr)
    gate_and_project(k, 0, y, [96] * 16 + [P] * 4, scr)


def compress(k, kc, vc, kcmp, vcmp, scr):
    nc, s = k.nc, k.s
    m2 = NSA_G * NCMP
    x = k.at(scr, 2, 4 * m2)
    hid = k.at(scr + 512, 4, 64)
    w2 = k.at(scr + 768, 4, P)
    load(k, [(w2, k.dram["cmp_w2"])])
    ready, done, part, act_done = s["dve_step"], s["product_done"], s["pe_step"], s["act_step"]
    his, los = s["hi_done"], s["lo_done"]
    n = 16
    k.slabs_end(part, [part.at(j + 1) for j in range(n)])

    with nc.Block() as block:
        @block.sync
        def _(sp):
            k.stream(sp)

        @block.gpsimd
        def _(pool):
            k.low(pool)

        @block.vector
        def _(dve):
            def low(u):
                dve.wait_ge(his.handle, his.at(u + 1))
                nc.vector.tensor_tensor(k.r_lo[:, u % 2, 0:4 * m2], x[:, u % 2, :],
                                        k.r_hi[:, u % 2, 0:4 * m2].bitcast(F32), ALU.subtract).then_inc(los.handle, 1)
                dve.wait_ge(los.handle, los.at(u + 1))

            for u in range(n):
                src = kc if u < 8 else vc
                for li in range(4):
                    l = 4 * (u % 8) + li
                    dst = x[:, u % 2, li * m2:(li + 1) * m2].rearrange("p (g j) -> p g j", g=2)
                    ins = nc.vector.tensor_scalar(dst, src[:, :, l:l + 16 * (NCMP - 1) + 1:16],
                                                  k.v("cmp_pe", 32 * (u // 8) + l), None, ALU.add)
                ins.then_inc(ready.handle, 1)
                dve.wait_ge(ready.handle, ready.at(u + 1))
                low(u)

        @block.tensor
        def _(pe):
            for u in range(n):
                kind = u // 8
                hi, lo = k.slab(pe, STREAM_AT["cmp0"][0] + u, P)
                pe.wait_ge(los.handle, los.at(u + 1))
                for li in range(4):
                    cols = slice(li * m2, (li + 1) * m2)
                    for m in range(2):
                        ins = k.product(k.ps[:, 2 * kind + m, 0:m2], (hi[:, 2 * li + m, :], lo[:, 2 * li + m, :]),
                                        (k.r_hi[:, u % 2, cols], k.r_lo[:, u % 2, cols]),
                                        u % 8 == 0 and li == 0, u % 8 == 7 and li == 3)
                ins.then_inc(part.handle, 1)
            pe.wait_ge(act_done.handle, act_done.at(4))
            for c in range(2):
                ins = nc.tensor.matmul(k.ps[:, 4, 0:m2], w2[:, c, :], hid[:, c, 0:m2], start=(c == 0), stop=(c == 1))
            ins.then_inc(done.handle, 1)
            for g in range(2):
                for c in range(2):
                    ins = nc.tensor.matmul(k.ps[0:NCMP, 5 + g, 0:P], hid[:, 2 + c, g * NCMP:(g + 1) * NCMP], w2[:, 2 + c, :],
                                           start=(c == 0), stop=(c == 1))
                ins.then_inc(done.handle, 1)

        @block.scalar
        def _(act):
            for u in range(n):
                act.wait_ge(ready.handle, ready.at(u + 1))
                if u >= 2:
                    k.high(act, STREAM_AT["cmp0"][0] + u - 2 + SPLIT)
                    act.wait_ge(part.handle, part.at(u - 1))
                nc.scalar.copy(k.r_hi[:, u % 2, 0:4 * m2], x[:, u % 2, :]).then_inc(his.handle, 1)
            k.all_high(act)
            for kind in range(2):
                act.wait_ge(part.handle, part.at(8 * (kind + 1)))
                for m in range(2):
                    nc.scalar.activation(hid[:, 2 * kind + m, 0:m2], k.ps[:, 2 * kind + m, 0:m2], ACT.Silu,
                                         bias=k.v("cmp_b1", 2 * kind + m)).then_inc(act_done.handle, 1)
            act.wait_ge(done.handle, done.at(1))
            nc.scalar.copy(kcmp[:, 0:m2], k.ps[:, 4, 0:m2])
            for g in range(2):
                act.wait_ge(done.handle, done.at(2 + g))
                nc.scalar.copy(vcmp[0:NCMP, g, :], k.ps[0:NCMP, 5 + g, 0:P])
    for g, v in ((ready, n), (part, n), (act_done, 4), (done, 3), (his, n), (los, n)):
        g.advance(v)


def distance_bias(k, bias, scr):
    nc, s = k.nc, k.s
    tab = k.at(scr, NSA_H)
    hot = k.at(scr + 16, FREV)
    frev = k.at(scr + 1040, FREV)
    half = BIASW // 2
    load(k, [(tab[0:32, :], k.dram["rel"]), (hot[0:33, :], k.dram["buckets"])])

    with nc.Block() as block:
        @block.vector
        def _(dve):
            nc.vector.tensor_scalar(tab[0:32, :], tab[0:32, :], -1.0, None, ALU.mult)
            nc.vector.memset(tab[32:33, :], BIG).then_inc(s["dve_step"].handle, 1)

        @block.tensor
        def _(pe):
            pe.wait_ge(s["dve_step"].handle, s["dve_step"].at(1))
            for j in range(2):
                nc.tensor.matmul(k.ps[0:NSA_H, j, :], tab[0:33, :], hot[0:33, j * SEQ:(j + 1) * SEQ], start=True,
                                 stop=True).then_inc(s["pe_step"].handle, 1)
            pe.wait_ge(k.aux.handle, k.aux.at(16))
            for h in range(NSA_H):
                if h >= 3:
                    pe.wait_ge(s["act_step"].handle, s["act_step"].at(2 + 2 * (h - 2)))
                for j in range(2):
                    ins = nc.tensor.matmul(k.ps[:, 2 + 2 * (h % 3) + j, 0:half], k.c("flip"),
                                           bias[:, h, j * half:(j + 1) * half], start=True, stop=True)
                ins.then_inc(s["pe_step"].handle, 1)

        @block.scalar
        def _(act):
            for j in range(2):
                act.wait_ge(s["pe_step"].handle, s["pe_step"].at(j + 1))
                nc.scalar.copy(frev[0:NSA_H, j * SEQ:(j + 1) * SEQ], k.ps[0:NSA_H, j, :]).then_inc(s["act_step"].handle, 1)
            for h in range(NSA_H):
                act.wait_ge(s["pe_step"].handle, s["pe_step"].at(h + 3))
                for j in range(2):
                    nc.scalar.copy(bias[:, h, j * half:(j + 1) * half],
                                   k.ps[:, 2 + 2 * (h % 3) + j, 0:half]).then_inc(s["act_step"].handle, 1)

        @block.sync
        def _(sp):
            sp.wait_ge(s["act_step"].handle, s["act_step"].at(2))
            sp.dma_start(k.dram["frev"], frev[0:NSA_H, :]).then_inc(k.stored.handle, 16)
            sp.wait_ge(k.stored.handle, k.stored.at(16))
            rows = bass.AP(k.dram["frev"].tensor, 0, [[1, P], [FREV, NSA_H], [1, BIASW]])
            sp.dma_start(bias, rows).then_inc(k.aux.handle, 16)
            sp.wait_ge(k.aux.handle, k.aux.at(16))
    s["dve_step"].advance(1)
    s["pe_step"].advance(2 + NSA_H)
    s["act_step"].advance(2 + 2 * NSA_H)
    k.stored.advance(16)
    k.aux.advance(16)


def second_odd(k):
    nc, s = k.nc, k.s
    y = k.at(0, 16, SEQ)
    base = 8192
    mem_attention(k, 1, y[:, 12:16], base)
    kcmp = k.at(base, 64)
    vcmp = k.at(base + 64, 2, P)
    gl = k.at(base + 320, TT, 36)
    seen = k.at(base + 464, TT, NSA_H)
    kvc = k.at(base + 512, 4, SEQ)
    dense_f(k, "kvc", [P] * 4, lambda m, ps: nc.scalar.copy(kvc[:, m, :], ps))
    compress(k, kvc[:, 0:2], kvc[:, 2:4], kcmp, vcmp, base + 2560)

    keys = k.at(base + 512, 4, SEQ)
    vals = k.at(base + 2560, TT, 512)
    bias = k.at(base + 4608, NSA_H, BIASW)
    scr = base + 4608 + NSA_H * BIASW
    distance_bias(k, bias, scr)
    dense_f(k, "nsaq", [P] * 12, lambda m, ps: nc.scalar.mul(y[:, m, :], ps, -(P ** -0.5)))
    dense_f(k, "nsak", [P] * 4, lambda m, ps: nc.scalar.copy(keys[:, m, :], ps))

    def evac(j, t, ps):
        if j == 2:
            return nc.scalar.activation(gl[:, t, :], ps, ACT.Sigmoid)
        return nc.scalar.copy(vals[:, t, j * 256:(j + 1) * 256], ps)

    dense_t(k, "nsav", [256, 256, 36], evac)
    with nc.Block() as block:
        @block.vector
        def _(dve):
            nc.vector.tensor_scalar(gl[:, 0, 0:NSA_H], gl[:, 0, 0:NSA_H], k.c("seen"), None, ALU.mult)

    units = []
    for i in range(TT):
        q = slice(i * P, (i + 1) * P)
        w = P * (i + 1)
        for h in range(NSA_H):
            g = h // 6
            qh = y[:, h, q]
            c0 = 415 - P * i
            units.append(Unit(qh, kcmp[:, g * NCMP:(g + 1) * NCMP], bias[:, h, c0:c0 + 16 * (NCMP - 1) + 1:16],
                              [(NCMP, vcmp[0:NCMP, g, :])], gate=gl[:, i, h:h + 1], last=False))
            for b in range(2):
                units.append(Unit(qh, keys[:, 2 * b + g, 0:w], bias[:, h, SEQ - w:SEQ],
                                  [(P, vals[:, j, b * 256 + g * P:b * 256 + (g + 1) * P]) for j in range(i + 1)],
                                  gate=gl[:, i, NSA_H * (b + 1) + h:NSA_H * (b + 1) + h + 1], first=False,
                                  last=(b == 1), dst=qh))
    attention(k, units, scr)
    gate_and_project(k, 1, y, [P] * 16, scr)


def finish(k):
    nc = k.nc
    out = k.at(0, KT, SEQ)
    rms(k, k.h, "final_g", scratch=4096, dst=out)
    with nc.Block() as block:
        @block.sync
        def _(sp):
            sp.dma_start(k.dram["out"], out).then_inc(k.stored.handle, 16)
            sp.wait_ge(k.stored.handle, k.stored.at(16))
    k.stored.advance(16)


def build(nc, dram):
    with ExitStack() as ctx:
        k = Core(nc, ctx, dram)
        start(k)
        for layer in range(2):
            ffn(k, "ffn1", layer)
            (odd_mixer if layer else even_mixer)(k)
            ffn(k, "ffn2", layer)
            ple(k, layer)
        second_even(k)
        second_odd(k)
        finish(k)


def kernel(**inputs):
    import concourse.bacc as bacc
    from concourse.bass_utils import run_bass_kernel_spmd as run

    a = {n: np.asarray(v) for n, v in inputs.items()}

    def feature_major(x):
        return np.ascontiguousarray(x.T.reshape(-1, P, x.shape[0]).transpose(1, 0, 2))

    arrays = {
        "x": feature_major(a["x"][0]),
        "p": np.stack([feature_major(a["p"][l, 0]) for l in range(2)]),
        "mem": feature_major(a["mem_2"][0]),
        "pos": np.ascontiguousarray(a["pos"].reshape(1, SEQ)),
        "stream": lay_stream(a),
        "vec": lay_vectors(a),
        "cst": np.concatenate([CONSTS[n] for n in CONST_AT], axis=1),
        "w_uv": np.ascontiguousarray(a["a_w_uv"][0].transpose(1, 0, 2).reshape(P, 512)),
        "w_s": np.ascontiguousarray(a["c_w_s"][0].transpose(2, 0, 1)),
        "b_s": np.ascontiguousarray(np.repeat(a["c_b_s"][0], 64, axis=0).reshape(4, P, P).transpose(1, 0, 2)),
        "cln": np.concatenate([a["c_ln_g"], a["c_ln_b"]], axis=0),
        "pool_w": np.ascontiguousarray(a["ev_pool_w_2"][0].reshape(8, 96, 192).transpose(1, 0, 2)),
        "pool_recip": pool_tables().reshape(P, 4, SEQ),
        "rotary": rotary_tables().reshape(P, 2, SEQ),
        "decay": decay_tables().reshape(P, 4, SEQ),
        "cmp_w2": np.ascontiguousarray(a["od_cmp_w2_2"][0].reshape(4, P, P).transpose(1, 0, 2)),
        "rel": np.ascontiguousarray(a["rel_bias_2"]),
        "buckets": bucket_table(),
    }
    nc = bacc.Bacc("TRN2", target_bir_lowering=False, num_devices=1)
    dram = {n: nc.dram_tensor(f"in_{n}", v.shape, mybir.dt.from_np(v.dtype), kind="ExternalInput").ap()
            for n, v in arrays.items()}
    dram["frev"] = nc.dram_tensor("frev", (NSA_H, FREV), F32, kind="Internal").ap()
    dram["out"] = nc.dram_tensor("out_0", (P, KT, SEQ), F32, kind="ExternalOutput").ap()
    build(nc, dram)
    r = run(nc, [{f"in_{n}": v for n, v in arrays.items()}], core_ids=[0])
    got = r.results[0]["out_0"]
    return np.ascontiguousarray(got.transpose(2, 1, 0).reshape(1, SEQ, D))
```

```python
from contextlib import ExitStack

import numpy as np

import concourse.bass as bass
from concourse import mybir
from concourse.alu_op_type import AluOpType as ALU

F32 = mybir.dt.float32
F32R = mybir.dt.float32r
I32 = mybir.dt.int32
ACT = mybir.ActivationFunctionType

P = 128
SEQ = 512
TT = SEQ // P
D = 1024
KT = D // P
DFF = 2816
FT = DFF // P
EPS = 1e-6
BIG = 1e30
RING = 3
SPLIT = 3
SLAB = 1024
NMEM = 256
POOL_W = (2, 4, 8, 16)
RET_H, RET_DV = 4, 192
NSA_H, NSA_G = 12, 2
NCMP = (SEQ - 32) // 16 + 1
BIASW = 896
CONV_SPLIT = 16
FREV = 1024
TOPK = 128
SHRINK = 2.0 ** -40
OVERFLOW = (3.4028235e38 / 128) ** 0.5 * SHRINK


def t5_bucket(rel):
    n = np.maximum(rel, 0)
    nf = np.maximum(n, 1).astype(np.float32)
    large = 16 + (np.log(nf / np.float32(16)) / np.float32(np.log(8.0)) * np.float32(16)).astype(np.int32)
    return np.where(n < 16, n, np.minimum(large, 31))


def constant_pack():
    p = np.arange(P)
    f = np.float32
    out = {}
    out["ident"] = np.eye(P, dtype=f)
    out["flip"] = np.eye(P, dtype=f)[::-1]
    out["ones"] = np.ones((P, P), f)
    out["ones64"] = (p[:, None] // 64 == p[None, :] // 64).astype(f)
    for name, half in (("rot64", 32), ("rot128", 64)):
        r = np.zeros((P, P), f)
        for m in range(P):
            if m % (2 * half) < half:
                r[m + half, m] = -1.0
            else:
                r[m - half, m] = 1.0
        out[name] = r
    y = np.arange(SEQ)
    out["chunkmask"] = np.where((y[None, :] >= 448) & (p[:, None] < 64), f(BIG), f(0)).astype(f)
    inv = (10000.0 ** (-np.arange(0, 64, 2) / 64)).astype(f)
    out["inv64"] = inv[p % 32][:, None]
    out["seen"] = (p >= 31).astype(f)[:, None]
    out["eps"] = np.full((P, 1), EPS, f)
    out["eps_small"] = np.full((P, 1), EPS * SHRINK ** 2, f)
    return out


def rotary_tables():
    f = np.float32
    inv = (10000.0 ** (-np.arange(64) / 64)).astype(f)
    ang = (np.arange(SEQ, dtype=f)[None, :] * inv[:, None]).astype(f)
    c, s = np.cos(ang), np.sin(ang)
    return np.concatenate([np.tile(c, (2, 1)), np.tile(s, (2, 1))], axis=1).astype(f)


def decay_tables():
    m, x = np.arange(P)[:, None], np.arange(SEQ)[None, :]
    out = []
    for h in range(RET_H):
        lg = np.log(1.0 - 2.0 ** (-5.0 - h))
        out.append(np.where(x >= m, np.exp(lg * np.maximum(x - m, 0)), 0.0))
    return np.concatenate(out, axis=1).astype(np.float32)


def pool_tables():
    t = np.arange(SEQ)
    return np.tile(np.concatenate([1.0 / np.minimum(t + 1, w) for w in POOL_W])[None], (P, 1)).astype(np.float32)


def bucket_table():
    z = np.arange(FREV)
    rel = 511 - z
    out = np.zeros((33, FREV), np.float32)
    b = t5_bucket(rel)
    out[b[z <= 511], z[z <= 511]] = 1.0
    out[32, z > 511] = 1.0
    return out


CONSTS = constant_pack()
CONST_AT = {}
_at = 0
for _n, _a in CONSTS.items():
    CONST_AT[_n] = (_at, _a.shape[1])
    _at += _a.shape[1]
CONST_N = _at

def tiles(lo, n, w=P):
    return [(lo + i * w, w) for i in range(n)]


EV = dict(aq=0, ak=512, av=576, iq=704, ik=960, iw=1024, bq=1028, bk=1540, bv=2052)
EV_F = (tiles(EV["aq"], 4) + [(EV["ak"], 64, 2)] + tiles(EV["iq"], 2) + [(EV["ik"], 64, 2)]
        + tiles(EV["bq"], 4) + tiles(EV["bk"], 4))
EV_T = [(EV["av"], P), (EV["iw"], 4)] + tiles(EV["bv"], 4)
OD_F = [t for c in range(4) for t in (tiles(1024, 4)[c], tiles(1536, 4)[c])] + tiles(0, 4)
OD_T = tiles(512, 4)
E2 = dict(za=0, rq=768, rk=1280, rv=1792, xq=2560, gate=3072)
O2 = dict(q=0, kc=1536, vc=1792, ks=2048, vs=2304, kw=2560, vw=2816, gl=3072, xq=3108, gate=3620)


ZA_ORDER = (6, 7, 4, 5, 2, 3, 0, 1)


def stream_plan():
    plan = []
    for l in range(2):
        for n in ("ffn1", "mix", "ffn2"):
            if n == "mix":
                if l == 0:
                    plan += [("ev_f", "ev_w_in", 0, "cols", EV_F), ("ev_t", "ev_w_in", 0, "tcols", EV_T),
                             ("ev_out", "ev_w_out", 0, "rows", tiles(0, KT))]
                else:
                    plan += [("od_f", "od_w_in", 0, "cols", OD_F), ("od_t", "od_w_in", 0, "tcols", OD_T),
                             ("od_out", "od_w_out", 0, "rows", tiles(0, KT))]
                continue
            plan += [(f"{n}_up{l}", (f"{n}_wg", f"{n}_wu"), l, "pair", tiles(0, FT)),
                     (f"{n}_down{l}", f"{n}_wd", l, "rows", tiles(0, FT))]
        plan += [(f"ple_p{l}", "ple_wproj", l, "rows", tiles(0, 2)),
                 (f"ple_g{l}", "ple_wgate", l, "cols", tiles(0, KT))]
    for l, (w, c, kv, wo) in enumerate((("ev_w_in_2", E2, "ev_w_mem_kv_2", "ev_w_out_2"),
                                        ("od_w_in_2", O2, "od_w_mem_kv_2", "od_w_out_2"))):
        plan += [(f"mk{l}", kv, 0, "cols", tiles(0, 4)), (f"mv{l}", kv, 0, "tcols", tiles(512, 4)),
                 (f"xq{l}", w, 0, "cols", tiles(c["xq"], 4))]
        if l == 0:
            plan += [("za", w, 0, "cols", [tiles(c["za"], 8, 96)[m] for m in ZA_ORDER]),
                     ("rqk", w, 0, "cols", tiles(c["rq"], 8)), ("rv", w, 0, "tcols", tiles(c["rv"], 6)),
                     ("gate0", w, 0, "cols", tiles(c["gate"], 16, 96) + tiles(c["gate"] + 1536, 4)),
                     ("wo0", wo, 0, "rows", tiles(0, 16, 96) + tiles(1536, 4))]
        else:
            plan += [("kvc", w, 0, "cols", tiles(c["kc"], 4)),
                     ("nsaqk", w, 0, "cols", tiles(c["q"], 12) + tiles(c["ks"], 2) + tiles(c["kw"], 2)),
                     ("nsav", w, 0, "tcols", tiles(c["vs"], 2) + tiles(c["vw"], 2) + [(c["gl"], 36)]),
                     ("gate1", w, 0, "cols", tiles(c["gate"], 16)),
                     ("wo1", wo, 0, "rows", tiles(0, 16))]
    return plan


def slab_count(kind, t):
    return {"cols": len(t), "tcols": 2 * ((len(t) + 1) // 2), "pair": 2 * len(t), "rows": len(t)}[kind]


PLAN = stream_plan()
STREAM_AT = {}
_at = 0
for _s, _w, _l, _k, _t in PLAN:
    STREAM_AT[_s] = (_at, slab_count(_k, _t))
    _at += slab_count(_k, _t)
NSLAB = _at


def lay_stream(inputs):
    out = np.zeros((NSLAB, P, SLAB), np.float32)

    def column_slabs(w, t, at, step):
        w3 = w.reshape(KT, P, -1).transpose(1, 0, 2)
        for i, tile in enumerate(t):
            lo, n = tile[:2]
            view = out[at + i * step].reshape(P, KT, P)
            for r in range(tile[2] if len(tile) > 2 else 1):
                view[:, :, r * n:(r + 1) * n] = w3[:, :, lo:lo + n]

    for stage, name, layer, kind, t in PLAN:
        at, _ = STREAM_AT[stage]
        if kind == "pair":
            for j in range(2):
                column_slabs(inputs[name[j]][layer], t, at + j, 2)
        elif kind == "cols":
            column_slabs(inputs[name][layer], t, at, 1)
        elif kind == "tcols":
            w3 = inputs[name][layer].reshape(KT, P, -1).transpose(1, 0, 2)
            for i, (lo, n) in enumerate(t):
                for half in range(2):
                    view = out[at + 2 * (i // 2) + half].reshape(P, 4, 2, P)
                    view[:, :, i % 2, 0:n] = w3[:, 4 * half:4 * half + 4, lo:lo + n]
        else:
            for i, (lo, n) in enumerate(t):
                out[at + i, :n] = inputs[name][layer][lo:lo + n]
    return out


VEC = []
for _l in range(2):
    VEC += [(f"ffn1_g{_l}", "ffn1_g", _l, P), (f"mix_g{_l}", "mix_g", _l, P), (f"ffn2_g{_l}", "ffn2_g", _l, P),
            (f"ple_g{_l}", "ple_g", _l, P), (f"norm2_g{_l}", "norm_g_2", _l, P)]
VEC += [("final_g", "final_g_2", None, P), ("memnorm_g", "mem_norm_g_2", None, P),
        ("subln_g", "b_subln_g", 0, P), ("conv_b", "d_conv_b", 0, P),
        ("dln_g", "d_ln_g", 0, P), ("dln_b", "d_ln_b", 0, P), ("pool_scale", "ev_pool_scale_2", 0, 96)]
VEC_N = {"ffn1_g": 8, "mix_g": 8, "ffn2_g": 8, "ple_g": 8, "norm_g_2": 8, "final_g_2": 8, "mem_norm_g_2": 8,
         "b_subln_g": 1, "d_conv_b": 4, "d_ln_g": 4, "d_ln_b": 4, "ev_pool_scale_2": 8}
VEC_AT = {}
_at = 0
for _n, _a, _i, _w in VEC:
    VEC_AT[_n] = (_at, VEC_N[_a])
    _at += VEC_N[_a]
for _n, _c in (("aq_g", 1), ("ak_g", 1), ("bq_g", 1), ("bk_g", 1), ("conv_w", 4 * 31), ("lams", 4),
               ("cmp_b1", 4), ("cmp_pe", 64)):
    VEC_AT[_n] = (_at, _c)
    _at += _c
VEC_TOTAL = _at


def lay_vectors(inputs):
    out = np.zeros((P, VEC_TOTAL), np.float32)
    for name, arr, idx, w in VEC:
        at, n = VEC_AT[name]
        a = inputs[arr] if idx is None else inputs[arr][idx]
        out[:w, at:at + n] = a.reshape(n, w).T
    for name, arr in (("aq_g", "a_q_g"), ("ak_g", "a_k_g"), ("bq_g", "b_q_g"), ("bk_g", "b_k_g")):
        out[0:64, VEC_AT[name][0]] = inputs[arr][0]
        out[64:128, VEC_AT[name][0]] = inputs[arr][0]
    at = VEC_AT["conv_w"][0]
    out[:, at:at + 124] = inputs["d_conv_w"][0].reshape(31, 4, P).transpose(2, 1, 0).reshape(P, 124)
    at = VEC_AT["lams"][0]
    for j, arr in enumerate(("b_lam_q1", "b_lam_k1", "b_lam_q2", "b_lam_k2")):
        out[0:64, at + j] = inputs[arr][0]
    at = VEC_AT["cmp_b1"][0]
    out[:, at:at + 4] = inputs["od_cmp_b1_2"][0].reshape(4, P).T
    at = VEC_AT["cmp_pe"][0]
    out[:, at:at + 64] = inputs["od_cmp_pe_2"][0].reshape(64, P).T
    return out


class Signal:

    def __init__(self, handle):
        self.handle, self.base = handle, 0

    def at(self, n):
        return self.base + n

    def advance(self, n):
        self.base += n


class Core:

    def __init__(self, nc, ctx, dram):
        self.nc, self.dram = nc, dram
        self.ctx = ctx
        sb = lambda n, s, dt=F32: ctx.enter_context(nc.sbuf_tensor(n, s, dt))
        self.ring = sb("ring", [P, RING, SLAB])
        self.w_hi = sb("w_hi", [P, SPLIT, SLAB], F32R)
        self.w_lo = sb("w_lo", [P, SPLIT, SLAB], F32R)
        self.h = sb("h", [P, KT, SEQ])
        self.x_hi = sb("x_hi", [P, KT, SEQ], F32R)
        self.x_lo = sb("x_lo", [P, KT, SEQ], F32R)
        self.r_hi = sb("r_hi", [P, 2, SEQ], F32R)
        self.r_lo = sb("r_lo", [P, 2, SEQ], F32R)
        self.inv = sb("inv", [P, SEQ])
        self.cst = sb("cst", [P, CONST_N])
        self.vec = sb("vec", [P, VEC_TOTAL])
        self.arena_n = (nc.sbuf_top - nc.sbuf_base) // 4 - 8
        self.arena = sb("arena", [P, self.arena_n])
        self.ps = ctx.enter_context(nc.psum_tensor("ps", [P, 8, SEQ], F32))
        names = ("product_done", "evacuated", "squares_done", "pairs_done", "sum_done", "root_done", "vec_chain",
                 "pool_chain", "act_step", "dve_step", "pe_step", "pe_step2", "pool_step", "dve_read", "scores_done",
                 "biased", "exp_done", "diag_done", "turned", "turned_copied", "out_done", "out_copied", "tmp_ready",
                 "high_done", "split_done", "raw_done", "hi_done", "lo_done", "x_ready", "h_written", "row_part",
                 "row_done", "row_high", "row_low", "x_loaded", "cst_loaded", "bias_loaded")
        self.s = {n: Signal(ctx.enter_context(nc.semaphore(n))) for n in names}
        self.slab_loaded = [ctx.enter_context(nc.semaphore(f"slab_loaded{i}")) for i in range(RING)]
        self.aux = Signal(ctx.enter_context(nc.semaphore("aux_loaded")))
        self.stored = Signal(ctx.enter_context(nc.semaphore("stored")))
        self.cmp_loaded = [Signal(ctx.enter_context(nc.semaphore(f"cmp_loaded{i}"))) for i in range(2)]
        self.loaded = self.highs = self.lows = 0
        self.slab_end = []
        self.early = []
        self.late = []

    def c(self, name):
        a, n = CONST_AT[name]
        return self.cst[:, a:a + n]

    def v(self, name, j=0, rows=P):
        a, _ = VEC_AT[name]
        return self.vec[0:rows, a + j:a + j + 1]

    def at(self, off, *shape):
        n = int(np.prod(shape))
        assert off + n <= self.arena_n, (off, shape, self.arena_n)
        a = self.arena[:, off:off + n]
        if len(shape) == 2:
            a = a.rearrange("p (a b) -> p a b", b=shape[1])
        elif len(shape) == 3:
            a = a.rearrange("p (a b c) -> p a b c", b=shape[1], c=shape[2])
        return a

    def vlink(self, ins):
        s = self.s["vec_chain"]
        ins.then_inc(s.handle, 1)
        s.advance(1)
        self.nc.vector.wait_ge(s.handle, s.base)

    def plink(self, ins):
        s = self.s["pool_chain"]
        ins.then_inc(s.handle, 1)
        s.advance(1)
        self.nc.gpsimd.wait_ge(s.handle, s.base)

    def slabs_end(self, signal, values):
        self.slab_end += [(signal.handle, v) for v in values]

    def slabs_upto(self, sp, upto):
        while self.loaded < min(NSLAB, upto):
            n = self.loaded
            if n >= RING:
                sp.wait_ge(self.s["split_done"].handle, n - RING + 1)
            sp.dma_start(self.ring[:, n % RING, :], self.dram["stream"][n]).then_inc(self.slab_loaded[n % RING], 16)
            self.loaded += 1

    def stream(self, sp):
        for dst, src in self.early:
            sp.dma_start(dst, src).then_inc(self.aux.handle, 16)
        self.aux.advance(16 * len(self.early))
        self.slabs_upto(sp, len(self.slab_end) + SPLIT + RING)
        for dst, src, signal in self.late:
            sp.wait_ge(self.stored.handle, self.stored.at(0))
            sp.dma_start(dst, src).then_inc(signal.handle, 16)
        if self.early:
            sp.wait_ge(self.aux.handle, self.aux.at(0))
        self.early, self.late = [], []

    def high(self, act, upto):
        while self.highs < min(NSLAB, upto):
            n = self.highs
            act.wait_ge(self.slab_loaded[n % RING], 16 * (n // RING + 1))
            if n >= SPLIT:
                act.wait_ge(*self.slab_end[n - SPLIT])
            self.nc.scalar.copy(self.w_hi[:, n % SPLIT, :],
                                self.ring[:, n % RING, :]).then_inc(self.s["high_done"].handle, 1)
            self.highs += 1

    def all_high(self, act):
        self.high(act, len(self.slab_end) + SPLIT)

    def low(self, pool, square=None):
        if square:
            self.lows_upto(pool, len(self.slab_end) + SPLIT - 1)
            square.pool(pool)
        self.lows_upto(pool, len(self.slab_end) + SPLIT)

    def lows_upto(self, pool, upto):
        while self.lows < min(NSLAB, upto):
            n = self.lows
            pool.wait_ge(self.s["high_done"].handle, n + 1)
            self.nc.gpsimd.tensor_tensor(self.w_lo[:, n % SPLIT, :], self.ring[:, n % RING, :],
                                         self.w_hi[:, n % SPLIT, :].bitcast(F32),
                                         ALU.subtract).then_inc(self.s["split_done"].handle, 1)
            self.lows += 1

    def slab(self, pe, n, *shape):
        pe.wait_ge(self.s["split_done"].handle, n + 1)
        parts = self.w_hi[:, n % SPLIT, :], self.w_lo[:, n % SPLIT, :]
        return [w.rearrange("p (a b) -> p a b", b=shape[-1]) for w in parts]

    def product(self, out, a, b, start, stop):
        nc = self.nc
        nc.tensor.matmul(out, a[0], b[0], start=start, stop=False)
        nc.tensor.matmul(out, a[0], b[1], start=False, stop=False)
        return nc.tensor.matmul(out, a[1], b[0], start=False, stop=stop)


def start(k, cos, sin):
    nc, s = k.nc, k.s
    pos_i = k.at(14336, SEQ).bitcast(I32)
    tab, hot, frev = k.at(16384, NSA_H), k.at(16400, FREV), k.at(17424, FREV)
    k.early = [(k.vec[:, :], k.dram["vec"]), (pos_i, k.dram["pos"].partition_broadcast(P)), (tab[0:32, :], k.dram["rel"]),
                (hot[0:33, :], k.dram["buckets"])]

    square = MeanSquare(k, k.h)
    rotary = Rotary(k, cos, sin, pos_i, k.at(14848, SEQ), k.at(15360, 2, SEQ))
    negated, product, copied = s["tmp_ready"], s["pe_step"], s["act_step"]
    x_in, cst_in = s["x_loaded"], s["cst_loaded"]
    with nc.Block() as block:
        @block.sync
        def _(sp):
            sp.dma_start(k.h[:, :, :], k.dram["x"]).then_inc(x_in.handle, 16)
            sp.dma_start(k.cst[:, :], k.dram["cst"]).then_inc(cst_in.handle, 16)
            k.stream(sp)
            sp.wait_ge(copied.handle, copied.at(2))
            sp.dma_start(k.dram["frev"], frev[0:NSA_H, :]).then_inc(k.stored.handle, 16)

        @block.gpsimd
        def _(pool):
            square.pool(pool)
            k.low(pool)

        @block.scalar
        def _(act):
            act.wait_ge(x_in.handle, x_in.at(16))
            act.wait_ge(cst_in.handle, cst_in.at(16))
            square.act(act, k.all_high)
            for j in range(2):
                act.wait_ge(product.handle, product.at(j + 1))
                nc.scalar.copy(frev[0:NSA_H, j * SEQ:(j + 1) * SEQ], k.ps[0:NSA_H, 1 + j, :]).then_inc(copied.handle, 1)

        @block.tensor
        def _(pe):
            pe.wait_ge(cst_in.handle, cst_in.at(16))
            square.pe(pe)
            pe.wait_ge(negated.handle, negated.at(1))
            for j in range(2):
                nc.tensor.matmul(k.ps[0:NSA_H, 1 + j, :], tab[0:33, :], hot[0:33, j * SEQ:(j + 1) * SEQ], start=True,
                                 stop=True).then_inc(product.handle, 1)

        @block.vector
        def _(dve):
            dve.wait_ge(k.aux.handle, k.aux.at(0))
            nc.vector.tensor_scalar(tab[0:32, :], tab[0:32, :], -1.0, None, ALU.mult)
            nc.vector.memset(tab[32:33, :], BIG).then_inc(negated.handle, 1)
            square.dve(dve)
    x_in.advance(16)
    cst_in.advance(16)
    negated.advance(1)
    product.advance(2)
    copied.advance(2)
    k.stored.advance(16)
    return rotary


class MeanSquare:

    def __init__(self, k, src, n=SEQ, inv=None, written=False):
        self.k, self.src, self.n, self.written, self.bank = k, src, n, written, 0
        self.inv = k.inv[:, 0:n] if inv is None else inv
        self.sq, self.pair = k.at(k.arena_n - 4608, 4, SEQ), k.at(k.arena_n - 2560, 2, SEQ)
        self.root = k.at(k.arena_n - 1536, SEQ)
        self.squared, self.paired, self.summed, self.rooted = (k.s[n] for n in ("squares_done", "pairs_done", "sum_done",
                                                                               "root_done"))

    def act(self, act, between=None):
        k, n = self.k, self.n
        for c in range(KT):
            if self.written:
                act.wait_ge(k.s["h_written"].handle, k.s["h_written"].at(c + 1))
            if c >= 4:
                act.wait_ge(self.paired.handle, self.paired.at((c - 4) // 2 + 1))
            k.nc.scalar.activation(self.sq[:, c % 4, 0:n], self.src[:, c, 0:n],
                                   ACT.Square).then_inc(self.squared.handle, 1)
        if between:
            between(act)
        act.wait_ge(self.summed.handle, self.summed.at(KT // 2))
        k.nc.scalar.activation(self.root[:, 0:n], k.ps[:, self.bank, 0:n], ACT.Sqrt, bias=k.c("eps"),
                               scale=1.0 / D).then_inc(self.rooted.handle, 1)

    def pool(self, pool):
        k, n = self.k, self.n
        for j in range(KT // 2):
            pool.wait_ge(self.squared.handle, self.squared.at(2 * j + 2))
            if j >= 2:
                pool.wait_ge(self.summed.handle, self.summed.at(j - 1))
            k.nc.gpsimd.tensor_tensor(self.pair[:, j % 2, 0:n], self.sq[:, 2 * j % 4, 0:n], self.sq[:, 2 * j % 4 + 1, 0:n],
                                      ALU.add).then_inc(self.paired.handle, 1)

    def pe(self, pe):
        k, n = self.k, self.n
        for j in range(KT // 2):
            pe.wait_ge(self.paired.handle, self.paired.at(j + 1))
            k.nc.tensor.matmul(k.ps[:, self.bank, 0:n], k.c("ones"), self.pair[:, j % 2, 0:n], start=(j == 0),
                               stop=(j == KT // 2 - 1)).then_inc(self.summed.handle, 1)

    def dve(self, dve):
        dve.wait_ge(self.rooted.handle, self.rooted.at(1))
        self.k.nc.vector.reciprocal(self.inv, self.root[:, 0:self.n])
        self.close()

    def close(self):
        self.squared.advance(KT)
        self.paired.advance(KT // 2)
        self.summed.advance(KT // 2)
        self.rooted.advance(1)
        if self.written:
            self.k.s["h_written"].advance(KT)

    def alone(self, block):
        block.scalar(self.act)
        block.gpsimd(self.pool)
        block.tensor(self.pe)
        block.vector(self.dve)


class Normalise:

    def __init__(self, k, src, gain, n=SEQ, inv=None):
        self.k, self.src, self.gain, self.n = k, src, gain, n
        self.inv = k.inv[:, 0:n] if inv is None else inv
        self.raw = k.at(k.arena_n - 1024, 2, SEQ)
        self.raws, self.his, self.ready = k.s["raw_done"], k.s["hi_done"], k.s["x_ready"]

    def act(self, act):
        k, n = self.k, self.n
        for c in range(KT):
            act.wait_ge(self.raws.handle, self.raws.at(c + 1))
            k.nc.scalar.copy(k.x_hi[:, c, 0:n], self.raw[:, c % 2, 0:n]).then_inc(self.his.handle, 1)

    def dve(self, dve):
        k, n = self.k, self.n

        def low(c):
            dve.wait_ge(self.his.handle, self.his.at(c + 1))
            k.nc.vector.tensor_tensor(k.x_lo[:, c, 0:n], self.raw[:, c % 2, 0:n], k.x_hi[:, c, 0:n].bitcast(F32),
                                      ALU.subtract).then_inc(self.ready.handle, 1)
            dve.wait_ge(self.ready.handle, self.ready.at(c + 1))

        for c in range(KT):
            k.nc.vector.scalar_tensor_tensor(self.raw[:, c % 2, 0:n], self.src[:, c, 0:n], k.v(self.gain, c),
                                             self.inv, ALU.mult, ALU.mult).then_inc(self.raws.handle, 1)
            if c >= 1:
                low(c - 1)
        low(KT - 1)

    def first_two(self, pe, slabs, widths, done):
        k, n = self.k, self.n
        for c in range(KT):
            pe.wait_ge(self.ready.handle, self.ready.at(c + 1))
            for m, ((hi, lo), w) in enumerate(zip(slabs, widths)):
                ins = k.product(k.ps[0:w, m, 0:n], (hi[:, c, 0:w], lo[:, c, 0:w]),
                                (k.x_hi[:, c, 0:n], k.x_lo[:, c, 0:n]), c == 0, c == KT - 1)
                if c == KT - 1:
                    ins.then_inc(done[m].handle, 1)

    def close(self):
        for g in (self.raws, self.his, self.ready):
            g.advance(KT)


def dense_f(k, stage, widths, evacuate, n=SEQ, norm=None, meanwhile=None):
    nc, s = k.nc, k.s
    first, slabs = STREAM_AT[stage]
    done, read = s["product_done"], s["evacuated"]
    assert slabs == len(widths)
    k.slabs_end(done, [done.at(m + 1) for m in range(slabs)])

    with nc.Block() as block:
        @block.sync
        def _(sp):
            k.stream(sp)

        @block.gpsimd
        def _(pool):
            k.low(pool)

        @block.tensor
        def _(pe):
            if norm:
                norm.first_two(pe, [k.slab(pe, first + m, P) for m in range(2)], widths, (done, done))
            for m in range(2 if norm else 0, slabs):
                w = widths[m]
                hi, lo = k.slab(pe, first + m, P)
                if m >= 8:
                    pe.wait_ge(read.handle, read.at(m - 7))
                for c in range(KT):
                    ins = k.product(k.ps[0:w, m % 8, 0:n], (hi[:, c, 0:w], lo[:, c, 0:w]),
                                    (k.x_hi[:, c, 0:n], k.x_lo[:, c, 0:n]), c == 0, c == KT - 1)
                ins.then_inc(done.handle, 1)

        @block.scalar
        def _(act):
            if norm:
                norm.act(act)
            for m, w in enumerate(widths):
                k.high(act, first + m + SPLIT)
                act.wait_ge(done.handle, done.at(m + 1))
                k.high(act, first + m + 1 + SPLIT)
                evacuate(m, k.ps[0:w, m % 8, 0:n]).then_inc(read.handle, 1)

        @block.vector
        def _(dve):
            if norm:
                norm.dve(dve)
            if meanwhile:
                meanwhile(dve, read)
    if norm:
        norm.close()
    done.advance(slabs)
    read.advance(slabs)


def dense_t(k, stage, widths, evacuate, tts=TT, meanwhile=None):
    nc, s = k.nc, k.s
    first, slabs = STREAM_AT[stage]
    part, done, read = s["pe_step"], s["product_done"], s["evacuated"]
    assert slabs == 2 * len(widths)
    for j in range(len(widths)):
        k.slabs_end(part, [part.at(j + 1)])
        k.slabs_end(done, [done.at(tts * (j + 1))])

    with nc.Block() as block:
        @block.sync
        def _(sp):
            k.stream(sp)

        @block.gpsimd
        def _(pool):
            k.low(pool)

        @block.tensor
        def _(pe):
            for j in range(len(widths)):
                for half in range(2):
                    hi, lo = k.slab(pe, first + 2 * j + half, 256)
                    for t in range(tts):
                        u = j * tts + t
                        if u >= 8 and half == 0:
                            pe.wait_ge(read.handle, read.at(u - 7))
                        tok = slice(t * P, (t + 1) * P)
                        for ci in range(4):
                            c = 4 * half + ci
                            ins = k.product(k.ps[:, u % 8, 0:256], (k.x_hi[:, c, tok], k.x_lo[:, c, tok]),
                                            (hi[:, ci, :], lo[:, ci, :]), c == 0, c == KT - 1)
                        if half:
                            ins.then_inc(done.handle, 1)
                    if half == 0:
                        ins.then_inc(part.handle, 1)

        @block.scalar
        def _(act):
            for j, w in enumerate(widths):
                for t in range(tts):
                    u = j * tts + t
                    k.high(act, first + 2 * j + 1 + SPLIT)
                    act.wait_ge(done.handle, done.at(u + 1))
                    if t == tts - 1:
                        k.high(act, first + 2 * j + 2 + SPLIT)
                    evacuate(j, t, k.ps[:, u % 8, 0:w]).then_inc(read.handle, 1)
            k.all_high(act)

        if meanwhile:
            block.vector(meanwhile)
    part.advance(len(widths))
    done.advance(tts * len(widths))
    read.advance(tts * len(widths))


def dense_gated(k, stage, widths, func, finish, scratch, norm=None, square=None):
    nc, s = k.nc, k.s
    first, slabs = STREAM_AT[stage]
    done, gate, read = s["product_done"], s["act_step"], s["evacuated"]
    buf = k.at(scratch, 4, SEQ)
    n = len(widths)
    free = k.s["h_written"] if square else read
    k.slabs_end(done, [done.at(m + 1) for m in range(n)])

    with nc.Block() as block:
        @block.sync
        def _(sp):
            k.stream(sp)

        @block.gpsimd
        def _(pool):
            k.low(pool, square)

        @block.tensor
        def _(pe):
            if norm:
                norm.first_two(pe, [k.slab(pe, first + m, P) for m in range(2)], widths, (done, done))
            for m in range(2 if norm else 0, n):
                w = widths[m]
                hi, lo = k.slab(pe, first + m, P)
                if m >= 8:
                    pe.wait_ge(gate.handle, gate.at(m - 7))
                for c in range(KT):
                    ins = k.product(k.ps[0:w, m % 8, :], (hi[:, c, 0:w], lo[:, c, 0:w]),
                                    (k.x_hi[:, c, :], k.x_lo[:, c, :]), c == 0, c == KT - 1)
                ins.then_inc(done.handle, 1)
            if square:
                square.pe(pe)

        @block.scalar
        def _(act):
            if norm:
                norm.act(act)
            for m, w in enumerate(widths):
                k.high(act, first + m + SPLIT)
                act.wait_ge(done.handle, done.at(m + 1))
                k.high(act, first + m + 1 + SPLIT)
                if m >= 4:
                    act.wait_ge(free.handle, free.at(m - 3))
                nc.scalar.activation(buf[0:w, m % 4, :], k.ps[0:w, m % 8, :], func).then_inc(gate.handle, 1)
            if square:
                square.act(act)

        @block.vector
        def _(dve):
            if norm:
                norm.dve(dve)
            for m, w in enumerate(widths):
                dve.wait_ge(gate.handle, gate.at(m + 1))
                ins = finish(m, buf[0:w, m % 4, :])
                ins.then_inc((k.s["h_written"] if square else read).handle, 1)
            if square:
                square.dve(dve)
    if norm:
        norm.close()
    for g in (done, gate) + (() if square else (read,)):
        g.advance(n)


class Rows:

    def __init__(self, k, stage, x, heights, evacuate, square=None, bank=0):
        self.k, self.x, self.heights, self.evacuate, self.square = k, x, heights, evacuate, square
        self.first, slabs = STREAM_AT[stage]
        self.n, self.bank = len(heights), bank
        assert slabs == self.n
        self.part, self.done, self.his, self.los = (k.s[n] for n in ("row_part", "row_done", "row_high", "row_low"))
        k.slabs_end(self.part, [self.part.at(j + 1) for j in range(self.n - 1)])
        k.slabs_end(self.done, [self.done.at(KT)])
        if square:
            square.bank = bank

    def act(self, act, tile_ready=None):
        k = self.k
        for i, w in enumerate(self.heights):
            if i >= 2:
                k.high(act, self.first + i - 2 + SPLIT)
                act.wait_ge(self.part.handle, self.part.at(i - 1))
            if tile_ready:
                tile_ready(act, i)
            k.nc.scalar.copy(k.r_hi[0:w, i % 2, :], self.x[0:w, i, :]).then_inc(self.his.handle, 1)
        if self.square:
            k.high(act, self.first + self.n - 1 + SPLIT)
            self.square.act(act)
        k.all_high(act)

    def pe(self, pe, bank_free=None):
        k = self.k
        for i, w in enumerate(self.heights):
            hi, lo = k.slab(pe, self.first + i, P)
            pe.wait_ge(self.los.handle, self.los.at(i + 1))
            for m in range(KT):
                b = (self.bank + m) % 8
                if i == 0 and bank_free:
                    bank_free(pe, b)
                ins = k.product(k.ps[:, b, :], (hi[0:w, m, :], lo[0:w, m, :]),
                                (k.r_hi[0:w, i % 2, :], k.r_lo[0:w, i % 2, :]), i == 0, i == self.n - 1)
                if i == self.n - 1:
                    ins.then_inc(self.done.handle, 1)
            if i < self.n - 1:
                ins.then_inc(self.part.handle, 1)
        if self.square:
            self.square.pe(pe)

    def dve(self, dve):
        k = self.k
        for i, w in enumerate(self.heights):
            dve.wait_ge(self.his.handle, self.his.at(i + 1))
            k.nc.vector.tensor_tensor(k.r_lo[0:w, i % 2, :], self.x[0:w, i, :], k.r_hi[0:w, i % 2, :].bitcast(F32),
                                      ALU.subtract).then_inc(self.los.handle, 1)
        for m in range(KT):
            dve.wait_ge(self.done.handle, self.done.at(m + 1))
            ins = self.evacuate(m, k.ps[:, (self.bank + m) % 8, :])
            if self.square:
                ins.then_inc(k.s["h_written"].handle, 1)
        if self.square:
            self.square.dve(dve)
        self.part.advance(self.n - 1)
        self.done.advance(KT)
        self.his.advance(self.n)
        self.los.advance(self.n)

    def alone(self):
        k = self.k
        with k.nc.Block() as block:
            @block.sync
            def _(sp):
                k.stream(sp)

            @block.gpsimd
            def _(pool):
                k.low(pool, self.square)

            block.scalar(self.act)
            block.tensor(self.pe)
            block.vector(self.dve)


def rows_add(k, stage, x, heights, scale, bank=0):
    return Rows(k, stage, x, heights,
                lambda m, ps: k.nc.vector.scalar_tensor_tensor(k.h[:, m, :], ps, scale, k.h[:, m, :], ALU.mult, ALU.add),
                MeanSquare(k, k.h, written=True), bank)


def ffn(k, name, layer, rotary=None):
    nc, s = k.nc, k.s
    hidden = k.at(0, FT, SEQ)
    norm = Normalise(k, k.h, f"{name}_g{layer}")
    first, slabs = STREAM_AT[f"{name}_up{layer}"]
    part, done, gate, read = s["pe_step"], s["product_done"], s["act_step"], s["evacuated"]
    for f in range(FT):
        k.slabs_end(part, [part.at(f + 1)])
        k.slabs_end(done, [done.at(f + 1)])
    down = rows_add(k, f"{name}_down{layer}", hidden, [P] * FT, 0.5, bank=(2 * FT) % 8)

    with nc.Block() as block:
        @block.sync
        def _(sp):
            k.stream(sp)

        @block.gpsimd
        def _(pool):
            k.low(pool, down.square)

        @block.tensor
        def _(pe):
            norm.first_two(pe, [k.slab(pe, first + j, P) for j in range(2)], (P, P), (part, done))
            for f in range(1, FT):
                if f >= 4:
                    pe.wait_ge(read.handle, read.at(f - 3))
                for j, finished in enumerate((part, done)):
                    hi, lo = k.slab(pe, first + 2 * f + j, P)
                    for c in range(KT):
                        ins = k.product(k.ps[:, (2 * f + j) % 8, :], (hi[:, c, :], lo[:, c, :]),
                                        (k.x_hi[:, c, :], k.x_lo[:, c, :]), c == 0, c == KT - 1)
                    ins.then_inc(finished.handle, 1)

            def bank_free(pe, b):
                last = max(f for f in range(FT) if b in ((2 * f) % 8, (2 * f + 1) % 8))
                pe.wait_ge(read.handle, read.at(last + 1))

            down.pe(pe, bank_free)

        @block.scalar
        def _(act):
            norm.act(act)
            for f in range(FT):
                k.high(act, first + 2 * f + SPLIT)
                act.wait_ge(part.handle, part.at(f + 1))
                nc.scalar.activation(hidden[:, f, :], k.ps[:, (2 * f) % 8, :], ACT.Silu).then_inc(gate.handle, 1)
                k.high(act, first + 2 * f + 1 + SPLIT)
                if rotary and f == 3:
                    rotary.act(act)
            down.act(act, lambda act, i: act.wait_ge(read.handle, read.at(i + 1)))

        @block.vector
        def _(dve):
            norm.dve(dve)
            if rotary:
                rotary.dve(dve)
            for f in range(FT):
                dve.wait_ge(gate.handle, gate.at(f + 1))
                dve.wait_ge(done.handle, done.at(f + 1))
                nc.vector.tensor_tensor(hidden[:, f, :], hidden[:, f, :], k.ps[:, (2 * f + 1) % 8, :],
                                        ALU.mult).then_inc(read.handle, 1)
            down.dve(dve)
    norm.close()
    for g in (part, done, gate, read):
        g.advance(FT)


def ple(k, layer):
    nc = k.nc
    pt = k.at(12288, 2, SEQ)
    proj = k.at(1024, KT, SEQ)
    Rows(k, f"ple_p{layer}", pt, [P] * 2, lambda m, ps: nc.vector.tensor_copy(proj[:, m, :], ps)).alone()

    def finish(m, gate):
        k.vlink(nc.vector.tensor_tensor(gate, gate, proj[:, m, :], ALU.mult))
        return nc.vector.tensor_tensor(k.h[:, m, :], k.h[:, m, :], gate, ALU.add)

    dense_gated(k, f"ple_g{layer}", [P] * KT, ACT.Sigmoid, finish, 8192, Normalise(k, k.h, f"ple_g{layer}"),
                MeanSquare(k, k.h, written=True))


ATTENTION = 3984


class Unit:

    def __init__(self, q, key, bias, v, gate=None, first=True, last=True, dst=None, clamp=False,
                 steps=0):
        self.q, self.key, self.bias, self.v, self.gate = q, key, bias, v, gate
        self.first, self.last, self.dst, self.clamp, self.steps = first, last, dst, clamp, steps
        self.w = key.shape[-1]


def attention(k, units, scratch, background=()):
    nc, s = k.nc, k.s
    n = len(units)
    ex = k.at(scratch, 5, SEQ)
    pt = k.at(scratch + 2560, 2, SEQ)
    dg = k.at(scratch + 3584, 3, P)
    low = k.at(scratch + 3968, 5)
    tot = k.at(scratch + 3973, 5)
    inv = k.at(scratch + 3978, 5)
    scored, biased, expd = s["scores_done"], s["biased"], s["exp_done"]
    diag, turned, copied = s["diag_done"], s["turned"], s["turned_copied"]
    summed, stored = s["out_done"], s["out_copied"]
    group = np.cumsum([u.first for u in units]) - 1
    last_of = {int(group[i]): i for i in range(n)}

    with nc.Block() as block:
        @block.tensor
        def _(pe):
            def scores(i):
                u = units[i]
                if i >= 4:
                    pe.wait_ge(biased.handle, biased.at(i - 3))
                nc.tensor.matmul(k.ps[:, i % 4, 0:u.w], u.q, u.key, start=True, stop=True).then_inc(scored.handle, 1)

            def turn(i):
                u = units[i]
                pe.wait_ge(diag.handle, diag.at(i + 1))
                if i >= 2:
                    pe.wait_ge(copied.handle, copied.at(i - 1))
                for j, (rows, _) in enumerate(u.v):
                    ins = nc.tensor.matmul(k.ps[0:rows, 4 + i % 2, j * P:(j + 1) * P],
                                           ex[:, i % 5, j * P:j * P + rows], dg[:, i % 3, :], start=True, stop=True)
                ins.then_inc(turned.handle, 1)

            def values(i):
                u = units[i]
                g = int(group[i])
                pe.wait_ge(copied.handle, copied.at(i + 1))
                if u.first and g >= 2:
                    pe.wait_ge(stored.handle, stored.at(g - 1))
                for j, (rows, v) in enumerate(u.v):
                    ins = nc.tensor.matmul(k.ps[0:v.shape[-1], 6 + g % 2, 0:P], v, pt[0:rows, i % 2, j * P:(j + 1) * P],
                                           start=(u.first and j == 0), stop=(u.last and j == len(u.v) - 1))
                ins.then_inc(summed.handle, 1)

            for i in range(n + 4):
                if i < n:
                    scores(i)
                if 3 <= i < n + 3:
                    turn(i - 3)
                if i >= 4:
                    values(i - 4)

        @block.vector
        def _(dve):
            def bias(i):
                u = units[i]
                dve.wait_ge(scored.handle, scored.at(i + 1))
                if i >= 5:
                    dve.wait_ge(turned.handle, turned.at(i - 4))
                nc.vector.tensor_tensor_reduce(ex[:, i % 5, 0:u.w], k.ps[:, i % 4, 0:u.w], u.bias, 1.0, 3e38,
                                               ALU.add, ALU.min, low[:, i % 5:i % 5 + 1]).then_inc(biased.handle, 1)

            def diagonal(i):
                u = units[i]
                dve.wait_ge(expd.handle, expd.at(i + 1))
                k.vlink(nc.vector.reciprocal(inv[:, i % 5:i % 5 + 1], tot[:, i % 5:i % 5 + 1]))
                if i >= 3:
                    dve.wait_ge(turned.handle, turned.at(i - 2))
                if u.gate is None:
                    ins = nc.vector.tensor_scalar(dg[:, i % 3, :], k.c("ident"), inv[:, i % 5:i % 5 + 1], None, ALU.mult)
                else:
                    ins = nc.vector.tensor_scalar(dg[:, i % 3, :], k.c("ident"), inv[:, i % 5:i % 5 + 1], u.gate,
                                                  ALU.mult, ALU.mult)
                ins.then_inc(diag.handle, 1)

            def store(g):
                u = units[last_of[g]]
                dve.wait_ge(summed.handle, summed.at(last_of[g] + 1))
                e = u.v[0][1].shape[-1]
                if u.clamp:
                    ins = nc.vector.tensor_scalar(u.dst, k.ps[0:e, 6 + g % 2, 0:P], -BIG, BIG, ALU.max, ALU.min)
                else:
                    ins = nc.vector.tensor_copy(u.dst, k.ps[0:e, 6 + g % 2, 0:P])
                ins.then_inc(stored.handle, 1)

            steps = iter(background)
            needed = max(u.steps for u in units)
            before = next(i for i in range(n) if units[i].steps == needed)
            width = np.cumsum([u.w for u in units])
            taken = 0

            def steps_upto(count):
                nonlocal taken
                while taken < count:
                    next(steps)
                    taken += 1

            for i in range(n + 5):
                if i < n:
                    steps_upto(units[i].steps)
                    bias(i)
                if 2 <= i < n + 2:
                    diagonal(i - 2)
                if i >= 5 and units[i - 5].last:
                    store(int(group[i - 5]))
                if i < before:
                    steps_upto(int(needed * width[i] / width[before - 1]))

        @block.scalar
        def _(act):
            def exponentials(i):
                u = units[i]
                act.wait_ge(biased.handle, biased.at(i + 1))
                nc.scalar.activation(ex[:, i % 5, 0:u.w], ex[:, i % 5, 0:u.w], ACT.Exp, bias=low[:, i % 5:i % 5 + 1],
                                     scale=-1.0, accum_out=tot[:, i % 5:i % 5 + 1]).then_inc(expd.handle, 1)

            def copy(i):
                u = units[i]
                rows, m = u.v[0][0], len(u.v)
                act.wait_ge(turned.handle, turned.at(i + 1))
                if i >= 2:
                    act.wait_ge(summed.handle, summed.at(i - 1))
                nc.scalar.copy(pt[0:rows, i % 2, 0:m * P], k.ps[0:rows, 4 + i % 2, 0:m * P]).then_inc(copied.handle, 1)

            for i in range(n + 3):
                if i < n:
                    exponentials(i)
                if i >= 3:
                    copy(i - 3)
    for g in (scored, biased, expd, diag, turned, copied, summed):
        g.advance(n)
    stored.advance(len(last_of))


class Rotary:

    def __init__(self, k, cos, sin, pos_i, pos_f, tmp):
        self.k, self.cos, self.sin, self.pos_i, self.pos_f, self.tmp = k, cos, sin, pos_i, pos_f, tmp
        self.reduced = k.s["dve_step"]

    def dve(self, dve):
        k, nc = self.k, self.k.nc
        two_pi = 2 * np.pi
        c1 = 6.28125
        c2 = float(np.float32(np.round((two_pi - c1) * 2 ** 20) / 2 ** 20))
        c3 = float(np.float32(two_pi - c1 - c2))
        magic = 1.5 * 2.0 ** 23
        edge = 3.1415925
        ang, turns = self.tmp[:, 0, :], self.tmp[:, 1, :]
        k.vlink(nc.vector.tensor_copy(self.pos_f, self.pos_i))
        k.vlink(nc.vector.tensor_scalar(ang, self.pos_f, k.c("inv64"), None, ALU.mult))
        for dst, quarter in ((self.sin, 0.0), (self.cos, 0.25)):
            k.vlink(nc.vector.tensor_scalar(turns, ang, 1.0 / two_pi, quarter, ALU.mult, ALU.add))
            k.vlink(nc.vector.tensor_scalar(turns, turns, magic, None, ALU.add))
            k.vlink(nc.vector.tensor_scalar(turns, turns, -magic, None, ALU.add))
            for c, x in ((c1, ang), (c2, dst), (c3, dst)):
                k.vlink(nc.vector.scalar_tensor_tensor(dst, turns, -c, x, ALU.mult, ALU.add))
            if quarter:
                k.vlink(nc.vector.tensor_scalar(dst, dst, float(np.pi / 2), None, ALU.add))
            nc.vector.tensor_scalar(dst, dst, -edge, edge, ALU.max, ALU.min).then_inc(self.reduced.handle, 1)
        self.reduced.advance(2)

    def act(self, act):
        for i, dst in enumerate((self.sin, self.cos)):
            act.wait_ge(self.reduced.handle, self.reduced.at(i + 1))
            self.k.nc.scalar.activation(dst, dst, ACT.Sin)


def dense_rope(k, stage, jobs, rot, cos, sin, scratch, norm=None):
    nc, s = k.nc, k.s
    first, n = STREAM_AT[stage]
    assert n == len(jobs)
    sq, root = k.at(scratch, 2, SEQ), k.at(scratch + 1024, 2, SEQ)
    t1, t2 = k.at(scratch + 2048, SEQ), k.at(scratch + 2560, SEQ)
    done, read, squared, sums, rooted = (s["product_done"], s["evacuated"], s["squares_done"], s["sum_done"],
                                         s["root_done"])
    normed, rotated, used = s["dve_step"], s["pe_step2"], s["dve_read"]
    k.slabs_end(done, [done.at(m + 1) for m in range(n)])
    rank = {m: a for a, m in enumerate(m for m in range(n) if jobs[m][1] is not None)}

    with nc.Block() as block:
        @block.sync
        def _(sp):
            k.stream(sp)

        @block.gpsimd
        def _(pool):
            k.low(pool)

        @block.tensor
        def _(pe):
            def product(m):
                hi, lo = k.slab(pe, first + m, P)
                if m >= 4:
                    pe.wait_ge(read.handle, read.at(m - 3))
                for c in range(KT):
                    ins = k.product(k.ps[:, m % 4, :], (hi[:, c, :], lo[:, c, :]),
                                    (k.x_hi[:, c, :], k.x_lo[:, c, :]), c == 0, c == KT - 1)
                ins.then_inc(done.handle, 1)

            def head_sums(m):
                a = rank[m]
                pe.wait_ge(squared.handle, squared.at(a + 1))
                if a >= 2:
                    pe.wait_ge(rooted.handle, rooted.at(a - 1))
                nc.tensor.matmul(k.ps[:, 4 + a % 2, :], k.c("ones64"), sq[:, a % 2, :], start=True,
                                 stop=True).then_inc(sums.handle, 1)

            def rotate(m):
                if m in rank:
                    pe.wait_ge(normed.handle, normed.at(rank[m] + 1))
                else:
                    pe.wait_ge(read.handle, read.at(m + 1))
                if m >= 2:
                    pe.wait_ge(used.handle, used.at(m - 1))
                nc.tensor.matmul(k.ps[:, 6 + m % 2, :], k.c(rot), jobs[m][0], start=True,
                                 stop=True).then_inc(rotated.handle, 1)

            if norm:
                norm.first_two(pe, [k.slab(pe, first + m, P) for m in range(2)], (P, P), (done, done))
            for m in range(n + 2):
                if (2 if norm else 0) <= m < n:
                    product(m)
                if m - 1 in rank:
                    head_sums(m - 1)
                if m >= 2:
                    rotate(m - 2)

        @block.scalar
        def _(act):
            if norm:
                norm.act(act)
            for m in range(n + 1):
                if m < n:
                    k.high(act, first + m + SPLIT)
                    act.wait_ge(done.handle, done.at(m + 1))
                    k.high(act, first + m + 1 + SPLIT)
                    if m in rank:
                        a = rank[m]
                        if a >= 2:
                            act.wait_ge(sums.handle, sums.at(a - 1))
                        nc.scalar.activation(sq[:, a % 2, :], k.ps[:, m % 4, :], ACT.Square).then_inc(squared.handle, 1)
                    nc.scalar.copy(jobs[m][0], k.ps[:, m % 4, :]).then_inc(read.handle, 1)
                if m - 1 in rank:
                    a = rank[m - 1]
                    act.wait_ge(sums.handle, sums.at(a + 1))
                    if a >= 2:
                        act.wait_ge(normed.handle, normed.at(a - 1))
                    nc.scalar.activation(root[:, a % 2, :], k.ps[:, 4 + a % 2, :], ACT.Sqrt, bias=k.c("eps"),
                                         scale=1.0 / 64).then_inc(rooted.handle, 1)

        @block.vector
        def _(dve):
            if norm:
                norm.dve(dve)

            def normalise(m):
                x, gain, _ = jobs[m]
                a = rank[m]
                dve.wait_ge(rooted.handle, rooted.at(a + 1))
                k.vlink(nc.vector.reciprocal(t2, root[:, a % 2, :]))
                nc.vector.scalar_tensor_tensor(x, x, k.v(gain), t2, ALU.mult, ALU.mult).then_inc(normed.handle, 1)
                dve.wait_ge(normed.handle, normed.at(a + 1))

            def rope(m):
                x, _, scale = jobs[m]
                dve.wait_ge(rotated.handle, rotated.at(m + 1))
                nc.vector.scalar_tensor_tensor(t1, x, scale, cos, ALU.mult, ALU.mult)
                nc.vector.scalar_tensor_tensor(t2, k.ps[:, 6 + m % 2, :], scale, sin, ALU.mult,
                                               ALU.mult).then_inc(used.handle, 1)
                dve.wait_ge(used.handle, used.at(m + 1))
                k.vlink(nc.vector.tensor_tensor(x, t1, t2, ALU.add))

            for m in range(n + 1):
                if m in rank:
                    normalise(m)
                if m >= 1:
                    rope(m - 1)
    if norm:
        norm.close()
    for g in (squared, sums, rooted, normed):
        g.advance(len(rank))
    for g in (done, read, rotated, used):
        g.advance(n)


def index_scores(k, iq, ik, iw, scores, cut_dots):
    nc, s = k.nc, k.s
    done, cut, used = s["product_done"], s["act_step"], s["dve_read"]
    at = {1: 0, 2: 4 * 2 * P, 3: 4 * 5 * P}

    def dots(i, h):
        w = P * (i + 1)
        return cut_dots[:, at[i] + h * w:at[i] + (h + 1) * w]

    with nc.Block() as block:
        @block.tensor
        def _(pe):
            for i in range(1, TT):
                for h in range(4):
                    u = (i - 1) * 4 + h
                    lo = 64 * (h % 2)
                    if u >= 4:
                        pe.wait_ge(cut.handle, cut.at(u - 3))
                    nc.tensor.matmul(k.ps[:, u % 4, 0:P * (i + 1)], iq[lo:lo + 64, h // 2, i * P:(i + 1) * P],
                                     ik[lo:lo + 64, 0:P * (i + 1)], start=True, stop=True).then_inc(done.handle, 1)

        @block.scalar
        def _(act):
            for i in range(1, TT):
                for h in range(4):
                    u = (i - 1) * 4 + h
                    act.wait_ge(done.handle, done.at(u + 1))
                    nc.scalar.activation(dots(i, h), k.ps[:, u % 4, 0:P * (i + 1)], ACT.Relu).then_inc(cut.handle, 1)

        @block.vector
        def _(dve):
            k.vlink(nc.vector.tensor_copy(scores[:, 0, 0:P], k.c("chunkmask")[:, SEQ - P:SEQ]))
            for i in range(1, TT):
                w = P * (i + 1)
                work = scores[:, i, 0:w]
                for h in range(4):
                    u = (i - 1) * 4 + h
                    dve.wait_ge(cut.handle, cut.at(u + 1))
                    wt = iw[:, i, h:h + 1]
                    if h == 0:
                        ins = nc.vector.tensor_scalar(work, dots(i, h), wt, None, ALU.mult)
                    else:
                        ins = nc.vector.scalar_tensor_tensor(work, dots(i, h), wt, work, ALU.mult, ALU.add)
                    ins.then_inc(used.handle, 1)
                    dve.wait_ge(used.handle, used.at(u + 1))
                k.vlink(nc.vector.tensor_tensor(work, work, k.c("chunkmask")[:, SEQ - w:SEQ], ALU.subtract))
    for g in (done, cut, used):
        g.advance(4 * (TT - 1))


SELECT_STEPS = TOPK // 8 + 1


def select_keys(k, scores, top):
    nc = k.nc
    gone = -3e38
    for i in range(1, TT):
        work = scores[:, i, 0:P * (i + 1)]
        for _ in range(TOPK // 8):
            k.vlink(nc.vector.max(top, work))
            k.vlink(nc.vector.match_replace(work, top, work, gone))
            yield
        k.vlink(nc.vector.tensor_scalar(work, work, gone, BIG, ALU.not_equal, ALU.mult))
        yield


def even_mixer(k, cos, sin):
    nc, s = k.nc, k.s
    qk = k.at(0, 16, SEQ)
    vt = k.at(8192, TT, 132)
    bv = k.at(8720, TT, 512)
    o = k.at(10768, KT, SEQ)
    olat = k.at(14864, KT, SEQ)
    negmask = k.at(19984, TT, SEQ)
    uv = k.at(22032, 512)
    small = k.at(22544, 16)
    scr = 22560
    aq, ak, iq, ik = qk[:, 0:4], qk[:, 4], qk[:, 5:7], qk[:, 7]
    bq, bk = qk[:, 8:12], qk[:, 12:16]

    k.early = [(uv, k.dram["w_uv"])]
    scale = -(64 ** -0.5)
    jobs = ([(aq[:, m, :], "aq_g", scale) for m in range(4)] + [(ak, "ak_g", 1.0)]
            + [(iq[:, m, :], None, 1.0) for m in range(2)] + [(ik, None, 1.0)]
            + [(bq[:, m, :], "bq_g", scale) for m in range(4)] + [(bk[:, m, :], "bk_g", 1.0) for m in range(4)])
    dense_rope(k, "ev_f", jobs, "rot64", cos, sin, scr, Normalise(k, k.h, "mix_g0"))

    def token_major(j, t, ps):
        dst = vt[:, t, :] if j == 0 else bv[:, t, (j - 1) * 256:j * 256]
        return nc.scalar.copy(dst, ps)

    dense_t(k, "ev_t", [132, 256, 256], token_major)
    index_scores(k, iq, ik, vt[:, :, 128:132], negmask, k.at(14864, 5120))

    lams = k.vec[:, VEC_AT["lams"][0]:VEC_AT["lams"][0] + 4]
    with nc.Block() as block:
        @block.vector
        def _(dve):
            nc.vector.tensor_tensor(small[:, 0:2], lams[:, 0:4:2], lams[:, 1:4:2], ALU.mult).then_inc(s["dve_step"].handle, 1)
            dve.wait_ge(s["act_step"].handle, s["act_step"].at(1))
            k.vlink(nc.vector.tensor_tensor(small[:, 4:5], small[:, 3:4], small[:, 2:3], ALU.subtract))
            k.vlink(nc.vector.tensor_scalar(small[:, 5:6], small[:, 4:5], -0.2, None, ALU.add))

        @block.tensor
        def _(pe):
            pe.wait_ge(s["dve_step"].handle, s["dve_step"].at(1))
            nc.tensor.matmul(k.ps[:, 0, 0:2], k.c("ones"), small[:, 0:2], start=True,
                             stop=True).then_inc(s["pe_step"].handle, 1)

        @block.scalar
        def _(act):
            act.wait_ge(s["pe_step"].handle, s["pe_step"].at(1))
            nc.scalar.activation(small[:, 2:4], k.ps[:, 0, 0:2], ACT.Exp).then_inc(s["act_step"].handle, 1)
    for g in ("dve_step", "act_step", "pe_step"):
        s[g].advance(1)

    sparse, differential = [], []
    for i in range(TT):
        q = slice(i * P, (i + 1) * P)
        w = P * (i + 1)
        for h in range(8):
            lo = 64 * (h % 2)
            sparse.append(Unit(aq[lo:lo + 64, h // 2, q], ak[lo:lo + 64, 0:w], negmask[:, i, 0:w],
                               [(P, vt[:, j, 0:P]) for j in range(i + 1)], dst=olat[:, h, q], steps=SELECT_STEPS * i))
    for i in reversed(range(TT)):
        q = slice(i * P, (i + 1) * P)
        w = P * (i + 1)
        for h in range(4):
            for c in range(2):
                differential.append(Unit(bq[64 * c:64 * c + 64, h, q], bk[64 * c:64 * c + 64, h, 0:w],
                                         k.c("chunkmask")[:, SEQ - w:SEQ],
                                         [(P, bv[:, j, h * P:(h + 1) * P]) for j in range(i + 1)],
                                         gate=small[:, 5:6] if c else None, first=(c == 0), last=(c == 1),
                                         dst=o[:, 4 + h, q], clamp=True))
    attention(k, differential + sparse, scr, select_keys(k, negmask, small[:, 8:16]))

    sq = k.at(scr, 2, SEQ)
    root = k.at(scr + 1024, 2, SEQ)
    inv = k.at(scr + 2048, SEQ)
    lifted, copied, squared, sums, rooted, used = (s["product_done"], s["evacuated"], s["squares_done"], s["sum_done"],
                                                   s["root_done"], s["dve_read"])
    with nc.Block() as block:
        @block.tensor
        def _(pe):
            def lift(h):
                if h >= 4:
                    pe.wait_ge(copied.handle, copied.at(h - 3))
                nc.tensor.matmul(k.ps[0:64, h % 4, :], uv[:, h * 64:(h + 1) * 64], olat[:, h, :], start=True,
                                 stop=True).then_inc(lifted.handle, 1)

            for h in range(4):
                lift(2 * h)
                pe.wait_ge(squared.handle, squared.at(h + 1))
                nc.tensor.matmul(k.ps[:, 4 + h, :], k.c("ones"), sq[:, h % 2, :], start=True,
                                 stop=True).then_inc(sums.handle, 1)
                lift(2 * h + 1)

        @block.scalar
        def _(act):
            def copy(h):
                act.wait_ge(lifted.handle, lifted.at(h + 1))
                lo = 64 * (h % 2)
                nc.scalar.copy(o[lo:lo + 64, h // 2, :], k.ps[0:64, h % 4, :]).then_inc(copied.handle, 1)

            for h in range(5):
                if h < 4:
                    if h >= 2:
                        act.wait_ge(sums.handle, sums.at(h - 1))
                    nc.scalar.activation(sq[:, h % 2, :], o[:, 4 + h, :], ACT.Square,
                                         scale=SHRINK).then_inc(squared.handle, 1)
                if h >= 1:
                    act.wait_ge(sums.handle, sums.at(h))
                    if h >= 3:
                        act.wait_ge(used.handle, used.at(h - 2))
                    nc.scalar.activation(root[:, (h - 1) % 2, :], k.ps[:, 3 + h, :], ACT.Sqrt, bias=k.c("eps_small"),
                                         scale=1.0 / P).then_inc(rooted.handle, 1)
                    copy(2 * h - 2)
                    copy(2 * h - 1)

        @block.vector
        def _(dve):
            k.vlink(nc.vector.tensor_scalar(small[:, 6:7], k.v("subln_g"), SHRINK * (1.0 - 0.2), None, ALU.mult))
            for h in range(4):
                dve.wait_ge(rooted.handle, rooted.at(h + 1))
                k.vlink(nc.vector.reciprocal(inv, root[:, h % 2, :]))
                ins = nc.vector.scalar_tensor_tensor(inv, root[:, h % 2, :], OVERFLOW, inv, ALU.is_lt, ALU.mult)
                ins.then_inc(used.handle, 1)
                dve.wait_ge(used.handle, used.at(h + 1))
                k.vlink(nc.vector.scalar_tensor_tensor(o[:, 4 + h, :], o[:, 4 + h, :], small[:, 6:7], inv,
                                                       ALU.mult, ALU.mult))
    for g, v in ((lifted, 8), (copied, 8), (squared, 4), (sums, 4), (rooted, 4), (used, 4)):
        g.advance(v)
    rows_add(k, "ev_out", o, [P] * KT, 1.0).alone()


def layer_norm_f(k, groups, rows, scratch, finish=None):
    nc, s = k.nc, k.s
    sq = k.at(scratch, 4, SEQ)
    root = k.at(scratch + 2048, SEQ)
    inv = k.at(scratch + 2560, SEQ)
    summed, centred, squared, sums, rooted, used = (s["product_done"], s["dve_step"], s["squares_done"], s["sum_done"],
                                                    s["root_done"], s["dve_read"])
    per = len(groups[0])
    dim = per * rows
    n = len(groups)
    ones = k.c("ones")[0:rows, 0:rows]

    with nc.Block() as block:
        @block.tensor
        def _(pe):
            def total(g):
                if g >= 2:
                    pe.wait_ge(centred.handle, centred.at((g - 1) * per))
                for j, x in enumerate(groups[g]):
                    ins = nc.tensor.matmul(k.ps[0:rows, g % 2, :], ones, x, start=(j == 0), stop=(j == per - 1))
                ins.then_inc(summed.handle, 1)

            def total_squares(g):
                if g >= 2:
                    pe.wait_ge(rooted.handle, rooted.at(g - 1))
                for j in range(per):
                    u = g * per + j
                    pe.wait_ge(squared.handle, squared.at(u + 1))
                    nc.tensor.matmul(k.ps[0:rows, 2 + g % 2, :], ones, sq[0:rows, u % 4, :], start=(j == 0),
                                     stop=(j == per - 1)).then_inc(sums.handle, 1)

            for g in range(n + 1):
                if g < n:
                    total(g)
                if g >= 1:
                    total_squares(g - 1)

        @block.scalar
        def _(act):
            for g in range(n + 1):
                if g < n:
                    for j, x in enumerate(groups[g]):
                        u = g * per + j
                        act.wait_ge(centred.handle, centred.at(u + 1))
                        if u >= 4:
                            act.wait_ge(sums.handle, sums.at(u - 3))
                        nc.scalar.activation(sq[0:rows, u % 4, :], x, ACT.Square).then_inc(squared.handle, 1)
                if g >= 1:
                    act.wait_ge(sums.handle, sums.at(g * per))
                    if g >= 2:
                        act.wait_ge(used.handle, used.at((g - 1) * per))
                    nc.scalar.activation(root[0:rows, :], k.ps[0:rows, 2 + (g - 1) % 2, :], ACT.Sqrt,
                                         bias=k.c("eps")[0:rows, :], scale=1.0 / dim).then_inc(rooted.handle, 1)
                    if finish and g == n:
                        for j in range(n * per):
                            act.wait_ge(used.handle, used.at(j + 1))
                            finish(j)

        @block.vector
        def _(dve):
            for g in range(n + 1):
                if g < n:
                    dve.wait_ge(summed.handle, summed.at(g + 1))
                    for x in groups[g]:
                        nc.vector.scalar_tensor_tensor(x, k.ps[0:rows, g % 2, :], -1.0 / dim, x, ALU.mult,
                                                       ALU.add).then_inc(centred.handle, 1)
                if g >= 1:
                    dve.wait_ge(rooted.handle, rooted.at(g))
                    k.vlink(nc.vector.reciprocal(inv[0:rows, :], root[0:rows, :]))
                    for x in groups[g - 1]:
                        ins = nc.vector.tensor_tensor(x, x, inv[0:rows, :], ALU.mult)
                        ins.then_inc(used.handle, 1)
                    dve.wait_ge(used.handle, used.at(g * per))
    for g, v in ((summed, n), (centred, n * per), (squared, n * per), (sums, n * per), (rooted, n), (used, n * per)):
        g.advance(v)


def odd_mixer(k):
    nc, s = k.nc, k.s
    o = k.at(0, KT, SEQ)
    a = k.at(4096, 4, SEQ)
    g = k.at(6144, 4, 30 + SEQ)
    vt = k.at(8312, TT, 512)
    ws = k.at(10360, 8, P)
    bs = k.at(11384, 4, P)
    lng, lnb = k.at(11896, 512), k.at(12408, 512)
    acc = k.at(12920, 4, SEQ)
    stats, aggr, sm = k.at(14968, TT, 6), k.at(14992, TT, 2), k.at(15000, 16)
    scr = 15016
    k.early = [(ws, k.dram["w_s"]), (bs, k.dram["b_s"]), (lng, k.dram["cln"][0:1].partition_broadcast(P)),
               (lnb, k.dram["cln"][1:2].partition_broadcast(P))]

    def evac(m, ps):
        if m >= 8:
            return nc.scalar.activation(o[:, m - 8, :], ps, ACT.Gelu_apprx_tanh)
        if m % 2 == 0:
            return nc.scalar.copy(a[:, m // 2, :], ps)
        return nc.scalar.activation(g[:, m // 2, 30:], ps, ACT.Sigmoid)

    at = VEC_AT["conv_w"][0]

    def convolve(c, taps):
        dst = o[:, 4 + c, :]
        for tap in taps:
            wt = k.vec[:, at + c * 31 + tap:at + c * 31 + tap + 1]
            src = g[:, c, tap:tap + SEQ]
            if tap == 0:
                nc.vector.memset(g[:, c, 0:30], 0.0)
                k.vlink(nc.vector.tensor_tensor(g[:, c, 30:], g[:, c, 30:], a[:, c, :], ALU.mult))
                k.vlink(nc.vector.tensor_scalar(dst, src, wt, k.v("conv_b", c), ALU.mult, ALU.add))
            else:
                k.vlink(nc.vector.scalar_tensor_tensor(dst, src, wt, dst, ALU.mult, ALU.add))

    def first_tiles(dve, read):
        for c in range(3):
            dve.wait_ge(read.handle, read.at(2 * c + 2))
            convolve(c, range(31 if c < 2 else CONV_SPLIT))

    def last_tiles(dve):
        convolve(2, range(CONV_SPLIT, 31))
        convolve(3, range(31))

    dense_f(k, "od_f", [P] * 12, evac, norm=Normalise(k, k.h, "mix_g1"), meanwhile=first_tiles)
    dense_t(k, "od_t", [256, 256],
            lambda j, t, ps: nc.scalar.activation(vt[:, t, j * 256:(j + 1) * 256], ps, ACT.Gelu_apprx_tanh),
            meanwhile=last_tiles)

    rooted, normed, mixed = s["root_done"], s["dve_step"], s["product_done"]
    with nc.Block() as block:
        @block.gpsimd
        def _(pool):
            nc.gpsimd.memset(ws[64:128, :, 0:64], 0.0).then_inc(s["pool_step"].handle, 1)

        @block.scalar
        def _(act):
            act.wait_ge(s["tmp_ready"].handle, s["tmp_ready"].at(1))
            nc.scalar.activation(sm[:, 0:4], aggr[:, :, 1], ACT.Sqrt, bias=k.c("eps")).then_inc(rooted.handle, 1)

        @block.vector
        def _(dve):
            for t in range(TT):
                k.vlink(nc.vector.bn_stats(stats[:, t, :], vt[:, t, :]))
            for t in range(TT):
                ins = nc.vector.bn_aggr(aggr[:, t, :], stats[:, t, :])
            ins.then_inc(s["tmp_ready"].handle, 1)
            dve.wait_ge(rooted.handle, rooted.at(1))
            k.vlink(nc.vector.reciprocal(sm[:, 4:8], sm[:, 0:4]))
            for t in range(TT):
                k.vlink(nc.vector.tensor_scalar(vt[:, t, :], vt[:, t, :], aggr[:, t, 0:1], sm[:, 4 + t:5 + t],
                                                ALU.subtract, ALU.mult))
                k.vlink(nc.vector.tensor_tensor(vt[:, t, :], vt[:, t, :], lng, ALU.mult))
                nc.vector.tensor_tensor(vt[:, t, :], vt[:, t, :], lnb, ALU.add).then_inc(normed.handle, 1)
            for gp in range(4):
                dve.wait_ge(mixed.handle, mixed.at(gp + 1))
                for half in range(2):
                    lo = 64 * half
                    tmp = acc[lo:lo + 64, gp, :].rearrange("p (t i) -> p t i", t=TT)
                    for t in range(TT):
                        ins = nc.vector.tensor_tensor(tmp[:, t, :], k.ps[lo:lo + 64, 4 * (gp % 2) + t,
                                                                         half * P:(half + 1) * P],
                                                      bs[lo:lo + 64, gp, :], ALU.add)
                ins.then_inc(s["dve_read"].handle, 1)
                dve.wait_ge(s["dve_read"].handle, s["dve_read"].at(gp + 1))
                nc.vector.tensor_tensor(o[:, gp, :], o[:, gp, :], acc[:, gp, :], ALU.mult)

        @block.tensor
        def _(pe):
            pe.wait_ge(s["pool_step"].handle, s["pool_step"].at(1))
            for gp in range(4):
                if gp >= 2:
                    pe.wait_ge(s["dve_read"].handle, s["dve_read"].at(gp - 1))
                for t in range(TT):
                    if gp == 0:
                        pe.wait_ge(normed.handle, normed.at(t + 1))
                    ins = nc.tensor.matmul(k.ps[:, 4 * (gp % 2) + t, 0:256], vt[:, t, gp * P:(gp + 1) * P],
                                           ws[:, 2 * gp:2 * gp + 2, :], start=True, stop=True)
                ins.then_inc(mixed.handle, 1)
    for n, v in (("pool_step", 1), ("tmp_ready", 1), ("root_done", 1), ("dve_step", 4), ("product_done", 4), ("dve_read", 4)):
        s[n].advance(v)

    layer_norm_f(k, [[o[:, 4 + c, :] for c in range(4)]], P, scr,
                 lambda c: nc.scalar.activation(o[:, 4 + c, :], o[:, 4 + c, :], ACT.Silu, bias=k.v("dln_b", c),
                                                scale=k.v("dln_g", c)))
    rows_add(k, "od_out", o, [P] * KT, 1.0).alone()


def mem_attention(k, layer, out, base):
    nc = k.nc
    mem = k.at(base + 4096, KT, NMEM)
    inv = k.at(base + 6144, NMEM)
    with nc.Block() as block:
        MeanSquare(k, mem, NMEM, inv).alone(block)
    mk = k.at(base, 4, NMEM)
    mv = k.at(base + 1024, 2, 512)
    xq = k.at(base + 2048, 4, SEQ)
    zero = k.c("chunkmask")[:, 0:NMEM]
    dense_f(k, f"mk{layer}", [P] * 4, lambda m, ps: nc.scalar.copy(mk[:, m, :], ps), NMEM,
            Normalise(k, mem, "memnorm_g", NMEM, inv))
    dense_t(k, f"mv{layer}", [256, 256],
            lambda j, t, ps: nc.scalar.copy(mv[:, t, j * 256:(j + 1) * 256], ps), tts=2)
    dense_f(k, f"xq{layer}", [P] * 4, lambda m, ps: nc.scalar.mul(xq[:, m, :], ps, -(P ** -0.5)),
            norm=Normalise(k, k.h, f"norm2_g{layer}"))
    attention(k, [Unit(xq[:, h, i * P:(i + 1) * P], mk[:, h, :], zero,
                       [(P, mv[:, j, h * P:(h + 1) * P]) for j in range(2)], dst=out[:, h, i * P:(i + 1) * P])
                  for i in range(TT) for h in range(4)], base + 4096)


def pool_windows(k, za, recip, buf):
    nc = k.nc

    def windows(dve, read):
        for i, g in enumerate(reversed(range(4))):
            w = POOL_W[g]
            dve.wait_ge(read.handle, read.at(2 * i + 2))
            z = src = za[0:96, 2 * g:2 * g + 2, :]
            step, b = 1, 0
            while step < w:
                dst = buf[0:96, b, :].rearrange("p (a t) -> p a t", a=2)
                nc.vector.tensor_copy(dst[:, :, 0:step], src[:, :, 0:step])
                k.vlink(nc.vector.tensor_tensor(dst[:, :, step:], src[:, :, step:], src[:, :, 0:SEQ - step], ALU.add))
                src, step, b = dst, 2 * step, 1 - b
            for a in range(2):
                k.vlink(nc.vector.tensor_tensor(src[:, a, :], src[:, a, :], recip[0:96, g, :], ALU.mult))
            k.vlink(nc.vector.tensor_tensor(z, src, z, ALU.subtract))
    return windows


def pool_mixer(k, za, out, wg):
    nc, done = k.nc, k.s["product_done"]
    with nc.Block() as block:
        @block.tensor
        def _(pe):
            for g in range(4):
                for m in range(2):
                    for c in range(2):
                        ins = nc.tensor.matmul(k.ps[0:96, 2 * g + m, :], wg[0:96, 2 * g + c, m * 96:(m + 1) * 96],
                                               za[0:96, 2 * g + c, :], start=(c == 0), stop=(c == 1))
                    ins.then_inc(done.handle, 1)

        @block.scalar
        def _(act):
            for m in range(8):
                act.wait_ge(done.handle, done.at(m + 1))
                nc.scalar.activation(out[0:96, m, :], k.ps[0:96, m, :], ACT.Copy, scale=k.v("pool_scale", m, 96))
    done.advance(8)


def retention(k, q, key, v, out, decay, scr):
    nc, s = k.nc, k.s
    att = k.at(scr, 2, SEQ)
    scored, decayed, summed, copied = s["scores_done"], s["biased"], s["out_done"], s["out_copied"]

    with nc.Block() as block:
        @block.tensor
        def _(pe):
            def scores(u):
                h, j = u // TT, u % TT
                if u >= 2:
                    pe.wait_ge(decayed.handle, decayed.at(u - 1))
                nc.tensor.matmul(k.ps[:, u % 2, 0:SEQ - j * P], key[:, h, j * P:(j + 1) * P], q[:, h, j * P:],
                                 start=True, stop=True).then_inc(scored.handle, 1)

            def values(u):
                h, j = u // TT, u % TT
                pe.wait_ge(decayed.handle, decayed.at(u + 1))
                if j == 0 and h >= 2:
                    pe.wait_ge(copied.handle, copied.at(2 * (h - 1)))
                for m in range(2):
                    c = h * RET_DV + m * 96
                    ins = nc.tensor.matmul(k.ps[0:96, 2 + 2 * (h % 2) + m, j * P:SEQ], v[:, j, c:c + 96],
                                           att[:, u % 2, 0:SEQ - j * P], start=(j == 0), stop=(j == TT - 1))
                ins.then_inc(summed.handle, 1)

            for u in range(RET_H * TT + 1):
                if u < RET_H * TT:
                    scores(u)
                if u >= 1:
                    values(u - 1)

        @block.vector
        def _(dve):
            for u in range(RET_H * TT):
                h, j = u // TT, u % TT
                dve.wait_ge(scored.handle, scored.at(u + 1))
                if u >= 2:
                    dve.wait_ge(summed.handle, summed.at(u - 1))
                nc.vector.tensor_tensor(att[:, u % 2, 0:SEQ - j * P], k.ps[:, u % 2, 0:SEQ - j * P],
                                        decay[:, h, 0:SEQ - j * P], ALU.mult).then_inc(decayed.handle, 1)

        @block.scalar
        def _(act):
            for h in range(RET_H):
                act.wait_ge(summed.handle, summed.at((h + 1) * TT))
                for m in range(2):
                    nc.scalar.copy(out[0:96, 2 * h + m, :], k.ps[0:96, 2 + 2 * (h % 2) + m, :]).then_inc(copied.handle, 1)
    for g in (scored, decayed, summed):
        g.advance(RET_H * TT)
    copied.advance(2 * RET_H)
    layer_norm_f(k, [[out[0:96, 2 * h + m, :] for m in range(2)] for h in range(RET_H)], 96, scr)


def gate_and_project(k, layer, y, heights, scratch):
    nc = k.nc
    dense_gated(k, f"gate{layer}", heights, ACT.Silu,
                lambda m, gate: nc.vector.tensor_tensor(y[0:heights[m], m, :], y[0:heights[m], m, :], gate, ALU.mult),
                scratch)
    rows_add(k, f"wo{layer}", y, heights, 1.0).alone()


EVEN_BASE, ODD_BASE = 20 * SEQ, 16 * SEQ


def second_even(k):
    nc = k.nc
    y = k.at(0, 20, SEQ)
    base = EVEN_BASE
    recip = k.at(base + 13312, 4, SEQ)
    k.early = [(recip, k.dram["pool_recip"])]
    mem_attention(k, 0, y[:, 16:20], base)
    za = k.at(base, 8, SEQ)
    wg = k.at(base + 4096, 8, 192)
    tab = k.at(base + 10240, 2, SEQ)
    decay = k.at(base + 11264, 4, SEQ)
    k.early = [(tab, k.dram["rotary"]), (decay, k.dram["decay"])] + [(wg[0:96], k.dram["pool_w"])]
    dense_f(k, "za", [96] * 8, lambda m, ps: nc.scalar.copy(za[0:96, ZA_ORDER[m], :], ps),
            meanwhile=pool_windows(k, za, recip, k.at(base + 7680, 2, 2 * SEQ)))
    pool_mixer(k, za, y[:, 0:8], wg)
    qk = k.at(base, 8, SEQ)
    v = k.at(base + 4096, TT, 768)
    scr = base + 7168
    dense_rope(k, "rqk", [(qk[:, m, :], None, P ** -0.5 if m < 4 else 1.0) for m in range(8)], "rot128",
               tab[:, 0, :], tab[:, 1, :], scr)
    dense_t(k, "rv", [256] * 3, lambda j, t, ps: nc.scalar.copy(v[:, t, j * 256:(j + 1) * 256], ps))
    retention(k, qk[:, 0:4], qk[:, 4:8], v, y[:, 8:16], decay, scr)
    k.early = [(k.at(ODD_BASE + 4096, KT, NMEM), k.dram["mem"])]
    gate_and_project(k, 0, y, [96] * 16 + [P] * 4, scr)


def compress_and_project(k, kc, vc, kcmp, vcmp, scr, w1, evacuate):
    nc, s = k.nc, k.s
    m2 = NSA_G * NCMP
    x = k.at(scr, 2, 4 * m2)
    hid = k.at(scr + 512, 4, 64)
    w2 = k.at(scr + 768, 4, P)
    ready, part, hidden, second = s["dve_step"], s["pe_step"], s["act_step"], s["pe_step2"]
    done, read = s["product_done"], s["evacuated"]
    first, n = STREAM_AT["nsaqk"]
    steps = 16
    assert n == steps
    k.slabs_end(done, [done.at(u + 1) for u in range(n)])

    with nc.Block() as block:
        @block.sync
        def _(sp):
            for u in range(n - 2):
                k.slabs_upto(sp, first + u + SPLIT + RING)
                sp.wait_ge(part.handle, part.at(u + 1))
                sp.dma_start(w1[u % 2], k.dram["cmp_w1"][u + 2]).then_inc(k.cmp_loaded[u % 2].handle, 16)
            k.stream(sp)

        @block.gpsimd
        def _(pool):
            k.low(pool)

        @block.vector
        def _(dve):
            for u in range(n):
                src = kc if u < 8 else vc
                if u >= 2:
                    dve.wait_ge(part.handle, part.at(u - 1))
                for li in range(4):
                    l = 4 * (u % 8) + li
                    dst = x[:, u % 2, li * m2:(li + 1) * m2].rearrange("p (g j) -> p g j", g=2)
                    ins = nc.vector.tensor_scalar(dst, src[:, :, l:l + 16 * (NCMP - 1) + 1:16],
                                                  k.v("cmp_pe", 32 * (u // 8) + l), None, ALU.add)
                ins.then_inc(ready.handle, 1)

        @block.tensor
        def _(pe):
            for u in range(n):
                kind = u // 8
                pe.wait_ge(k.cmp_loaded[u % 2].handle, 16 * (u // 2 + 1))
                pe.wait_ge(ready.handle, ready.at(u + 1))
                for li in range(4):
                    for m in range(2):
                        ins = nc.tensor.matmul(k.ps[:, 2 * kind + m, 0:m2], w1[u % 2][:, li, m * P:(m + 1) * P],
                                               x[:, u % 2, li * m2:(li + 1) * m2], start=(u % 8 == 0 and li == 0),
                                               stop=(u % 8 == 7 and li == 3))
                ins.then_inc(part.handle, 1)
                hi, lo = k.slab(pe, first + u, P)
                if u >= 4:
                    pe.wait_ge(read.handle, read.at(u - 3))
                for c in range(KT):
                    ins = k.product(k.ps[:, 4 + u % 4, :], (hi[:, c, :], lo[:, c, :]),
                                    (k.x_hi[:, c, :], k.x_lo[:, c, :]), c == 0, c == KT - 1)
                ins.then_inc(done.handle, 1)
            pe.wait_ge(hidden.handle, hidden.at(4))
            for c in range(2):
                ins = nc.tensor.matmul(k.ps[:, 0, 0:m2], w2[:, c, :], hid[:, c, 0:m2], start=(c == 0), stop=(c == 1))
            ins.then_inc(second.handle, 1)
            for g in range(2):
                for c in range(2):
                    ins = nc.tensor.matmul(k.ps[0:NCMP, 1 + g, 0:P], hid[:, 2 + c, g * NCMP:(g + 1) * NCMP], w2[:, 2 + c, :],
                                           start=(c == 0), stop=(c == 1))
                ins.then_inc(second.handle, 1)

        @block.scalar
        def _(act):
            for u in range(n):
                k.high(act, first + u + SPLIT)
                if u % 8 == 7:
                    act.wait_ge(part.handle, part.at(u + 1))
                    for m in range(u // 8 * 2, u // 8 * 2 + 2):
                        nc.scalar.activation(hid[:, m, 0:m2], k.ps[:, m, 0:m2], ACT.Silu,
                                             bias=k.v("cmp_b1", m)).then_inc(hidden.handle, 1)
                act.wait_ge(done.handle, done.at(u + 1))
                k.high(act, first + u + 1 + SPLIT)
                evacuate(u, k.ps[:, 4 + u % 4, :]).then_inc(read.handle, 1)
            k.all_high(act)
            act.wait_ge(second.handle, second.at(1))
            nc.scalar.copy(kcmp[:, 0:m2], k.ps[:, 0, 0:m2])
            for g in range(2):
                act.wait_ge(second.handle, second.at(2 + g))
                nc.scalar.copy(vcmp[0:NCMP, g, :], k.ps[0:NCMP, 1 + g, 0:P])
    for g, v in ((ready, n), (part, n), (hidden, 4), (second, 3), (done, n), (read, n)):
        g.advance(v)


def turn_bias(k, bias):
    nc, turned, copied = k.nc, k.s["pe_step"], k.s["act_step"]
    half = BIASW // 2

    with nc.Block() as block:
        @block.tensor
        def _(pe):
            pe.wait_ge(k.s["bias_loaded"].handle, 16)
            for h in range(NSA_H):
                if h >= 4:
                    pe.wait_ge(copied.handle, copied.at(2 * (h - 3)))
                for j in range(2):
                    ins = nc.tensor.matmul(k.ps[:, 2 * (h % 4) + j, 0:half], k.c("flip"),
                                           bias[:, h, j * half:(j + 1) * half], start=True, stop=True)
                ins.then_inc(turned.handle, 1)

        @block.scalar
        def _(act):
            for h in range(NSA_H):
                act.wait_ge(turned.handle, turned.at(h + 1))
                for j in range(2):
                    nc.scalar.copy(bias[:, h, j * half:(j + 1) * half],
                                   k.ps[:, 2 * (h % 4) + j, 0:half]).then_inc(copied.handle, 1)
    turned.advance(NSA_H)
    copied.advance(2 * NSA_H)


def second_odd(k):
    nc, s = k.nc, k.s
    y = k.at(0, 16, SEQ)
    base = ODD_BASE
    mem_attention(k, 1, y[:, 12:16], base)
    kcmp = k.at(base, 64)
    vcmp = k.at(base + 64, 2, P)
    gl = k.at(base + 320, TT, 36)
    kvc = k.at(base + 512, 4, SEQ)
    scr = base + 464
    vals = k.at(scr + ATTENTION, TT, 512)
    w1 = [k.at(scr + ATTENTION + u * SLAB, 4, 256) for u in range(2)]
    bias = k.at(scr + ATTENTION + 2048, NSA_H, BIASW)
    keys = k.at(scr + ATTENTION + 2048 + NSA_H * BIASW, 4, SEQ)
    k.early = [(k.at(base + 2560 + 768, 4, P), k.dram["cmp_w2"])]
    k.late = [(w1[u], k.dram["cmp_w1"][u], k.cmp_loaded[u]) for u in range(2)]
    k.late += [(bias, bass.AP(k.dram["frev"].tensor, 0, [[1, P], [FREV, NSA_H], [1, BIASW]]), s["bias_loaded"])]
    dense_f(k, "kvc", [P] * 4, lambda m, ps: nc.scalar.copy(kvc[:, m, :], ps))
    compress_and_project(k, kvc[:, 0:2], kvc[:, 2:4], kcmp, vcmp, base + 2560, w1,
                         lambda m, ps: nc.scalar.mul(y[:, m, :], ps, -(P ** -0.5)) if m < NSA_H
                         else nc.scalar.copy(keys[:, m - NSA_H, :], ps))
    turn_bias(k, bias)

    def evac(j, t, ps):
        if j == 2:
            return nc.scalar.activation(gl[:, t, :], ps, ACT.Sigmoid)
        return nc.scalar.copy(vals[:, t, j * 256:(j + 1) * 256], ps)

    dense_t(k, "nsav", [256, 256, 36], evac)
    with nc.Block() as block:
        @block.vector
        def _(dve):
            nc.vector.tensor_scalar(gl[:, 0, 0:NSA_H], gl[:, 0, 0:NSA_H], k.c("seen"), None, ALU.mult)

    units = []
    for i in range(TT):
        q = slice(i * P, (i + 1) * P)
        w = P * (i + 1)
        for h in range(NSA_H):
            g = h // 6
            qh = y[:, h, q]
            c0 = 415 - P * i
            units.append(Unit(qh, kcmp[:, g * NCMP:(g + 1) * NCMP], bias[:, h, c0:c0 + 16 * (NCMP - 1) + 1:16],
                              [(NCMP, vcmp[0:NCMP, g, :])], gate=gl[:, i, h:h + 1], last=False))
            for b in range(2):
                units.append(Unit(qh, keys[:, 2 * b + g, 0:w], bias[:, h, SEQ - w:SEQ],
                                  [(P, vals[:, j, b * 256 + g * P:b * 256 + (g + 1) * P]) for j in range(i + 1)],
                                  gate=gl[:, i, NSA_H * (b + 1) + h:NSA_H * (b + 1) + h + 1], first=False,
                                  last=(b == 1), dst=qh))
    attention(k, units, scr)
    gate_and_project(k, 1, y, [P] * 16, scr)


def finish(k):
    nc = k.nc
    out = k.at(0, KT, SEQ)
    ready = k.s["dve_step"]
    with nc.Block() as block:
        @block.vector
        def _(dve):
            for c in range(KT):
                nc.vector.scalar_tensor_tensor(out[:, c, :], k.h[:, c, :], k.v("final_g", c), k.inv[:, :], ALU.mult,
                                               ALU.mult).then_inc(ready.handle, 1)

        @block.sync
        def _(sp):
            for c in range(0, KT, 2):
                sp.wait_ge(ready.handle, ready.at(c + 2))
                sp.dma_start(k.dram["out"][:, c:c + 2, :], out[:, c:c + 2, :]).then_inc(k.stored.handle, 16)
            sp.wait_ge(k.stored.handle, k.stored.at(16 * KT // 2))
    ready.advance(KT)
    k.stored.advance(16 * KT // 2)


def build(nc, dram):
    with ExitStack() as ctx:
        k = Core(nc, ctx, dram)
        cos, sin = k.at(18960, SEQ), k.at(19472, SEQ)
        rotary = start(k, cos, sin)
        for layer in range(2):
            ffn(k, "ffn1", layer, None if layer else rotary)
            if layer == 0:
                even_mixer(k, cos, sin)
            else:
                odd_mixer(k)
            k.early = [(k.at(12288, 2, SEQ), k.dram["p"][layer])]
            ffn(k, "ffn2", layer)
            if layer == 1:
                k.early = [(k.at(EVEN_BASE + 4096, KT, NMEM), k.dram["mem"])]
            ple(k, layer)
        second_even(k)
        second_odd(k)
        finish(k)


def kernel(**inputs):
    import concourse.bacc as bacc
    from concourse.bass_utils import run_bass_kernel_spmd as run

    a = {n: np.asarray(v) for n, v in inputs.items()}

    def feature_major(x):
        return np.ascontiguousarray(x.T.reshape(-1, P, x.shape[0]).transpose(1, 0, 2))

    arrays = {
        "x": feature_major(a["x"][0]),
        "p": np.stack([feature_major(a["p"][l, 0]) for l in range(2)]),
        "mem": feature_major(a["mem_2"][0]),
        "pos": np.ascontiguousarray(a["pos"].reshape(1, SEQ)),
        "stream": lay_stream(a),
        "vec": lay_vectors(a),
        "cst": np.concatenate([CONSTS[n] for n in CONST_AT], axis=1),
        "w_uv": np.ascontiguousarray(a["a_w_uv"][0].transpose(1, 0, 2).reshape(P, 512)),
        "w_s": np.ascontiguousarray(a["c_w_s"][0].transpose(2, 0, 1)),
        "b_s": np.ascontiguousarray(np.repeat(a["c_b_s"][0], 64, axis=0).reshape(4, P, P).transpose(1, 0, 2)),
        "cln": np.concatenate([a["c_ln_g"], a["c_ln_b"]], axis=0),
        "pool_w": np.ascontiguousarray(a["ev_pool_w_2"][0].reshape(8, 96, 192).transpose(1, 0, 2)),
        "pool_recip": pool_tables().reshape(P, 4, SEQ),
        "rotary": rotary_tables().reshape(P, 2, SEQ),
        "decay": decay_tables().reshape(P, 4, SEQ),
        "cmp_w1": np.ascontiguousarray(a["od_cmp_w1_2"][0].reshape(16, 4, P, 256).transpose(0, 2, 1, 3)),
        "cmp_w2": np.ascontiguousarray(a["od_cmp_w2_2"][0].reshape(4, P, P).transpose(1, 0, 2)),
        "rel": np.ascontiguousarray(a["rel_bias_2"]),
        "buckets": bucket_table(),
    }
    nc = bacc.Bacc("TRN2", target_bir_lowering=False, num_devices=1)
    dram = {n: nc.dram_tensor(f"in_{n}", v.shape, mybir.dt.from_np(v.dtype), kind="ExternalInput").ap()
            for n, v in arrays.items()}
    dram["frev"] = nc.dram_tensor("frev", (NSA_H, FREV), F32, kind="Internal").ap()
    dram["out"] = nc.dram_tensor("out_0", (P, KT, SEQ), F32, kind="ExternalOutput").ap()
    build(nc, dram)
    r = run(nc, [{f"in_{n}": v for n, v in arrays.items()}], core_ids=[0])
    got = r.results[0]["out_0"]
    return np.ascontiguousarray(got.transpose(2, 1, 0).reshape(1, SEQ, D))
```
